# Optimizing a Trainium2 kernel written in Bass

```python
import functools
import jax
import jax.numpy as jnp
from jax import lax
import numpy as np

D_MODEL = 1024
BATCH = 1
SEQ = 1024
DEPTH = 1
DEC_BATCH = 8
DEC_SEQ = 8
PAST_LEN = 1024
PAGE_SIZE = 128

N_BRANCH = 3
BRANCH_W = 512
CONV_W = BRANCH_W
CONV_K = 31
HG_HEADS = 4
HG_DK = 128
HG_DV = 128
HG_CHUNK = 64
ATT_HEADS = 8
ATT_HD = 64
Q_BLOCK = 128
PEER_HEADS = 8
N_KEYS = 128
N_EXPERTS = N_KEYS * N_KEYS
PEER_DK = 256
PEER_TOPK = 16
PEER_BLOCK = 128
FORGET_BIAS_INIT = 3.0
EPS = 1e-6
GATE_FLOOR = 1e-20
MASK_VALUE = -1e30
IN_SIZES = (2 * CONV_W, HG_HEADS * HG_DK, HG_HEADS * HG_DK, HG_HEADS * HG_DV, HG_HEADS * HG_DV,
            ATT_HEADS * ATT_HD, ATT_HEADS * ATT_HD, ATT_HEADS * ATT_HD, ATT_HEADS, N_BRANCH * D_MODEL)
IN_COLS = sum(IN_SIZES)

kernel_name = 'hybrid_conv_hgrn2_fox_peer_step'

def _rmsnorm(x, g):
    xf = x.astype(jnp.float32)
    y = xf * lax.rsqrt(jnp.mean(xf * xf, axis=-1, keepdims=True) + EPS)
    return (y * g.astype(jnp.float32)).astype(x.dtype)

def _split_cols(z):
    return jnp.split(z, np.cumsum(IN_SIZES)[:-1].tolist(), axis=-1)

def _conv_branch(a, buf, w_dw, b_dw, ln_g, ln_b):
    u = a[..., :CONV_W] * jax.nn.sigmoid(a[..., CONV_W:])
    ext = jnp.concatenate([buf.astype(u.dtype), u], axis=1)
    y = lax.conv_general_dilated(ext, w_dw[:, None, :].astype(u.dtype), (1,), 'VALID',
                                 dimension_numbers=('NWC', 'WIO', 'NWC'),
                                 feature_group_count=CONV_W)
    y = y.astype(jnp.float32) + b_dw.astype(jnp.float32)
    mu = jnp.mean(y, axis=-1, keepdims=True)
    var = jnp.mean(jnp.square(y - mu), axis=-1, keepdims=True)
    y = (y - mu) * lax.rsqrt(var + EPS) * ln_g.astype(jnp.float32) + ln_b.astype(jnp.float32)
    return jax.nn.silu(y).astype(a.dtype), ext[:, -(CONV_K - 1):]

def _hgrn_lower_bounds(logits):
    p = jax.nn.softmax(logits.astype(jnp.float32), axis=0)
    return jnp.cumsum(p, axis=0) - p[0:1]

def _hgrn_branch(q, fpre, i, g, s0, lb, norm_g):
    B, L, _ = q.shape
    f32 = jnp.float32
    qh = jax.nn.silu(q.astype(f32)).reshape(B, L, HG_HEADS, HG_DK)
    lbf = jnp.clip(lb.astype(f32), 0.0, 1.0)
    f = lbf + (1.0 - lbf) * jax.nn.sigmoid(fpre.astype(f32))
    kh = (1.0 - f).reshape(B, L, HG_HEADS, HG_DK)
    logf = jnp.log(jnp.maximum(f, GATE_FLOOR)).reshape(B, L, HG_HEADS, HG_DK)
    vh = i.astype(f32).reshape(B, L, HG_HEADS, HG_DV)
    c = HG_CHUNK if L % HG_CHUNK == 0 else L
    n = L // c
    causal = jnp.tril(jnp.ones((c, c), bool))[None, :, :, None, None]

    def to_chunks(t):
        return t.reshape(B, n, c, *t.shape[2:]).swapaxes(0, 1)

    def step(S, inp):
        qc, kc, vc, lfc = inp
        b = jnp.cumsum(lfc, axis=1)
        o_inter = jnp.einsum('bthk,bhkv->bthv', qc * jnp.exp(b), S)
        decay = jnp.exp(jnp.where(causal, b[:, :, None] - b[:, None, :], MASK_VALUE))
        A = jnp.einsum('bthk,bshk,btshk->bths', qc, kc, decay)
        o = o_inter + jnp.einsum('bths,bshv->bthv', A, vc)
        b_last = b[:, -1]
        S = jnp.exp(b_last)[..., None] * S + jnp.einsum('bshk,bshv->bhkv', kc * jnp.exp(b_last[:, None] - b), vc)
        return S, o

    S, o = lax.scan(step, s0.astype(f32), (to_chunks(qh), to_chunks(kh), to_chunks(vh), to_chunks(logf)))
    o = o.swapaxes(0, 1).reshape(B, L, HG_HEADS, HG_DV)
    o = o * lax.rsqrt(jnp.mean(o * o, axis=-1, keepdims=True) + EPS) * norm_g.astype(f32)
    o = o.reshape(B, L, HG_HEADS * HG_DV) * jax.nn.sigmoid(g.astype(f32))
    return o.astype(q.dtype), S.astype(s0.dtype)

def _fox_prompt(q, k, v, logf):
    B, S, H, HD = q.shape
    nblk = S // Q_BLOCK
    c = jnp.cumsum(logf, axis=1).transpose(0, 2, 1)
    qb = q.reshape(B, nblk, Q_BLOCK, H, HD).swapaxes(0, 1)
    kpos = jnp.arange(S)
    scale = ATT_HD ** -0.5

    def block(args):
        qi, bi = args
        qpos = bi * Q_BLOCK + jnp.arange(Q_BLOCK)
        cq = lax.dynamic_slice_in_dim(c, bi * Q_BLOCK, Q_BLOCK, axis=2)
        s = jnp.einsum('bqhd,bkhd->bhqk', qi, k).astype(jnp.float32) * scale
        s = s + (cq[..., None] - c[:, :, None, :])
        s = jnp.where(kpos[None, :] <= qpos[:, None], s, MASK_VALUE)
        p = jax.nn.softmax(s, axis=-1).astype(v.dtype)
        return jnp.einsum('bhqk,bkhd->bqhd', p, v)

    o = lax.map(block, (qb, jnp.arange(nblk)))
    return o.swapaxes(0, 1).reshape(B, S, H, HD)

def _fox_sample(q, k, v, logf, ck, cv, clf, page_table):
    DB, T, H, HD = q.shape
    kp = ck[page_table].reshape(DB, -1, H, HD)
    vp = cv[page_table].reshape(DB, -1, H, HD)
    lfp = clf[page_table].reshape(DB, -1, H).astype(jnp.float32)
    P = kp.shape[1]
    c_all = jnp.cumsum(jnp.concatenate([lfp, logf], axis=1), axis=1).transpose(0, 2, 1)
    bias = c_all[:, :, P:, None] - c_all[:, :, None, :]
    scale = ATT_HD ** -0.5
    s = jnp.concatenate([jnp.einsum('bqhd,bkhd->bhqk', q, kp),
                         jnp.einsum('bqhd,bkhd->bhqk', q, k)], axis=-1).astype(jnp.float32) * scale + bias
    mask = jnp.concatenate([jnp.ones((T, P), bool), jnp.tril(jnp.ones((T, T), bool))], axis=1)
    p = jax.nn.softmax(jnp.where(mask, s, MASK_VALUE), axis=-1).astype(v.dtype)
    return jnp.einsum('bhqk,bkhd->bqhd', p[..., :P], vp) + jnp.einsum('bhqk,bkhd->bqhd', p[..., P:], v)

def _peer(x, wq, keys, u, v):
    B, L, D = x.shape
    n = B * L
    xt = jnp.pad(x.reshape(n, D), ((0, (-n) % PEER_BLOCK), (0, 0)))
    kk = PEER_TOPK * PEER_TOPK

    def block(xb):
        q = jnp.einsum('td,dc->tc', xb, wq).reshape(-1, PEER_HEADS, 2, PEER_DK // 2)
        s = jnp.einsum('thpd,hpnd->thpn', q, keys).astype(jnp.float32)
        sv, si = lax.top_k(s, PEER_TOPK)
        cand = (sv[:, :, 0, :, None] + sv[:, :, 1, None, :]).reshape(-1, PEER_HEADS, kk)
        cidx = (si[:, :, 0, :, None] * N_KEYS + si[:, :, 1, None, :]).reshape(-1, PEER_HEADS, kk)
        top_s, pos = lax.top_k(cand, PEER_TOPK)
        eidx = jnp.take_along_axis(cidx, pos, axis=-1)
        w = jax.nn.softmax(top_s, axis=-1)
        hid = jnp.einsum('td,thkd->thk', xb, u[eidx]).astype(jnp.float32)
        act = (jax.nn.gelu(hid, approximate=False) * w).astype(xb.dtype)
        return jnp.einsum('thk,thkd->td', act, v[eidx])

    out = lax.map(block, xt.reshape(-1, PEER_BLOCK, D))
    return out.reshape(-1, D)[:n].reshape(B, L, D)

def _layer(x, conv_buf, hg_state, attn_fn, l, lb, norm1_g, w_in, conv_dw, conv_db, conv_ln_g, conv_ln_b,
           hg_norm_g, att_fb, w_branch, w_out, norm2_g, peer_wq, peer_keys, peer_u, peer_v):
    B, L, _ = x.shape
    xn = _rmsnorm(x, norm1_g[l])
    z = jnp.einsum('bld,dc->blc', xn, w_in[l])
    a_conv, hq, hf, hi, hg, aq, ak, av, af, gates = _split_cols(z)
    y_conv, conv_new = _conv_branch(a_conv, conv_buf, conv_dw[l], conv_db[l], conv_ln_g[l], conv_ln_b[l])
    y_hgrn, hg_new = _hgrn_branch(hq, hf, hi, hg, hg_state, lb, hg_norm_g[l])
    k_rows = ak.reshape(B, L, ATT_HEADS, ATT_HD)
    v_rows = av.reshape(B, L, ATT_HEADS, ATT_HD)
    logf = jax.nn.log_sigmoid(af.astype(jnp.float32) + att_fb[l].astype(jnp.float32))
    y_att = attn_fn(aq.reshape(B, L, ATT_HEADS, ATT_HD), k_rows, v_rows, logf)
    branches = jnp.stack([y_conv, y_hgrn, y_att.reshape(B, L, BRANCH_W).astype(x.dtype)], axis=0)
    proj = jnp.einsum('nblw,nwd->nbld', branches, w_branch[l])
    gate = jax.nn.sigmoid(gates.reshape(B, L, N_BRANCH, D_MODEL))
    merged = jnp.einsum('blnd,nbld->bld', gate, proj)
    h = x + jnp.einsum('bld,de->ble', merged, w_out[l])
    h = h + _peer(_rmsnorm(h, norm2_g[l]), peer_wq[l], peer_keys[l], peer_u[l], peer_v[l])
    return h, conv_new, hg_new, k_rows, v_rows, logf

def setup_inputs(seed: int = 0) -> dict:
    key = jax.random.key(seed)
    ks = jax.random.split(key, 32)
    f32 = jnp.float32
    n_pages = PAST_LEN // PAGE_SIZE
    n_phys = (DEC_BATCH * n_pages * 5) // 4

    def nrm(k, shape, s):
        return s * jax.random.normal(k, shape, f32)

    inp = {}
    inp['x_prompt'] = nrm(ks[0], (BATCH, SEQ, D_MODEL), 1.0)
    inp['x_sample'] = nrm(ks[1], (DEC_BATCH, DEC_SEQ, D_MODEL), 1.0)
    inp['cache_k'] = nrm(ks[2], (DEPTH, n_phys, PAGE_SIZE, ATT_HEADS, ATT_HD), 1.0)
    inp['cache_v'] = nrm(ks[3], (DEPTH, n_phys, PAGE_SIZE, ATT_HEADS, ATT_HD), 1.0)
    inp['cache_logf'] = jax.nn.log_sigmoid(FORGET_BIAS_INIT + nrm(ks[4], (DEPTH, n_phys, PAGE_SIZE, ATT_HEADS), 1.0))
    inp['state_conv'] = nrm(ks[5], (DEPTH, DEC_BATCH, CONV_K - 1, CONV_W), 0.5)
    inp['state_hgrn'] = nrm(ks[6], (DEPTH, DEC_BATCH, HG_HEADS, HG_DK, HG_DV), 0.5)
    inp['page_table'] = jax.random.permutation(ks[7], n_phys)[:DEC_BATCH * n_pages].reshape(DEC_BATCH, n_pages).astype(jnp.int32)
    inp['norm1_g'] = 1.0 + nrm(ks[8], (DEPTH, D_MODEL), 0.01)
    inp['w_in'] = nrm(ks[9], (DEPTH, D_MODEL, IN_COLS), D_MODEL ** -0.5)
    inp['conv_dw'] = nrm(ks[10], (DEPTH, CONV_K, CONV_W), CONV_K ** -0.5)
    inp['conv_db'] = nrm(ks[11], (DEPTH, CONV_W), 0.01)
    inp['conv_ln_g'] = 1.0 + nrm(ks[12], (DEPTH, CONV_W), 0.01)
    inp['conv_ln_b'] = nrm(ks[13], (DEPTH, CONV_W), 0.01)
    inp['hg_lb_logits'] = nrm(ks[14], (DEPTH, HG_HEADS * HG_DK), 0.1)
    inp['hg_norm_g'] = 1.0 + nrm(ks[15], (DEPTH, HG_DV), 0.01)
    inp['att_fb'] = FORGET_BIAS_INIT + nrm(ks[16], (DEPTH, ATT_HEADS), 0.1)
    inp['w_branch'] = nrm(ks[17], (DEPTH, N_BRANCH, BRANCH_W, D_MODEL), BRANCH_W ** -0.5)
    inp['w_out'] = nrm(ks[18], (DEPTH, D_MODEL, D_MODEL), D_MODEL ** -0.5)
    inp['norm2_g'] = 1.0 + nrm(ks[19], (DEPTH, D_MODEL), 0.01)
    inp['peer_wq'] = nrm(ks[20], (DEPTH, D_MODEL, PEER_HEADS * PEER_DK), D_MODEL ** -0.5)
    inp['peer_keys'] = nrm(ks[21], (DEPTH, PEER_HEADS, 2, N_KEYS, PEER_DK // 2), (PEER_DK // 2) ** -0.5)
    inp['peer_u'] = nrm(ks[22], (DEPTH, N_EXPERTS, D_MODEL), D_MODEL ** -0.5)
    inp['peer_v'] = nrm(ks[23], (DEPTH, N_EXPERTS, D_MODEL), 0.5 * PEER_HEADS ** -0.5)
    inp['final_g'] = 1.0 + nrm(ks[24], (D_MODEL,), 0.01)
    return inp

def reference(x_prompt, x_sample, cache_k, cache_v, cache_logf, state_conv, state_hgrn, page_table,
              norm1_g, w_in, conv_dw, conv_db, conv_ln_g, conv_ln_b, hg_lb_logits, hg_norm_g, att_fb,
              w_branch, w_out, norm2_g, peer_wq, peer_keys, peer_u, peer_v, final_g):
    lbs = _hgrn_lower_bounds(hg_lb_logits)
    layer_w = (norm1_g, w_in, conv_dw, conv_db, conv_ln_g, conv_ln_b, hg_norm_g, att_fb,
               w_branch, w_out, norm2_g, peer_wq, peer_keys, peer_u, peer_v)
    hp, hs = x_prompt, x_sample
    bp = x_prompt.shape[0]
    rp_all, rs_all = [], []
    for l in range(DEPTH):
        buf0 = jnp.zeros((bp, CONV_K - 1, CONV_W), x_prompt.dtype)
        s0 = jnp.zeros((bp, HG_HEADS, HG_DK, HG_DV), x_prompt.dtype)
        hp, *rp = _layer(hp, buf0, s0, _fox_prompt, l, lbs[l], *layer_w)
        attn_s = functools.partial(_fox_sample, ck=cache_k[l], cv=cache_v[l], clf=cache_logf[l], page_table=page_table)
        hs, *rs = _layer(hs, state_conv[l], state_hgrn[l], attn_s, l, lbs[l], *layer_w)
        rp_all.append(rp)
        rs_all.append(rs)
    y_prompt = _rmsnorm(hp, final_g)
    y_sample = _rmsnorm(hs, final_g)
    new_conv_prompt = jnp.stack([r[0] for r in rp_all])
    new_hgrn_prompt = jnp.stack([r[1] for r in rp_all])
    new_k_prompt = jnp.stack([r[2] for r in rp_all])
    new_v_prompt = jnp.stack([r[3] for r in rp_all])
    new_logf_prompt = jnp.stack([r[4] for r in rp_all])
    new_conv_sample = jnp.stack([r[0] for r in rs_all])
    new_hgrn_sample = jnp.stack([r[1] for r in rs_all])
    new_k_sample = jnp.stack([r[2] for r in rs_all])
    new_v_sample = jnp.stack([r[3] for r in rs_all])
    new_logf_sample = jnp.stack([r[4] for r in rs_all])
    return (y_prompt, y_sample, new_k_prompt, new_v_prompt, new_logf_prompt, new_conv_prompt, new_hgrn_prompt,
            new_k_sample, new_v_sample, new_logf_sample, new_conv_sample, new_hgrn_sample)


_drawn_inputs = setup_inputs


def setup_inputs(seed=0):
    import zlib

    import numpy as np

    out = dict(_drawn_inputs(seed))
    spreads = {}
    factors = {'state_hgrn': 3.166,
     'norm1_g': 4.978,
     'conv_db': 5.847,
     'conv_ln_g': 56.806,
     'conv_ln_b': 51.695,
     'hg_norm_g': 56.318,
     'norm2_g': 41.775,
     'final_g': 32.455,
     'cache_logf': 5.815}
    for name, (base, spread) in spreads.items():
        noise = np.random.default_rng([zlib.crc32(name.encode()), seed]).standard_normal(out[name].shape)
        drawn = base * np.exp(spread * noise) if base else spread * noise
        out[name] = jnp.asarray(drawn.astype(out[name].dtype))
    for name, factor in factors.items():
        out[name] = (out[name] * factor).astype(out[name].dtype)
    return out
```

```python
from contextlib import ExitStack

import numpy as np

import concourse.bass as bass
from concourse import mybir

F32, I32, U32 = mybir.dt.float32, mybir.dt.int32, mybir.dt.uint32
ALU, ACT, AX = mybir.AluOpType, mybir.ActivationFunctionType, mybir.AxisListType

P = 128
D = 1024
KD = D // P
SEQ, DB, DT = 1024, 8, 8
NS = DB * DT
T = SEQ + NS
NT = 9
TP = NT * P
EPS = 1e-6
CHUNKS = ((0, 512), (512, 512), (1024, NS))
CONV_K, HALO = 31, 30
EXT_S = HALO + DT
PAGES, PAGE, PHYS = 8, 128, 80
LEVELS = (32, 16, 8, 4, 2, 1)
NEG = -1e30


def rows(i, n=P):
    return bass.ds(i * n, n)


class Link:

    def __init__(self, eng, sem, base=0):
        self.eng, self.sem, self.base, self.n = eng, sem, base, 0

    def __call__(self, ins):
        self.n += 1
        ins.then_inc(self.sem, 1)
        self.eng.wait_ge(self.sem, self.base + self.n)


class Place:

    def __init__(self, nc, ctx, psum=None):
        self.nc, self.ctx, self.psum, self.banks, self.sems = nc, ctx, psum, 0, []
        ctx.callback(self.clear)

    def sb(self, name, shape, dt=F32):
        return self.ctx.enter_context(self.nc.sbuf_tensor(name, shape, dt))

    def bank(self, name, banks=1):
        self.banks += banks
        return self.psum[:, 512 * (self.banks - banks):512 * self.banks]

    def sem(self, name):
        self.sems.append(self.nc.alloc_semaphore(name))
        return self.sems[-1]

    def clear(self):
        if self.sems:
            self.nc.clear_and_free_semaphores(self.sems)
            self.nc.all_engine_barrier()

    def block(self):
        return self.ctx.enter_context(self.nc.Block())


def project(pe, weights, xT, banks, ready):
    for c, (off, n) in enumerate(CHUNKS):
        for k in range(KD):
            last = pe.matmul(banks[c][:, 0:n], weights[:, k * P:(k + 1) * P], xT[:, k, off:off + n],
                             start=(k == 0), stop=(k == KD - 1))
        last.then_inc(ready, 1)


def stage_norm(nc, io, keep):
    with ExitStack() as ctx:
        m = Place(nc, ctx, keep["psum"])
        x_in, xs = m.sb("n_x", [P, 3, D]), m.sb("n_xs", [P, 3, D])
        junk, gain = m.sb("n_junk", [P, D]), m.sb("n_gain", [P, D])
        ss, rstd = m.sb("n_ss", [P, 3]), m.sb("n_rstd", [P, 3])
        pt = [m.bank(f"n_pt{u}", 2) for u in range(3)]
        x_loaded = [m.sem(f"n_x_loaded{u}") for u in range(3)]
        consts, sumsq, std, recip, scaled, turned, stored = (
            m.sem("n_" + s) for s in ("consts", "sumsq", "std", "recip", "scaled", "turned", "stored"))
        block = m.block()

        def store(act, i, u):
            act.wait_ge(turned, 3 * i + u + 1)
            act.activation(keep["xT"][:, :, rows(i * 3 + u)],
                           pt[u][:, :].rearrange("p (k t) -> p k t", k=KD), ACT.Copy).then_inc(stored, 1)

        @block.sync
        def _(sp):
            sp.dma_start(gain[:, :], io["norm1_g"].partition_broadcast(P)).then_inc(consts, 16)
            sp.dma_start(keep["ident"][:, :], io["c_ident"]).then_inc(consts, 16)
            sp.dma_start(keep["eps"][:, :], io["c_eps"]).then_inc(consts, 16)
            with sp.Fori(0, 3) as i:
                for u in range(3):
                    sp.wait_ge(scaled, 3 * i)
                    sp.dma_start(x_in[:, u, :], io["x_all"][rows(i * 3 + u), :]).then_inc(x_loaded[u], 16)

        @block.scalar
        def _(act):
            act.wait_ge(consts, 48)
            with act.Fori(0, 3) as i:
                for u in range(3):
                    act.wait_ge(x_loaded[u], i * 16 + 16)
                    act.wait_ge(recip, 3 * i)
                    act.activation(junk[:, :], x_in[:, u, :], ACT.Square, accum_out=ss[:, u:u + 1]).then_inc(sumsq, 1)
                    act.wait_ge(sumsq, 3 * i + u + 1)
                    act.activation(rstd[:, u:u + 1], ss[:, u:u + 1], ACT.Sqrt, scale=1.0 / D,
                                   bias=keep["eps"][:, 0:1]).then_inc(std, 1)
                    if u >= 1:
                        store(act, i, u - 1)
                store(act, i, 2)

        @block.vector
        def _(dve):
            dve.wait_ge(consts, 48)
            with dve.Fori(0, 3) as i:
                for u in range(3):
                    dve.wait_ge(std, 3 * i + u + 1)
                    dve.reciprocal(rstd[:, u:u + 1], rstd[:, u:u + 1]).then_inc(recip, 1)
                    dve.wait_ge(recip, 3 * i + u + 1)
                    dve.wait_ge(turned, 3 * i)
                    dve.scalar_tensor_tensor(xs[:, u, :], x_in[:, u, :], rstd[:, u:u + 1], gain[:, :],
                                             ALU.mult, ALU.mult).then_inc(scaled, 1)

        @block.tensor
        def _(pe):
            pe.wait_ge(consts, 48)
            with pe.Fori(0, 3) as i:
                for u in range(3):
                    pe.wait_ge(scaled, 3 * i + u + 1)
                    pe.wait_ge(stored, 3 * i)
                    for k in range(KD):
                        last = pe.transpose(pt[u][:, k * P:(k + 1) * P], xs[:, u, k * P:(k + 1) * P],
                                            keep["ident"][:, :])
                    last.then_inc(turned, 1)


def stage_conv(nc, io, keep):
    with ExitStack() as ctx:
        m = Place(nc, ctx, keep["psum"])
        w = [m.sb("c_w_gate", [P, KD * P]), m.sb("c_w_value", [P, KD * P])]
        sig = m.sb("c_sig", [P, T])
        ext_p, ext_s = m.sb("c_ext_p", [P, HALO + SEQ]), m.sb("c_ext_s", [P, DB, EXT_S])
        glu_s = m.sb("c_glu_s", [P, NS])
        acc_p, acc_s = m.sb("c_acc_p", [P, SEQ]), m.sb("c_acc_s", [P, DB, DT])
        y = m.sb("c_y", [P, 4, T])
        sq, std, rstd = m.sb("c_sq", [P, 4, 512]), m.sb("c_std", [P, 512]), m.sb("c_rstd", [P, 512])
        taps_all, taps = m.sb("c_taps_all", [P, 4, CONV_K + 1]), m.sb("c_taps", [P, CONV_K + 1])
        ln = m.sb("c_ln", [P, 2, 4])
        mean_w = m.sb("c_mean_w", [P, P])
        tail_p, tail_s = m.sb("c_tail_p", [HALO, 4 * P]), m.sb("c_tail_s", [NS, 4 * P])
        gate_ps = [m.bank(f"c_g{c}") for c in range(3)]
        value_ps = [m.bank(f"c_a{c}") for c in range(3)]
        tail_ps = m.bank("c_tail", 1)
        w_loaded = [m.sem("c_wg_loaded"), m.sem("c_wv_loaded")]
        (consts, halo, halo0, gate_ready, value_ready, sig_ready, glu, taps_ready, tap_done, tails, tails_out,
         mean, centred, squared, var, stdev, recip, normed, out_sem, link) = (
            m.sem("c_" + s) for s in ("consts", "halo", "halo0", "gate", "value", "sig", "glu", "taps", "tap",
                                      "tails", "tails_out", "mean", "centred", "squared", "var", "stdev", "recip",
                                      "normed", "out", "link"))
        block = m.block()

        @block.sync
        def _(sp):
            sp.dma_start(taps_all[:, :, :], io["conv_taps"]).then_inc(consts, 16)
            sp.dma_start(ln[:, :, :], io["conv_ln"]).then_inc(consts, 16)
            with sp.Fori(0, 4) as i:
                sp.wait_ge(gate_ready, 3 * i)
                sp.dma_start(w[0][:, :], io["w_conv"][rows(i * 2), :]).then_inc(w_loaded[0], 16)
                sp.wait_ge(value_ready, 3 * i)
                sp.dma_start(w[1][:, :], io["w_conv"][rows(i * 2 + 1), :]).then_inc(w_loaded[1], 16)
                sp.wait_ge(tap_done, 62 * i)
                sp.wait_ge(tails, i)
                sp.dma_start(ext_s[:, :, 0:HALO], io["state_convT"][rows(i), :, :]).then_inc(halo, 16)
            sp.dma_start(io["new_conv_sample"][0, :, 0:HALO - DT, :], io["state_conv"][0, :, DT:HALO, :]).then_inc(out_sem, 16)
            sp.wait_ge(tails_out, 8)
            sp.dma_start(io["new_conv_prompt"][0, 0, :, :], tail_p[:, :]).then_inc(out_sem, 16)
            for b in range(DB):
                sp.dma_start(io["new_conv_sample"][0, b, HALO - DT:HALO, :], tail_s[b * DT:(b + 1) * DT, :]).then_inc(out_sem, 16)
            sp.wait_ge(out_sem, 16 * (2 + DB))

        @block.gpsimd
        def _(pool):
            pool.memset(mean_w[:, :], 1.0 / 512).then_inc(halo0, 1)
            pool.memset(ext_p[:, 0:HALO], 0.0).then_inc(halo0, 1)

        @block.tensor
        def _(pe):
            with pe.Fori(0, 4) as i:
                pe.wait_ge(w_loaded[0], 16 * i + 16)
                pe.wait_ge(sig_ready, 3 * i)
                project(pe, w[0], keep["xT"], gate_ps, gate_ready)
                pe.wait_ge(w_loaded[1], 16 * i + 16)
                pe.wait_ge(glu, 3 * i)
                project(pe, w[1], keep["xT"], value_ps, value_ready)
                pe.wait_ge(glu, 3 * i + 3)
                pe.wait_ge(tails_out, 2 * i)
                pe.transpose(tail_ps[0:HALO, 0:P], ext_p[:, SEQ:SEQ + HALO], keep["ident"][:, :])
                pe.transpose(tail_ps[0:NS, P:2 * P], glu_s[:, :], keep["ident"][:, :]).then_inc(tails, 1)
            pe.wait_ge(halo0, 2)
            pe.wait_ge(tap_done, 62 * 4)
            for c, (off, n) in enumerate(CHUNKS):
                for i in range(4):
                    last = pe.matmul(gate_ps[c][:, 0:n], mean_w[:, :], y[:, i, off:off + n], start=(i == 0), stop=(i == 3))
                last.then_inc(mean, 1)
            for c, (off, n) in enumerate(CHUNKS):
                pe.wait_ge(squared, c + 1)
                for i in range(4):
                    last = pe.matmul(value_ps[c][:, 0:n], mean_w[:, :], sq[:, i, 0:n], start=(i == 0), stop=(i == 3))
                last.then_inc(var, 1)

        @block.scalar
        def _(act):
            act.wait_ge(consts, 32)
            with act.Fori(0, 4) as i:
                act.wait_ge(tap_done, 62 * i)
                act.activation(taps[:, :], taps_all[:, rows(i, 1), :], ACT.Copy).then_inc(taps_ready, 1)
                for c, (off, n) in enumerate(CHUNKS):
                    act.wait_ge(gate_ready, 3 * i + c + 1)
                    act.wait_ge(glu, 3 * i)
                    act.activation(sig[:, off:off + n], gate_ps[c][:, 0:n], ACT.Sigmoid).then_inc(sig_ready, 1)
                act.wait_ge(tails, i + 1)
                act.activation(tail_p[:, rows(i)], tail_ps[0:HALO, 0:P], ACT.Copy).then_inc(tails_out, 1)
                act.activation(tail_s[:, rows(i)], tail_ps[0:NS, P:2 * P], ACT.Copy).then_inc(tails_out, 1)
            for c, (off, n) in enumerate(CHUNKS):
                act.wait_ge(centred, c + 1)
                act.wait_ge(var, c)
                act.activation(sq[:, :, 0:n], y[:, :, off:off + n], ACT.Square).then_inc(squared, 1)
                act.wait_ge(var, c + 1)
                act.wait_ge(recip, c)
                act.activation(std[:, 0:n], value_ps[c][:, 0:n], ACT.Sqrt, bias=keep["eps"][:, 0:1]).then_inc(stdev, 1)
                act.wait_ge(normed, c + 1)
                for i in range(4):
                    act.activation(keep["branch"][:, i, off:off + n], y[:, i, off:off + n], ACT.Silu,
                                   scale=ln[:, 0, i:i + 1], bias=ln[:, 1, i:i + 1]).then_inc(link, 1)

        @block.vector
        def _(dve):
            dve.wait_ge(halo0, 2)
            with dve.Fori(0, 4) as i:
                dve.wait_ge(tap_done, 62 * i)
                dve.wait_ge(tails, i)
                for c, (off, n) in enumerate(CHUNKS):
                    dve.wait_ge(sig_ready, 3 * i + c + 1)
                    dve.wait_ge(value_ready, 3 * i + c + 1)
                    if c < 2:
                        dve.tensor_tensor(ext_p[:, HALO + off:HALO + off + n], value_ps[c][:, 0:n], sig[:, off:off + n],
                                          ALU.mult).then_inc(glu, 1)
                    else:
                        dve.tensor_tensor(glu_s[:, :], value_ps[c][:, 0:n], sig[:, off:off + n], ALU.mult)
                        dve.tensor_tensor(ext_s[:, :, HALO:EXT_S], value_ps[c][:, 0:n].rearrange("p (b t) -> p b t", b=DB),
                                          sig[:, off:off + n].rearrange("p (b t) -> p b t", b=DB), ALU.mult).then_inc(glu, 1)
                dve.wait_ge(taps_ready, i + 1)
                dve.wait_ge(halo, 16 * i + 16)
                dve.wait_ge(glu, 3 * i + 3)
                for j in range(CONV_K):
                    last_tap = j == CONV_K - 1
                    out_p = y[:, rows(i, 1), 0:SEQ] if last_tap else acc_p[:, :]
                    out_s = (y[:, rows(i, 1), SEQ:T].rearrange("p a (b t) -> p (a b) t", b=DB) if last_tap
                             else acc_s[:, :, :])
                    for s, (out, win, prev) in enumerate(((out_p, ext_p[:, j:j + SEQ], acc_p[:, :]),
                                                          (out_s, ext_s[:, :, j:j + DT], acc_s[:, :, :]))):
                        if j == 0:
                            ins = dve.tensor_scalar(out, win, taps[:, 0:1], taps[:, CONV_K:CONV_K + 1], ALU.mult, ALU.add)
                        else:
                            dve.wait_ge(tap_done, 62 * i + 2 * (j - 1) + s + 1)
                            ins = dve.scalar_tensor_tensor(out, win, taps[:, j:j + 1], prev, ALU.mult, ALU.add)
                        ins.then_inc(tap_done, 1)
            for c, (off, n) in enumerate(CHUNKS):
                dve.wait_ge(mean, c + 1)
                dve.tensor_tensor(y[:, :, off:off + n], y[:, :, off:off + n],
                                  gate_ps[c][:, 0:n].unsqueeze(1).broadcast_to([P, 4, n]), ALU.subtract).then_inc(centred, 1)
            for c, (off, n) in enumerate(CHUNKS):
                dve.wait_ge(stdev, c + 1)
                dve.reciprocal(rstd[:, 0:n], std[:, 0:n]).then_inc(recip, 1)
                dve.wait_ge(recip, c + 1)
                dve.wait_ge(squared, c + 1)
                dve.tensor_tensor(y[:, :, off:off + n], y[:, :, off:off + n],
                                  rstd[:, 0:n].unsqueeze(1).broadcast_to([P, 4, n]), ALU.mult).then_inc(normed, 1)


def stage_hgrn(nc, io, keep):
    with ExitStack() as ctx:
        m = Place(nc, ctx, keep["psum"])
        w = [m.sb(f"h_w{u}", [P, KD * P]) for u in range(2)]
        q, k, b = m.sb("h_q", [P, T]), m.sb("h_k", [P, T]), m.sb("h_b", [P, T])
        f, gate, lf = m.sb("h_f", [P, T]), m.sb("h_gate", [P, T]), m.sb("h_lf", [P, T])
        v = m.sb("h_v", [P, NT, P])
        reset = m.sb("h_reset", [P, T])
        decay, qe, ke = m.sb("h_decay", [P, T]), m.sb("h_qe", [P, T]), m.sb("h_ke", [P, T])
        qk = m.sb("h_qk", [P, len(LEVELS), T])
        masks = m.sb("h_masks", [P, 7, P])
        picked = m.sb("h_picked", [P, 7, P])
        at = [m.sb(f"h_at{u}", [P, P]) for u in range(2)]
        keT = m.sb("h_keT", [P, 2, P])
        state = m.sb("h_state", [P, 2, P])
        s_old, s_new, v_batch = m.sb("h_s_old", [P, DB, P]), m.sb("h_s_new", [P, DB, P]), m.sb("h_v_batch", [NS, DB, P])
        batch = m.sb("h_batch", [NS, DB])
        o, sq, std = m.sb("h_o", [P, T]), lf, f
        mean_w, lb, gain = m.sb("h_mean_w", [P, P]), m.sb("h_lb", [P, 8, 4]), m.sb("h_gain", [P, 1])
        pz = [m.bank(f"h_z{c}") for c in range(6)]
        pa6 = m.bank("h_a6", 2)
        pa = [pa6[:, 0:7 * P], None]
        p_turn, p_o, p_ds = pz[2], pz[3], pz[4]
        w_loaded = [m.sem(f"h_w{u}_loaded") for u in range(2)]
        (consts, pool_done, s_loaded, q_z, f_z, g_z, v_z, q_ok, f_ok, g_ok, v_ok, k_ok, fm_ok, lf_ok, b_ok, eb_ok, kd_sub, kd_exp,
         ke_ok, qe_ok, lv_sub, lv_exp, qk_ok, a_ok, at_ok, turn, turned, ds, st_ok, o_ps, o_ok, vb_ok, sq_ok, ms, sd_ok,
         rs_ok, y_ok, out_ok, link, tmp_ok, pick_ok, dss) = (
            m.sem("h_" + s) for s in (
                "consts pool s_loaded q_z f_z g_z v_z q_ok f_ok g_ok v_ok k_ok fm_ok lf_ok b_ok eb_ok kd_sub kd_exp ke_ok qe_ok "
                "lv_sub lv_exp qk_ok a_ok at_ok turn turned ds st_ok o_ps o_ok vb_ok sq_ok ms sd_ok rs_ok y_ok out link tmp "
                "pick_ok dss").split())
        NL = len(LEVELS)
        block = m.block()

        def halves(x, level):
            h = LEVELS[level]
            end = T if 2 * h <= DT else SEQ
            v4 = x[:, 0:end].rearrange("p (n s h) -> p n s h", s=2, h=h)
            return v4[:, :, 0, :], v4[:, :, 1, :], v4[:, :, 0, h - 1:h].broadcast_to([P, end // (2 * h), h])

        @block.sync
        def _(sp):
            sp.dma_start(reset[:, :], io["c_reset"].partition_broadcast(P)).then_inc(consts, 16)
            sp.dma_start(masks[:, :, :], io["c_levels"]).then_inc(consts, 16)
            sp.dma_start(batch[:, :], io["c_batch"]).then_inc(consts, 16)
            sp.dma_start(lb[:, 0, :], io["hg_lb"]).then_inc(consts, 16)
            sp.dma_start(gain[:, :], io["hg_norm"]).then_inc(consts, 16)
            with sp.Fori(0, 4) as i:
                for n, used in enumerate((g_z, v_z, None, None)):
                    u = n % 2
                    if used is None:
                        sp.wait_ge((q_z, f_z)[u], 3 * i + 3)
                    else:
                        sp.wait_ge(used, 3 * i)
                    sp.dma_start(w[u][:, :], io["w_hgrn"][rows(4 * i + n), :]).then_inc(w_loaded[u], 16)
                sp.wait_ge(dss, i)
                sp.dma_start(s_old[:, :, :], io["state_hgrn"][rows(i), :, :]).then_inc(s_loaded, 16)
                sp.wait_ge(dss, i + 1)
                sp.dma_start(io["new_hgrn_sample"][0].rearrange("b h k v -> h k b v")[bass.ds(i, 1)].rearrange("a k b v -> (a k) b v"), s_new[:, :, :]).then_inc(out_ok, 16)
                sp.dma_start(io["new_hgrn_prompt"][0, 0][bass.ds(i, 1)].rearrange("a k v -> (a k) v"), state[:, 0, :]).then_inc(out_ok, 16)
            sp.wait_ge(out_ok, 16 * 8)

        @block.gpsimd
        def _(pool):
            pool.memset(mean_w[:, :], 1.0 / P).then_inc(pool_done, 1)

        @block.tensor
        def _(pe):
            pe.wait_ge(pool_done, 1)
            with pe.Fori(0, 4) as i:
                pe.wait_ge(w_loaded[0], 32 * i + 16)
                pe.wait_ge(sd_ok, i)
                project(pe, w[0], keep["xT"], pz[0:3], q_z)
                pe.wait_ge(w_loaded[1], 32 * i + 16)
                pe.wait_ge(o_ok, NT * i)
                pe.wait_ge(dss, i)
                project(pe, w[1], keep["xT"], pz[3:6], f_z)
                pe.wait_ge(w_loaded[0], 32 * i + 32)
                pe.wait_ge(q_ok, 3 * i + 3)
                project(pe, w[0], keep["xT"], pz[0:3], g_z)
                pe.wait_ge(w_loaded[1], 32 * i + 32)
                pe.wait_ge(f_ok, 3 * i + 3)
                for t in range(NT):
                    for kk in range(KD):
                        last = pe.matmul(pz[3 + t // 4][:, t % 4 * P:(t % 4 + 1) * P], keep["xT"][:, kk, t * P:(t + 1) * P],
                                         w[1][:, kk * P:(kk + 1) * P], start=(kk == 0), stop=(kk == KD - 1))
                    if t % 4 == 3 or t == NT - 1:
                        last.then_inc(v_z, 1)
                pe.wait_ge(qk_ok, NL * i + NL)
                pe.wait_ge(v_ok, 3 * i + 3)
                pe.wait_ge(g_ok, 3 * i + 3)
                for t in range(NT):
                    n = P if t < NT - 1 else NS
                    cols = slice(t * P, t * P + n)
                    pe.wait_ge(ke_ok, i + 1)
                    pe.wait_ge(turned, NT * i + t)
                    pe.wait_ge(at_ok, NT * i + t)
                    first = 0 if t < NT - 1 else 3
                    for lv in range(first, NL + 1):
                        a, bb = (qk[:, lv, cols], qk[:, lv, cols]) if lv < NL else (k[:, cols], q[:, cols])
                        last = pe.matmul(pa6[0:n, lv * P:lv * P + n], a, bb, start=True, stop=True)
                    last.then_inc(a_ok, 1)
                    pe.transpose(p_turn[0:n, 0:P], ke[:, cols], keep["ident"][:, :]).then_inc(turn, 1)
                    pe.wait_ge(at_ok, NT * i + t + 1)
                    pe.wait_ge(o_ok, NT * i + t)
                    pe.wait_ge(qe_ok, i + 1)
                    if t < NT - 1:
                        pe.matmul(p_o[:, 0:P], v[:, t, :], at[t % 2][:, :], start=True, stop=False, skip_group_check=True)
                        pe.wait_ge(turned, NT * i + t + 1)
                        for c in range(2):
                            pe.wait_ge(st_ok, 17 * i + 2 * t + c + 1)
                            last = pe.matmul(p_o[:, c * 64:c * 64 + 64], state[:, c, :], qe[:, t * P + c * 64:t * P + c * 64 + 64],
                                             start=False, stop=(c == 1), skip_group_check=True)
                            if c == 1:
                                last.then_inc(o_ps, 1)
                            pe.matmul(p_ds[:, c * P:(c + 1) * P], keT[c * 64:c * 64 + 64, t % 2, :], v[c * 64:c * 64 + 64, t, :],
                                      start=True, stop=True).then_inc(ds, 1)
                    else:
                        pe.matmul(p_o[:, 0:n], v[0:n, t, :], at[t % 2][0:n, 0:n], start=True, stop=False, skip_group_check=True)
                        pe.wait_ge(s_loaded, 16 * i + 16)
                        for bt in range(DB):
                            last = pe.matmul(p_o[:, bt * DT:(bt + 1) * DT], s_old[:, bt, :], qe[:, SEQ + bt * DT:SEQ + (bt + 1) * DT],
                                             start=False, stop=(bt == DB - 1), skip_group_check=True)
                        last.then_inc(o_ps, 1)
                        pe.wait_ge(turned, NT * i + t + 1)
                        pe.wait_ge(vb_ok, i + 1)
                        pe.wait_ge(st_ok, 17 * i + 17)
                        for hf in range(2):
                            last = pe.matmul(pz[4 + hf][:, :], keT[0:n, t % 2, :], v_batch[:, 4 * hf:4 * hf + 4, :], start=True, stop=True)
                        last.then_inc(ds, 1)
                pe.wait_ge(sq_ok, i + 1)
                for c, (off, n) in enumerate(CHUNKS):
                    last = pe.matmul(pz[c][:, 0:n], mean_w[:, :], sq[:, off:off + n], start=True, stop=True)
                last.then_inc(ms, 1)

        @block.scalar
        def _(act):
            act.wait_ge(consts, 80)
            with act.Fori(0, 4) as i:
                act.wait_ge(y_ok, i)
                for c, (off, n) in enumerate(CHUNKS):
                    act.wait_ge(q_z, 3 * i + c + 1)
                    act.activation(q[:, off:off + n], pz[c][:, 0:n], ACT.Silu).then_inc(q_ok, 1)
                for c, (off, n) in enumerate(CHUNKS):
                    act.wait_ge(f_z, 3 * i + c + 1)
                    act.activation(f[:, off:off + n], pz[3 + c][:, 0:n], ACT.Sigmoid).then_inc(f_ok, 1)
                for c, (off, n) in enumerate(CHUNKS):
                    act.wait_ge(g_z, 3 * i + c + 1)
                    act.activation(gate[:, off:off + n], pz[c][:, 0:n], ACT.Sigmoid).then_inc(g_ok, 1)
                act.wait_ge(fm_ok, i + 1)
                act.activation(lf[:, :], lf[:, :], ACT.Ln).then_inc(lf_ok, 1)
                for c in range(3):
                    act.wait_ge(v_z, 3 * i + c + 1)
                    if c < 2:
                        act.activation(v[:, 4 * c:4 * c + 4, :], pz[3 + c][:, :].rearrange("p (a n) -> p a n", a=4), ACT.Copy).then_inc(v_ok, 1)
                    else:
                        act.activation(v[:, 8, :], pz[5][:, 0:P], ACT.Copy).then_inc(v_ok, 1)
                act.wait_ge(b_ok, i + 1)
                act.activation(decay[:, :], b[:, :], ACT.Exp).then_inc(eb_ok, 1)
                act.wait_ge(kd_sub, i + 1)
                act.activation(ke[:, :], ke[:, :], ACT.Exp).then_inc(kd_exp, 1)
                for lv in range(NL):
                    end = T if 2 * LEVELS[lv] <= DT else SEQ
                    act.wait_ge(lv_sub, NL * i + lv + 1)
                    act.activation(qk[:, lv, 0:end], qk[:, lv, 0:end], ACT.Exp).then_inc(lv_exp, 1)
                for t in range(NT):
                    n = P if t < NT - 1 else NS
                    act.wait_ge(turn, NT * i + t + 1)
                    if t >= 2:
                        act.wait_ge(ds, 17 * i + 2 * t - 2)
                    act.activation(keT[0:n, t % 2, :], p_turn[0:n, 0:P], ACT.Copy).then_inc(turned, 1)
                    act.wait_ge(o_ps, NT * i + t + 1)
                    act.activation(o[:, t * P:t * P + n], p_o[:, 0:n], ACT.Copy).then_inc(o_ok, 1)
                act.wait_ge(o_ok, NT * i + NT)
                act.activation(sq[:, :], o[:, :], ACT.Square).then_inc(sq_ok, 1)
                act.wait_ge(ms, i + 1)
                for c, (off, n) in enumerate(CHUNKS):
                    last = act.activation(std[:, off:off + n], pz[c][:, 0:n], ACT.Sqrt, bias=keep["eps"][:, 0:1])
                last.then_inc(sd_ok, 1)

        @block.vector
        def _(dve):
            lk = Link(dve, link)
            dve.wait_ge(consts, 80)
            lk(dve.tensor_tensor(lb[:, 1, :], lb[:, 0, :], lb[:, 0, :], ALU.max))
            lk(dve.tensor_tensor(lb[:, 2, :], lb[:, 0, :], lb[:, 1, :], ALU.subtract))
            lk(dve.tensor_scalar(lb[:, 3, :], lb[:, 2, :], 1.0, None, ALU.add))
            lk(dve.reciprocal(lb[:, 4, :], lb[:, 3, :]))
            lk(dve.tensor_tensor(lb[:, 4, :], lb[:, 3, :], lb[:, 4, :], ALU.mult))
            lk(dve.tensor_tensor(lb[:, 5, :], lb[:, 4, :], lb[:, 4, :], ALU.subtract))
            lk(dve.tensor_scalar(lb[:, 5, :], lb[:, 5, :], 0.0, 1.0, ALU.max, ALU.min))
            lk(dve.tensor_scalar(lb[:, 6, :], lb[:, 5, :], -1.0, 1.0, ALU.mult, ALU.add))
            dve.wait_ge(pool_done, 1)
            with dve.Fori(0, 4) as i:
                dve.wait_ge(f_ok, 3 * i + 3)
                dve.tensor_scalar(f[:, :], f[:, :], lb[:, 6, bass.ds(i, 1)], lb[:, 5, bass.ds(i, 1)], ALU.mult, ALU.add).then_inc(tmp_ok, 1)
                dve.wait_ge(tmp_ok, 2 * i + 1)
                dve.tensor_scalar(lf[:, :], f[:, :], 1e-20, None, ALU.max).then_inc(fm_ok, 1)
                dve.tensor_scalar(k[:, :], f[:, :], -1.0, 1.0, ALU.mult, ALU.add).then_inc(k_ok, 1)
                dve.wait_ge(lf_ok, i + 1)
                dve.tensor_tensor_scan(b[:, :], reset[:, :], lf[:, :], 0.0, ALU.mult, ALU.add).then_inc(b_ok, 1)
                dve.wait_ge(b_ok, i + 1)
                bp, bs = b[:, 0:SEQ].rearrange("p (n c) -> p n c", c=64), b[:, SEQ:T].rearrange("p (n c) -> p n c", c=DT)
                kp, ks = ke[:, 0:SEQ].rearrange("p (n c) -> p n c", c=64), ke[:, SEQ:T].rearrange("p (n c) -> p n c", c=DT)
                dve.tensor_tensor(kp, bp[:, :, 63:64].broadcast_to([P, 16, 64]), bp, ALU.subtract)
                dve.tensor_tensor(ks, bs[:, :, DT - 1:DT].broadcast_to([P, DB, DT]), bs, ALU.subtract).then_inc(kd_sub, 1)
                for lv in range(NL):
                    bl, br, ref = halves(b, lv)
                    xl, xr, _ = halves(qk[:, lv, :], lv)
                    dve.tensor_tensor(xl, ref, bl, ALU.subtract)
                    dve.tensor_tensor(xr, br, ref, ALU.subtract).then_inc(lv_sub, 1)
                dve.wait_ge(eb_ok, i + 1)
                dve.wait_ge(q_ok, 3 * i + 3)
                dve.tensor_tensor(qe[:, :], q[:, :], decay[:, :], ALU.mult).then_inc(qe_ok, 1)
                dve.wait_ge(kd_exp, i + 1)
                dve.wait_ge(k_ok, i + 1)
                dve.tensor_tensor(ke[:, :], ke[:, :], k[:, :], ALU.mult).then_inc(ke_ok, 1)
                for lv in range(NL):
                    kl, _, _ = halves(k, lv)
                    _, qr, _ = halves(q, lv)
                    xl, xr, _ = halves(qk[:, lv, :], lv)
                    dve.wait_ge(lv_exp, NL * i + lv + 1)
                    dve.tensor_tensor(xl, xl, kl, ALU.mult)
                    dve.tensor_tensor(xr, xr, qr, ALU.mult).then_inc(qk_ok, 1)
                dve.wait_ge(out_ok, 32 * i)
                dve.memset(state[:, 0, :], 0.0).then_inc(st_ok, 1)
                for t in range(NT):
                    n = P if t < NT - 1 else NS
                    dve.wait_ge(a_ok, NT * i + t + 1)
                    if t >= 2:
                        dve.wait_ge(o_ps, NT * i + t - 1)
                    first = 0 if t < NT - 1 else 3
                    products = pa6[0:n, 0:7 * P].rearrange("p (l t) -> p l t", l=7)[:, first:, 0:n]
                    dve.wait_ge(at_ok, NT * i + t)
                    dve.tensor_tensor(picked[0:n, first:, 0:n], products, masks[0:n, first:, 0:n], ALU.mult).then_inc(pick_ok, 1)
                    dve.wait_ge(pick_ok, NT * i + t + 1)
                    dve.tensor_reduce(at[t % 2][0:n, 0:n], picked[0:n, first:, 0:n].rearrange("p l t -> p t l"), AX.X, ALU.add).then_inc(at_ok, 1)
                    if t < NT - 1:
                        for c in range(2):
                            dve.wait_ge(ds, 17 * i + 2 * t + c + 1)
                            dve.wait_ge(st_ok, 17 * i + 2 * t + c + 1)
                            end = t * P + c * 64 + 63
                            dve.scalar_tensor_tensor(state[:, 1 - c, :], state[:, c, :], decay[:, end:end + 1],
                                                     p_ds[:, c * P:(c + 1) * P], ALU.mult, ALU.add).then_inc(st_ok, 1)
                    else:
                        dve.wait_ge(v_ok, 3 * i + 3)
                        dve.tensor_tensor(v_batch[:, :, :], v[0:NS, t, :].unsqueeze(1).broadcast_to([NS, DB, P]),
                                          batch[:, :].unsqueeze(2).broadcast_to([NS, DB, P]), ALU.mult).then_inc(vb_ok, 1)
                        dve.wait_ge(s_loaded, 16 * i + 16)
                        ends = decay[:, SEQ:T].rearrange("p (n c) -> p n c", c=DT)[:, :, DT - 1:DT]
                        dve.tensor_tensor(s_new[:, :, :], s_old[:, :, :], ends.broadcast_to([P, DB, P]), ALU.mult).then_inc(tmp_ok, 1)
                        dve.wait_ge(tmp_ok, 2 * i + 2)
                        dve.wait_ge(ds, 17 * i + 17)
                        dve.wait_ge(o_ps, NT * i + NT)
                        for hf in range(2):
                            last = dve.tensor_tensor(s_new[:, 4 * hf:4 * hf + 4, :], s_new[:, 4 * hf:4 * hf + 4, :],
                                                     pz[4 + hf][:, :].rearrange("p (b v) -> p b v", b=4), ALU.add)
                        last.then_inc(dss, 1)
                dve.wait_ge(sd_ok, i + 1)
                dve.reciprocal(std[:, :], std[:, :]).then_inc(rs_ok, 1)
                dve.wait_ge(rs_ok, 2 * i + 1)
                dve.scalar_tensor_tensor(o[:, :], o[:, :], gain[:, 0:1], std[:, :], ALU.mult, ALU.mult).then_inc(rs_ok, 1)
                dve.wait_ge(rs_ok, 2 * i + 2)
                dve.tensor_tensor(keep["branch"][:, bass.ds(i + 4, 1), :], o[:, :], gate[:, :], ALU.mult).then_inc(y_ok, 1)


def stage_fox(nc, io, keep):
    with ExitStack() as ctx:
        m = Place(nc, ctx, keep["psum"])
        w = [m.sb(f"f_w{u}", [P, KD * P]) for u in range(3)]
        w_af = m.sb("f_w_af", [P, KD * 64])
        q = [m.sb(f"f_q{u}", [P, SEQ]) for u in range(2)]
        kT, v, k_tok = m.sb("f_kT", [P, T]), m.sb("f_v", [P, NT, P]), m.sb("f_k_tok", [P, NT, P])
        bias_q = [m.sb(f"f_bias_q{u}", [64, SEQ]) for u in range(2)]
        bias_k, a, lf = m.sb("f_bias_k", [64, T]), m.sb("f_a", [64, T]), m.sb("f_lf", [64, T])
        e1, reset = m.sb("f_e1", [64, T]), m.sb("f_reset", [64, T])
        lf_tok = m.sb("f_lf_tok", [P, NT, 8])
        row_coef, heads, fb = m.sb("f_rows", [64, 2]), m.sb("f_heads", [64, 2, 8]), m.sb("f_fb", [64, 1])
        causal = m.sb("f_causal", [P, P])
        p, pT = m.sb("f_p", [P, 2, SEQ]), m.sb("f_pT", [P, 2, SEQ])
        nmax, rsum, rinv, diag = m.sb("f_nmax", [P, 2]), m.sb("f_rsum", [P, 2]), m.sb("f_rinv", [P, 2]), m.sb("f_diag", [P, 2, P])
        ps = [m.bank(f"f_s{u}", 2) for u in range(2)]
        pt = [m.bank(f"f_t{u}") for u in range(2)]
        po = [m.bank(f"f_o{u}") for u in range(2)]
        pz = [ps[0][:, 0:512], ps[0][:, 512:1024], ps[1][:, 0:512], ps[1][:, 512:1024], pt[0], pt[1]]
        w_loaded = [m.sem(f"f_w{u}_loaded") for u in range(3)]
        (consts, af_loaded, pool_done, af_z, a_ok, abs_ok, exp0_ok, ln_ok, lf_ok, c_ok, lft, lft_ok, bk_ok, q_z, k_z, v_z,
         q_ok, k_ok, v_ok, kt_ps, kt_ok, bq_ok, s_ps, max_ok, exp_ok, ri_ok, diag_ok, t0_ps, t1_ps, t0_ok, t1_ok, pv, o_ok, stored) = (
            m.sem("f_" + s) for s in (
                "consts af_loaded pool af_z a_ok abs_ok exp0_ok ln_ok lf_ok c_ok lft lft_ok bk_ok q_z k_z v_z q_ok k_ok v_ok kt_ps kt_ok "
                "bq_ok s_ps max_ok exp_ok ri_ok diag_ok t0_ps t1_ps t0_ok t1_ok pv o_ok stored").split())
        block = m.block()
        UNITS = [(qi, hh) for qi in range(8) for hh in range(2)]
        cs, qs_s, ks_s, vs_s = keep["c_new"], keep["q_new"], keep["k_new"], keep["v_new"]

        def tokens(name, width):
            return io[name + "_prompt"].rearrange(f"a b (t p) {width} -> p (a b t) ({width})", p=P)

        @block.sync
        def _(sp):
            sp.dma_start(w_af[:, :], io["w_af"]).then_inc(af_loaded, 16)
            for dst, src in ((row_coef, "c_rows"), (heads, "c_heads"), (fb, "att_fb"), (causal, "c_causal")):
                sp.dma_start(dst[:], io[src]).then_inc(consts, 16)
            sp.dma_start(reset[:, :], io["c_reset_c"].partition_broadcast(64)).then_inc(consts, 16)
            with sp.Fori(0, 4) as i:
                for u, used in enumerate((q_z, k_z, v_z)):
                    sp.wait_ge(used, 3 * i)
                    sp.dma_start(w[u][:, :], io["w_fox"][rows(3 * i + u), :]).then_inc(w_loaded[u], 16)
                for src, ok, name in ((v, v_ok, "new_v"), (k_tok, kt_ok, "new_k")):
                    sp.wait_ge(ok, 3 * i + 3)
                    sp.dma_start(tokens(name, "h d")[:, :, rows(i)], src[:, 0:8, :]).then_inc(stored, 16)
                    sp.dma_start(io[name + "_sample"].rearrange("a b t h d -> (a b t) (h d)")[:, rows(i)], src[0:NS, 8, :]).then_inc(stored, 16)
            sp.wait_ge(lft_ok, 2)
            with nc.allow_non_contiguous_dma(reason="8 values per token"):
                sp.dma_start(tokens("new_logf", "h"), lf_tok[:, 0:8, :]).then_inc(stored, 16)
                sp.dma_start(io["new_logf_sample"].rearrange("a b t h -> (a b t) h"), lf_tok[0:NS, 8, :]).then_inc(stored, 16)
            sp.wait_ge(stored, 16 * 18)

        @block.gpsimd
        def _(pool):
            pool.memset(q[0][64:P, :], 0.0).then_inc(pool_done, 1)
            pool.memset(q[1][0:64, :], 0.0).then_inc(pool_done, 1)

        @block.tensor
        def _(pe):
            pe.wait_ge(af_loaded, 16)
            for c, (off, n) in enumerate(CHUNKS):
                for kk in range(KD):
                    last = pe.matmul(pz[c][0:64, 0:n], w_af[:, kk * 64:(kk + 1) * 64], keep["xT"][:, kk, off:off + n],
                                     start=(kk == 0), stop=(kk == KD - 1))
                last.then_inc(af_z, 1)
            pe.wait_ge(lf_ok, 1)
            for t in range(NT):
                n = P if t < 8 else NS
                last = pe.transpose(po[t // 8][0:n, t % 8 * 64:t % 8 * 64 + 64], lf[:, t * P:t * P + n], keep["ident"][0:64, 0:64])
            last.then_inc(lft, 1)
            pe.wait_ge(pool_done, 2)

            def scores(i, n_unit):
                qi, hh = UNITS[n_unit]
                u = n_unit % 2
                if n_unit >= 2:
                    pe.wait_ge(exp_ok, 16 * i + n_unit - 1)
                for part in range(qi // 4 + 1):
                    n = min(512, (qi + 1) * P - part * 512)
                    out, keys = ps[u][:, part * 512:part * 512 + n], slice(part * 512, part * 512 + n)
                    pe.matmul(out, q[hh][:, qi * P:(qi + 1) * P], kT[:, keys], start=True, stop=False, skip_group_check=True)
                    last = pe.matmul(out, bias_q[hh][:, qi * P:(qi + 1) * P], bias_k[:, keys], start=False,
                                     stop=(part < qi // 4), skip_group_check=True)
                last = pe.matmul(ps[u][:, qi * P:(qi + 1) * P], keep["ident"][:, :], causal[:, :], start=False, stop=True,
                                 skip_group_check=True)
                last.then_inc(s_ps, 1)

            def turn(i, n_unit):
                qi, hh = UNITS[n_unit]
                u = n_unit % 2
                pe.wait_ge(diag_ok, 16 * i + n_unit + 1)
                for part in range(qi // 4 + 1):
                    done = 16 * i + n_unit if part == 0 else 8 * i + n_unit - 8
                    pe.wait_ge((t0_ok, t1_ok)[part], done)
                    for kb in range(4 * part, min(4 * part + 4, qi + 1)):
                        last = pe.matmul(pt[part][:, kb % 4 * P:kb % 4 * P + P], p[:, u, kb * P:(kb + 1) * P], diag[:, u, :],
                                         start=True, stop=True)
                    last.then_inc((t0_ps, t1_ps)[part], 1)

            def values(i, n_unit):
                qi, hh = UNITS[n_unit]
                u = n_unit % 2
                pe.wait_ge(t0_ok, 16 * i + n_unit + 1)
                if qi >= 4:
                    pe.wait_ge(t1_ok, 8 * i + n_unit - 7)
                if hh == 0 and qi >= 2:
                    pe.wait_ge(o_ok, 8 * i + qi - 1)
                for kb in range(qi + 1):
                    last = pe.matmul(po[qi % 2][hh * 64:(hh + 1) * 64, 0:P], v[:, kb, hh * 64:(hh + 1) * 64],
                                     pT[:, u, kb * P:(kb + 1) * P], start=(kb == 0), stop=(kb == qi))
                last.then_inc(pv, 1)

            with pe.Fori(0, 4) as i:
                pe.wait_ge(w_loaded[0], 16 * i + 16)
                pe.wait_ge(a_ok, 3)
                pe.wait_ge(exp_ok, 16 * i)
                project(pe, w[0], keep["xT"], pz[0:3], q_z)
                pe.wait_ge(w_loaded[1], 16 * i + 16)
                pe.wait_ge(t0_ok, 16 * i)
                pe.wait_ge(t1_ok, 8 * i)
                project(pe, w[1], keep["xT"], pz[3:6], k_z)
                pe.wait_ge(w_loaded[2], 16 * i + 16)
                pe.wait_ge(q_ok, 3 * i + 3)
                for t in range(NT):
                    for kk in range(KD):
                        last = pe.matmul(pz[t // 4][:, t % 4 * P:(t % 4 + 1) * P], keep["xT"][:, kk, t * P:(t + 1) * P],
                                         w[2][:, kk * P:(kk + 1) * P], start=(kk == 0), stop=(kk == KD - 1))
                    if t % 4 == 3 or t == NT - 1:
                        last.then_inc(v_z, 1)
                pe.wait_ge(k_ok, 3 * i + 3)
                for t in range(NT):
                    n = P if t < 8 else NS
                    last = pe.transpose(pz[3 + t // 4][0:n, t % 4 * P:(t % 4 + 1) * P], kT[:, t * P:t * P + n], keep["ident"][:, :])
                    if t % 4 == 3 or t == NT - 1:
                        last.then_inc(kt_ps, 1)
                pe.wait_ge(v_ok, 3 * i + 3)
                pe.wait_ge(kt_ok, 3 * i + 3)
                pe.wait_ge(bq_ok, 2 * i + 2)
                pe.wait_ge(lft_ok, 2)
                pe.wait_ge(o_ok, 8 * i)
                scores(i, 0)
                for n_unit in range(16):
                    if n_unit + 1 < 16:
                        scores(i, n_unit + 1)
                    if n_unit >= 1:
                        values(i, n_unit - 1)
                    turn(i, n_unit)
                values(i, 15)

        @block.scalar
        def _(act):
            act.wait_ge(consts, 80)
            for c, (off, n) in enumerate(CHUNKS):
                act.wait_ge(af_z, c + 1)
                act.activation(a[:, off:off + n], pz[c][0:64, 0:n], ACT.Identity, bias=fb[:, 0:1]).then_inc(a_ok, 1)
            act.wait_ge(a_ok, 3)
            act.activation(e1[:, :], a[:, :], ACT.Abs).then_inc(abs_ok, 1)
            act.wait_ge(abs_ok, 1)
            act.activation(e1[:, :], e1[:, :], ACT.Exp, scale=-1.0).then_inc(exp0_ok, 1)
            act.wait_ge(exp0_ok, 1)
            act.activation(e1[:, :], e1[:, :], ACT.Ln, bias=1.0).then_inc(ln_ok, 1)
            act.wait_ge(lft, 1)
            act.activation(lf_tok[:, 0:8, :], po[0][:, :].rearrange("p (t h) -> p t h", t=8)[:, :, 0:8], ACT.Copy).then_inc(lft_ok, 1)
            act.activation(lf_tok[0:NS, 8, :], po[1][0:NS, 0:8], ACT.Copy).then_inc(lft_ok, 1)
            with act.Fori(0, 4) as i:
                for c, (off, n) in enumerate(CHUNKS):
                    act.wait_ge(q_z, 3 * i + c + 1)
                    if c < 2:
                        act.activation(q[0][0:64, off:off + n], pz[c][0:64, 0:n], ACT.Copy, scale=0.125)
                        act.activation(q[1][64:P, off:off + n], pz[c][64:P, 0:n], ACT.Copy, scale=0.125).then_inc(q_ok, 1)
                    else:
                        act.activation(qs_s[:, bass.ds(i, 1), :], pz[c][:, 0:n], ACT.Copy, scale=0.125).then_inc(q_ok, 1)
                act.wait_ge(stored, 64 * i)
                for c in range(3):
                    act.wait_ge(v_z, 3 * i + c + 1)
                    if c < 2:
                        act.activation(v[:, 4 * c:4 * c + 4, :], pz[c][:, :].rearrange("p (a n) -> p a n", a=4), ACT.Copy).then_inc(v_ok, 1)
                    else:
                        act.activation(vs_s[:, rows(i)], pz[c][0:NS, 0:P], ACT.Copy)
                        act.activation(v[:, 8, :], pz[c][:, 0:P], ACT.Copy).then_inc(v_ok, 1)
                for n_unit, (qi, hh) in enumerate(UNITS):
                    u, n = n_unit % 2, (qi + 1) * P
                    act.wait_ge(max_ok, 16 * i + n_unit + 1)
                    if n_unit >= 2:
                        act.wait_ge(t0_ok, 16 * i + n_unit - 1)
                        if UNITS[n_unit - 2][0] >= 4:
                            act.wait_ge(t1_ok, 8 * i + n_unit - 9)
                        act.wait_ge(ri_ok, 16 * i + n_unit - 1)
                    act.activation(p[:, u, 0:n], ps[u][:, 0:n], ACT.Exp, bias=nmax[:, u:u + 1], accum_out=rsum[:, u:u + 1]).then_inc(exp_ok, 1)
                    if qi >= 4:
                        act.wait_ge(t1_ps, 8 * i + n_unit - 7)
                        if n_unit >= 10:
                            act.wait_ge(pv, 16 * i + n_unit - 1)
                        act.activation(pT[:, u, 512:n], pt[1][:, 0:n - 512], ACT.Copy).then_inc(t1_ok, 1)

        def out_tile(dve, i, qi):
            dve.wait_ge(pv, 16 * i + 2 * qi + 2)
            dve.tensor_copy(keep["branch"][:, bass.ds(i + 8, 1), qi * P:(qi + 1) * P], po[qi % 2][:, 0:P].unsqueeze(1)).then_inc(o_ok, 1)

        @block.vector
        def _(dve):
            dve.wait_ge(consts, 80)
            dve.wait_ge(ln_ok, 1)
            dve.scalar_tensor_tensor(lf[:, :], a[:, :], 0.0, e1[:, :], ALU.min, ALU.subtract).then_inc(lf_ok, 1)
            dve.wait_ge(lf_ok, 1)
            dve.tensor_tensor_scan(cs[:, :], reset[:, :], lf[:, :], 0.0, ALU.mult, ALU.add).then_inc(c_ok, 1)
            dve.wait_ge(c_ok, 1)
            dve.tensor_scalar(bias_k[:, :], cs[:, :], row_coef[:, 0:1], row_coef[:, 1:2], ALU.mult, ALU.add).then_inc(bk_ok, 1)
            with dve.Fori(0, 4) as i:
                dve.wait_ge(pv, 16 * i)
                for hh in range(2):
                    dve.tensor_scalar(bias_q[hh][:, :], cs[:, 0:SEQ], heads[:, 1, bass.ds(2 * i + hh, 1)],
                                      heads[:, 0, bass.ds(2 * i + hh, 1)], ALU.mult, ALU.add).then_inc(bq_ok, 1)
                for c, (off, n) in enumerate(CHUNKS):
                    dve.wait_ge(k_z, 3 * i + c + 1)
                    if c == 2:
                        dve.tensor_copy(ks_s[:, bass.ds(i, 1), :], pz[3 + c][:, 0:n].unsqueeze(1))
                    dve.tensor_copy(kT[:, off:off + n], pz[3 + c][:, 0:n]).then_inc(k_ok, 1)
                dve.wait_ge(stored, 64 * i)
                for c in range(3):
                    dve.wait_ge(kt_ps, 3 * i + c + 1)
                    if c < 2:
                        dve.tensor_copy(k_tok[:, 4 * c:4 * c + 4, :], pz[3 + c][:, :].rearrange("p (a n) -> p a n", a=4)).then_inc(kt_ok, 1)
                    else:
                        dve.tensor_copy(k_tok[0:NS, 8, :], pz[5][0:NS, 0:P]).then_inc(kt_ok, 1)

                def soft(n_unit):
                    qi, hh = UNITS[n_unit]
                    u, n = n_unit % 2, (qi + 1) * P
                    dve.wait_ge(s_ps, 16 * i + n_unit + 1)
                    dve.tensor_reduce(nmax[:, u:u + 1], ps[u][:, 0:n], AX.X, ALU.max, negate=True).then_inc(max_ok, 1)

                soft(0)
                for n_unit, (qi, hh) in enumerate(UNITS):
                    u, n = n_unit % 2, (qi + 1) * P
                    dve.wait_ge(exp_ok, 16 * i + n_unit + 1)
                    dve.reciprocal(rinv[:, u:u + 1], rsum[:, u:u + 1]).then_inc(ri_ok, 1)
                    dve.wait_ge(ri_ok, 16 * i + n_unit + 1)
                    dve.tensor_scalar(diag[:, u, :], keep["ident"][:, :], rinv[:, u:u + 1], None, ALU.mult).then_inc(diag_ok, 1)
                    if n_unit + 1 < 16:
                        soft(n_unit + 1)
                    dve.wait_ge(t0_ps, 16 * i + n_unit + 1)
                    if n_unit >= 2:
                        dve.wait_ge(pv, 16 * i + n_unit - 1)
                    dve.tensor_copy(pT[:, u, 0:min(n, 512)], pt[0][:, 0:min(n, 512)]).then_inc(t0_ok, 1)
                    if n_unit >= 2 and n_unit % 2 == 1:
                        out_tile(dve, i, (n_unit - 3) // 2)
                out_tile(dve, i, 7)


def stage_fox_sample(nc, io, keep):
    with ExitStack() as ctx:
        m = Place(nc, ctx, keep["psum"])
        W = PAGES * PAGE
        pages = m.sb("g_pages", [P, DB * PAGES], I32)
        lane = m.sb("g_lane", [P, 2], I32)
        pages_f, idx_f, lane_f = m.sb("g_pages_f", [P, 64]), m.sb("g_idx_f", [P, 2, 64]), m.sb("g_lane_f", [P, 2])
        idx = m.sb("g_idx", [P, 2, 64], I32)
        idx_now = [m.sb(f"g_idx_now{u}", [P, 2, PAGES], I32) for u in range(2)]
        kc, vc = m.sb("g_kc", [P, PAGES, 512]), m.sb("g_vc", [P, PAGES, 512])
        lfc = m.sb("g_lfc", [64, W])
        c_all, bias_k, ones = m.sb("g_c_all", [64, W + NS]), m.sb("g_bias_k", [64, W + NS]), m.sb("g_ones", [64, W])
        row_coef, sel = m.sb("g_rows", [64, 2]), m.sb("g_sel", [64, 2, P])
        bias_q = m.sb("g_bias_q", [64, P])
        mask_new = m.sb("g_mask", [P, DB, NS])
        q_rows = m.sb("g_q_rows", [P, 4, 32])
        p, pT = m.sb("g_p", [P, W + NS]), m.sb("g_pT", [P, 9, P])
        nmax, rsum, rinv, diag = m.sb("g_nmax", [P, 1]), m.sb("g_rsum", [P, 1]), m.sb("g_rinv", [P, 1]), m.sb("g_diag", [P, P])
        ps = m.bank("g_s", 3)
        pt = m.bank("g_t", 3)
        po = m.bank("g_o", 2)
        k_loaded, v_loaded, lf_loaded = ([m.sem(f"g_{x}_loaded{n}") for n in range(PAGES)] for x in "kvl")
        (consts, pool_done, gate, idx_tmp, idx_ok, now_ok, c_ok, cn_ok, bk_ok, bq_ok, bq0, qr_ok, s_ps, max_ok, exp_ok, ri_ok, diag_ok,
         t_ps, t_ok, pv, o_ok) = (m.sem("g_" + s) for s in (
             "consts pool gate idx_tmp idx_ok now_ok c_ok cn_ok bk_ok bq_ok bq0 qr_ok s_ps max_ok exp_ok ri_ok diag_ok t_ps t_ok pv o_ok").split())
        block = m.block()
        c_new, q_new, k_new, v_new = keep["c_new"], keep["q_new"], keep["k_new"], keep["v_new"]

        @block.sync
        def _(sp):
            sp.dma_start(pages[:, :], io["page_table"].partition_broadcast(P)).then_inc(consts, 16)
            for dst, src in ((lane, "c_lane"), (row_coef, "c_rows"), (sel, "c_sel"), (mask_new, "c_new")):
                sp.dma_start(dst[:], io[src]).then_inc(consts, 16)

        @block.gpsimd
        def _(pool):
            pool.memset(ones[:, :], 1.0)
            pool.memset(q_rows[:, :, :], 0.0).then_inc(pool_done, 1)
            pool.wait_ge(idx_ok, 2)
            with pool.Fori(0, DB // 2) as half:
                for u in range(2):
                    i, now = half * 2 + u, idx_now[u]
                    pool.tensor_copy(now[:, :, :], idx[:, :, rows(i, PAGES)]).then_inc(now_ok, 1)
                    pool.wait_ge(now_ok, i + 1)
                    pool.wait_ge(c_ok, i)
                    pool.sem_inc(gate, 1)
                    for n in range(PAGES):
                        pool.indirect_dma_start(lfc[:, n * PAGE:(n + 1) * PAGE], None, io["cache_lfT"],
                                                bass.IndirectOffsetOnAxis(ap=now[0:64, 1, n:n + 1], axis=0)).then_inc(lf_loaded[n], 16)
                    pool.wait_ge(s_ps, i)
                    pool.sem_inc(gate, 1)
                    for n in range(PAGES):
                        pool.indirect_dma_start(kc[:, n, :], None, io["cache_kT"],
                                                bass.IndirectOffsetOnAxis(ap=now[:, 0, n:n + 1], axis=0)).then_inc(k_loaded[n], 16)
                    pool.wait_ge(pv, i)
                    pool.sem_inc(gate, 1)
                    for n in range(PAGES):
                        pool.indirect_dma_start(vc[:, n, :], None, io["cache_v"],
                                                bass.IndirectOffsetOnAxis(ap=now[:, 0, n:n + 1], axis=0)).then_inc(v_loaded[n], 16)

        @block.tensor
        def _(pe):
            pe.wait_ge(consts, 80)
            with pe.Fori(0, DB) as i:
                pe.wait_ge(bq_ok, i + 1)
                pe.wait_ge(qr_ok, i + 1)
                pe.wait_ge(exp_ok, i)
                for n in range(PAGES):
                    pe.wait_ge(k_loaded[n], 16 * i + 16)
                for part, (off, n) in enumerate(CHUNKS):
                    out = ps[:, off:off + n]
                    pe.matmul(out, bias_q[:, :], bias_k[:, off:off + n], start=True, stop=False, skip_group_check=True)
                    if part == 2:
                        pe.matmul(out, keep["ident"][:, :], mask_new[:, bass.ds(i, 1), :], start=False, stop=False, skip_group_check=True)
                    for pair in range(4):
                        keys = kc[:, 4 * part:4 * part + 4, pair * P:(pair + 1) * P] if part < 2 else k_new[:, pair, :]
                        last = pe.matmul(ps[pair * 32:pair * 32 + 32, off:off + n], q_rows[:, pair, :], keys, start=False,
                                         stop=True, skip_group_check=True)
                last.then_inc(s_ps, 1)
                pe.wait_ge(diag_ok, i + 1)
                pe.wait_ge(t_ok, 2 * i)
                for n in range(9):
                    w = P if n < 8 else NS
                    last = pe.matmul(pt[0:w, n * P:(n + 1) * P], p[:, n * P:n * P + w], diag[:, :], start=True, stop=True)
                last.then_inc(t_ps, 1)
                pe.wait_ge(t_ok, 2 * i + 2)
                pe.wait_ge(o_ok, 8 * i)
                for n in range(PAGES):
                    pe.wait_ge(v_loaded[n], 16 * i + 16)
                for pair in range(4):
                    for n in range(9):
                        w = P if n < 8 else NS
                        vals = vc[:, n, pair * P:(pair + 1) * P] if n < 8 else v_new[:, pair * P:(pair + 1) * P]
                        last = pe.matmul(po[:, pair * 32:pair * 32 + 16], vals, pT[0:w, n, pair * 32:pair * 32 + 16],
                                         start=(n == 0), stop=(n == 8))
                last.then_inc(pv, 1)

        @block.scalar
        def _(act):
            with act.Fori(0, DB) as i:
                act.wait_ge(max_ok, i + 1)
                act.wait_ge(t_ps, i)
                act.wait_ge(ri_ok, i)
                act.activation(p[:, :], ps[:, 0:W + NS], ACT.Exp, bias=nmax[:, 0:1], accum_out=rsum[:, 0:1]).then_inc(exp_ok, 1)
                act.wait_ge(t_ps, i + 1)
                act.wait_ge(pv, i)
                act.activation(pT[:, 0:8, :], pt[:, 0:1024].rearrange("p (n r) -> p n r", n=8), ACT.Copy).then_inc(t_ok, 1)
                act.activation(pT[0:NS, 8, :], pt[0:NS, 1024:1152], ACT.Copy).then_inc(t_ok, 1)

        @block.vector
        def _(dve):
            lk = Link(dve, idx_tmp)
            dve.wait_ge(consts, 80)
            lk(dve.tensor_copy(pages_f[:, :], pages[:, :]))
            lk(dve.tensor_copy(lane_f[:, :], lane[:, :]))
            for s, size in enumerate((P, 8)):
                lk(dve.tensor_scalar(idx_f[:, s, :], pages_f[:, :], float(size), lane_f[:, s:s + 1], ALU.mult, ALU.add))
                dve.tensor_copy(idx[:, s, :], idx_f[:, s, :]).then_inc(idx_ok, 1)
            dve.wait_ge(pool_done, 1)
            with dve.Fori(0, DB) as i:
                for n in range(PAGES):
                    dve.wait_ge(lf_loaded[n], 16 * i + 16)
                dve.wait_ge(s_ps, i)
                dve.tensor_tensor_scan(c_all[:, 0:W], ones[:, :], lfc[:, :], 0.0, ALU.mult, ALU.add).then_inc(c_ok, 1)
                dve.wait_ge(c_ok, i + 1)
                dve.tensor_scalar(c_all[:, W:W + NS], c_new[:, SEQ:T], c_all[:, W - 1:W], None, ALU.add).then_inc(cn_ok, 1)
                dve.wait_ge(cn_ok, i + 1)
                dve.tensor_scalar(bias_k[:, :], c_all[:, :], row_coef[:, 0:1], row_coef[:, 1:2], ALU.mult, ALU.add).then_inc(bk_ok, 1)
                dve.tensor_tensor(bias_q[:, :].rearrange("p (g t) -> p g t", t=DT),
                                  c_all[:, bass.ds(i * DT + W, DT)].unsqueeze(1).broadcast_to([64, 16, DT]),
                                  sel[:, 1, :].rearrange("p (g t) -> p g t", t=DT), ALU.mult).then_inc(bq0, 1)
                dve.wait_ge(bq0, i + 1)
                dve.tensor_tensor(bias_q[:, :], bias_q[:, :], sel[:, 0, :], ALU.add).then_inc(bq_ok, 1)
                dve.tensor_copy(q_rows[0:64, :, 0:DT], q_new[0:64, :, rows(i, DT)])
                dve.tensor_copy(q_rows[64:P, :, DT:2 * DT], q_new[64:P, :, rows(i, DT)]).then_inc(qr_ok, 1)
                dve.wait_ge(s_ps, i + 1)
                dve.tensor_reduce(nmax[:, :], ps[:, 0:W + NS], AX.X, ALU.max, negate=True).then_inc(max_ok, 1)
                dve.wait_ge(exp_ok, i + 1)
                dve.reciprocal(rinv[:, :], rsum[:, :]).then_inc(ri_ok, 1)
                dve.wait_ge(ri_ok, i + 1)
                dve.tensor_scalar(diag[:, :], keep["ident"][:, :], rinv[:, 0:1], None, ALU.mult).then_inc(diag_ok, 1)
                dve.wait_ge(pv, i + 1)
                for pair in range(4):
                    for hh in range(2):
                        dve.tensor_copy(keep["branch"][hh * 64:hh * 64 + 64, 8 + pair, bass.ds(i * DT + SEQ, DT)],
                                        po[hh * 64:hh * 64 + 64, pair * 32 + hh * DT:pair * 32 + hh * DT + DT]).then_inc(o_ok, 1)


def stage_merge(nc, io, keep):
    with ExitStack() as ctx:
        m = Place(nc, ctx, keep["psum"])
        w = [m.sb(f"m_w{u}", [P, 12 * P]) for u in range(3)]
        sig = m.sb("m_sig", [P, T])
        part = m.sb("m_part", [P, T])
        acc = m.sb("m_acc", [P, T])
        merged = m.sb("m_merged", [P, KD, T])
        w_out = m.sb("m_w_out", [P, KD, D])
        x_in = h = m.sb("m_x", [P, 2, D])
        proj = [m.bank(f"m_p{c}") for c in range(3)]
        gate = [m.bank(f"m_g{c}") for c in range(3)]
        ph = [proj[0], proj[1], gate[0], gate[1]]
        w_loaded = [m.sem(f"m_w{u}_loaded") for u in range(3)]
        p_z2 = [m.sem(f"m_p_z2_{n}") for n in range(3)]
        x_loaded = [m.sem(f"m_x_loaded{u}") for u in range(2)]
        stored = [m.sem(f"m_stored{u}") for u in range(2)]
        (wo_loaded, p_z, g_z, sg_ok, part_ok, acc_ok, z_ok, ph_ok, h_ok) = (
            m.sem("m_" + s) for s in "wo_loaded p_z g_z sg_ok part_ok acc_ok z_ok ph_ok h_ok".split())
        block = m.block()

        @block.sync
        def _(sp):
            with sp.Fori(0, KD) as i:
                for n in range(3):
                    sp.wait_ge(p_z2[n], i)
                    sp.dma_start(w[n][:, :], io["w_merge"][rows(3 * i + n), :]).then_inc(w_loaded[n], 16)
            sp.dma_start(w_out[:, :, :], io["w_out"]).then_inc(wo_loaded, 16)
            for t in range(NT):
                u = t % 2
                if t >= 2:
                    sp.wait_ge(stored[u], 16 * (t // 2))
                sp.dma_start(x_in[:, u, :], io["x_all"][t * P:(t + 1) * P, :]).then_inc(x_loaded[u], 16)

        @block.gpsimd
        def _(pool):
            for t in range(NT):
                pool.wait_ge(h_ok, t + 1)
                pool.dma_start(io["h_scratch"][t * P:(t + 1) * P, :], h[:, t % 2, :]).then_inc(stored[t % 2], 16)
            for u in range(2):
                pool.wait_ge(stored[u], 16 * ((NT + 1 - u) // 2))

        @block.tensor
        def _(pe):
            with pe.Fori(0, KD) as i:
                for n in range(3):
                    pe.wait_ge(w_loaded[n], 16 * i + 16)
                    for c, (off, width) in enumerate(CHUNKS):
                        pe.wait_ge(sg_ok, 9 * i + 3 * n)
                        for kk in range(KD):
                            last = pe.matmul(gate[c][:, 0:width], w[n][:, (4 + kk) * P:(5 + kk) * P],
                                             keep["xT"][:, kk, off:off + width], start=(kk == 0), stop=(kk == KD - 1))
                        last.then_inc(g_z, 1)
                    for c, (off, width) in enumerate(CHUNKS):
                        pe.wait_ge(part_ok, 9 * i + 3 * n)
                        for kk in range(4):
                            last = pe.matmul(proj[c][:, 0:width], w[n][:, kk * P:(kk + 1) * P],
                                             keep["branch"][:, 4 * n + kk, off:off + width], start=(kk == 0), stop=(kk == 3))
                        last.then_inc(p_z if c < 2 else p_z2[n], 1)
            pe.wait_ge(wo_loaded, 16)
            pe.wait_ge(acc_ok, 2 * KD)
            for t in range(NT):
                n = P if t < 8 else NS
                if t >= 2:
                    pe.wait_ge(h_ok, t - 1)
                for hf in range(2):
                    for kk in range(KD):
                        last = pe.matmul(ph[2 * (t % 2) + hf][0:n, :], merged[:, kk, t * P:t * P + n], w_out[:, kk, hf * 512:(hf + 1) * 512],
                                         start=(kk == 0), stop=(kk == KD - 1))
                last.then_inc(ph_ok, 1)

        @block.scalar
        def _(act):
            with act.Fori(0, KD) as i:
                for n in range(3):
                    for c, (off, width) in enumerate(CHUNKS):
                        act.wait_ge(g_z, 9 * i + 3 * n + c + 1)
                        act.wait_ge(part_ok, 9 * i + 3 * n)
                        act.activation(sig[:, off:off + width], gate[c][:, 0:width], ACT.Sigmoid).then_inc(sg_ok, 1)

        @block.vector
        def _(dve):
            with dve.Fori(0, KD) as i:
                for n in range(3):
                    for c, (off, width) in enumerate(CHUNKS):
                        dve.wait_ge(sg_ok, 9 * i + 3 * n + c + 1)
                        if c < 2:
                            dve.wait_ge(p_z, 6 * i + 2 * n + c + 1)
                        else:
                            dve.wait_ge(p_z2[n], i + 1)
                        dve.wait_ge(acc_ok, 2 * i + max(n - 1, 0))
                        to = (acc if n == 0 else part)[:, off:off + width]
                        dve.tensor_tensor(to, proj[c][:, 0:width], sig[:, off:off + width], ALU.mult).then_inc(part_ok, 1)
                    dve.wait_ge(part_ok, 9 * i + 3 * n + 3)
                    if n > 0:
                        to = acc[:, :].unsqueeze(1) if n == 1 else merged[:, bass.ds(i, 1), :]
                        dve.tensor_tensor(to, acc[:, :].unsqueeze(1), part[:, :].unsqueeze(1), ALU.add).then_inc(acc_ok, 1)
            for t in range(NT):
                n, u = (P if t < 8 else NS), t % 2
                dve.wait_ge(ph_ok, t + 1)
                dve.wait_ge(x_loaded[u], 16 * (t // 2) + 16)
                for hf in range(2):
                    last = dve.tensor_tensor(h[0:n, u, hf * 512:(hf + 1) * 512], ph[2 * u + hf][0:n, :],
                                             x_in[0:n, u, hf * 512:(hf + 1) * 512], ALU.add)
                last.then_inc(h_ok, 1)


GROUPS, SLOTS = 16, 8
HEADS, TOPK = 8, 16


def stage_peer(nc, io, keep):
    with ExitStack() as ctx:
        m = Place(nc, ctx, keep["psum"])
        wq, keysT = m.sb("p_wq", [P, KD, 2048]), m.sb("p_keysT", [P, 16, P])
        u_rows, v_rows = m.sb("p_u_rows", [P, SLOTS, D]), m.sb("p_v_rows", [P, SLOTS, D])
        h, xn = m.sb("p_h", [P, 2, D]), m.sb("p_xn", [P, 2, D])
        xnT, qT, s = m.sb("p_xnT", [P, KD, P]), m.sb("p_qT", [P, 16, P]), m.sb("p_s", [P, 16, P])
        cand = m.sb("p_cand", [P, HEADS, TOPK, TOPK])
        gain2, gain_f = m.sb("p_gain2", [P, D]), m.sb("p_gain_f", [P, D])
        diag = m.sb("p_diag", [P, SLOTS, P])
        sv, si = m.sb("p_sv", [P, 16, TOPK]), m.sb("p_si", [P, 16, TOPK], U32)
        si_f = m.sb("p_si_f", [P, 16, TOPK])
        top, pos, pos2 = m.sb("p_top", [P, HEADS, TOPK]), m.sb("p_pos", [P, HEADS, TOPK], U32), m.sb("p_pos2", [P, HEADS, TOPK], U32)
        pos_f, e_f = m.sb("p_pos_f", [P, HEADS, TOPK]), m.sb("p_e_f", [P, 2, HEADS, TOPK])
        w, idx = m.sb("p_w", [P, 2, HEADS * TOPK]), m.sb("p_idx", [P, 2, HEADS * TOPK], U32)
        wsum, iota = m.sb("p_wsum", [P, HEADS, 1]), m.sb("p_iota", [P, TOPK])
        hid, gl, act_w = m.sb("p_hid", [P, 2, SLOTS]), m.sb("p_gl", [P, 2, SLOTS]), m.sb("p_act_w", [P, 2, SLOTS])
        stat, stat_f = m.sb("p_stat", [P, 2]), m.sb("p_stat_f", [P, 2])
        zero = m.sb("p_zero", [P, P])
        acc = [m.bank(f"p_acc{u}", 2) for u in range(2)]
        pb = [m.bank(f"p_b{u}") for u in range(4)]
        u_loaded, v_loaded = ([m.sem(f"p_{x}_loaded{n}") for n in range(SLOTS)] for x in "uv")
        h_loaded = [m.sem(f"p_h_loaded{u}") for u in range(2)]
        stored = [m.sem(f"p_stored{u}") for u in range(2)]
        (consts, gate, zero_ok, u_free, v_free, gl_ok, act_ok, diag_ok, acc_ps, y_ok, ss_ok, sd_ok, rs_ok, xn_ok, xt_ps, xt_ok,
         q_ps, q_ok, s_ps, s_ok, link, idx_ok, wd_ok, we_ok, w_ok, fss, fsd, frs) = (
            m.sem("p_" + x) for x in (
                "consts gate zero_ok u_free v_free gl_ok act_ok diag_ok acc_ps y_ok ss_ok sd_ok rs_ok xn_ok xt_ps xt_ok q_ps q_ok "
                "s_ps s_ok link idx_ok wd_ok we_ok w_ok fss fsd frs").split())
        block = m.block()
        LINKS = 1 + 16 * 5 + 1 + 8 * 5 + 12
        EXPERTS = HEADS * TOPK

        def choose_act(act, t, u, step):
            if step == 0:
                act.wait_ge(h_loaded[u], 16 * (t // 2) + 16 if isinstance(t, int) else t * 8 + 16 - 8 * u)
                act.wait_ge(xn_ok, t)
                act.activation(cand[:, 0:4, :, :].rearrange("p a b c -> p (a b c)"), h[:, u, :], ACT.Square,
                               accum_out=stat[:, 0:1]).then_inc(ss_ok, 1)
                act.wait_ge(ss_ok, t + 1)
                act.activation(stat[:, 1:2], stat[:, 0:1], ACT.Sqrt, scale=1.0 / D, bias=keep["eps"][:, 0:1]).then_inc(sd_ok, 1)
            if step == 1:
                for b in range(2):
                    act.wait_ge(xt_ps, 2 * t + b + 1)
                    act.activation(xnT[:, 4 * b:4 * b + 4, :], pb[b].rearrange("p (k n) -> p k n", k=4), ACT.Copy).then_inc(xt_ok, 1)
            if step in (2, 3):
                for b in range(2 * step - 4, 2 * step - 2):
                    act.wait_ge(q_ps, 4 * t + b + 1)
                    act.activation(qT[:, 4 * b:4 * b + 4, :], pb[(b + 2) % 4].rearrange("p (k n) -> p k n", k=4), ACT.Copy).then_inc(q_ok, 1)
            if step == 4:
                act.wait_ge(idx_ok, t)
                for b in range(4):
                    act.wait_ge(s_ps, 4 * t + b + 1)
                    act.activation(s[:, 4 * b:4 * b + 4, :], pb[b].rearrange("p (k n) -> p k n", k=4), ACT.Copy).then_inc(s_ok, 1)
            if step == 15:
                act.wait_ge(wd_ok, t + 1)
                act.activation(w[:, u, :], w[:, u, :], ACT.Exp).then_inc(we_ok, 1)

        def choose_pe(pe, t, u, step):
            if step == 1:
                pe.wait_ge(xn_ok, t + 1)
                pe.wait_ge(s_ok, 4 * t)
                for b in range(2):
                    for k in range(4 * b, 4 * b + 4):
                        last = pe.transpose(pb[b][:, k % 4 * P:k % 4 * P + P], xn[:, u, k * P:(k + 1) * P], keep["ident"][:, :])
                    last.then_inc(xt_ps, 1)
            if step in (2, 3):
                pe.wait_ge(xt_ok, 2 * t + 2)
                for b in range(2 * step - 4, 2 * step - 2):
                    for c in range(4 * b, 4 * b + 4):
                        for k in range(KD):
                            last = pe.matmul(pb[(b + 2) % 4][:, c % 4 * P:c % 4 * P + P], wq[:, k, c * P:(c + 1) * P], xnT[:, k, :],
                                             start=(k == 0), stop=(k == KD - 1))
                    last.then_inc(q_ps, 1)
            if step == 4:
                pe.wait_ge(q_ok, 4 * t + 4)
                for b in range(4):
                    for c in range(4 * b, 4 * b + 4):
                        last = pe.matmul(pb[b][:, c % 4 * P:c % 4 * P + P], qT[:, c, :], keysT[:, c, :], start=True, stop=True)
                    last.then_inc(s_ps, 1)

        class Chooser:

            def __init__(self, dve, t, u):
                self.dve, self.t, self.u = dve, t, u
                self.lk = Link(dve, link)

            def top16(self, values, val, ind):
                dve, lk = self.dve, self.lk
                lk(dve.max(val[:, 0:8], values))
                lk(dve.max_index(ind[:, 0:8], val[:, 0:8], values))
                lk(dve.match_replace(values, val[:, 0:8], values, -3.0e38))
                lk(dve.max(val[:, 8:16], values))
                lk(dve.max_index(ind[:, 8:16], val[:, 8:16], values))

            def step(self, n):
                dve, t, u, lk = self.dve, self.t, self.u, self.lk
                if n == 1:
                    dve.sem_clear(link)
                    dve.wait_ge(sd_ok, t + 1)
                    dve.reciprocal(stat[:, 1:2], stat[:, 1:2]).then_inc(rs_ok, 1)
                    dve.wait_ge(rs_ok, t + 1)
                    dve.scalar_tensor_tensor(xn[:, u, :], h[:, u, :], stat[:, 1:2], gain2[:, :], ALU.mult, ALU.mult).then_inc(xn_ok, 1)
                first = (0, 3, 6, 9, 12, 14, 16)
                if 5 <= n <= 10:
                    if n == 5:
                        dve.wait_ge(s_ok, 4 * t + 4)
                        lk(dve.memset(sv[:, :, :], 0.0))
                    for c in range(first[n - 5], first[n - 4]):
                        self.top16(s[:, c, :], sv[:, c, :], si[:, c, :])
                if n == 10:
                    pairs = sv[:, :, :].rearrange("p (h s) k -> p h s k", s=2)
                    shape = [P, HEADS, TOPK, TOPK]
                    lk(dve.tensor_tensor(cand[:, :, :, :], pairs[:, :, 0, :].unsqueeze(3).broadcast_to(shape),
                                         pairs[:, :, 1, :].unsqueeze(2).broadcast_to(shape), ALU.add))
                if 11 <= n <= 13:
                    for hd in range(3 * (n - 11), min(3 * (n - 11) + 3, HEADS)):
                        self.top16(cand[:, hd, :, :].rearrange("p a b -> p (a b)"), top[:, hd, :], pos[:, hd, :])
                if n in (14, 15):
                    half = n - 14
                    shape = [P, HEADS, TOPK, TOPK]
                    if half == 0:
                        lk(dve.tensor_copy(si_f[:, :, :], si[:, :, :]))
                        lk(dve.tensor_scalar(pos2[:, :, :], pos[:, :, :], 4, None, ALU.logical_shift_right))
                    else:
                        lk(dve.tensor_scalar(pos2[:, :, :], pos[:, :, :], 15, None, ALU.bitwise_and))
                    lk(dve.tensor_copy(pos_f[:, :, :], pos2[:, :, :]))
                    lk(dve.tensor_tensor(cand[:, :, :, :], pos_f[:, :, :].unsqueeze(3).broadcast_to(shape),
                                         iota[:, :].unsqueeze(1).unsqueeze(1).broadcast_to(shape), ALU.is_equal))
                    of_half = si_f[:, :, :].rearrange("p (h s) k -> p h s k", s=2)[:, :, half, :]
                    lk(dve.tensor_tensor(cand[:, :, :, :], cand[:, :, :, :], of_half.unsqueeze(2).broadcast_to(shape), ALU.mult))
                    lk(dve.tensor_reduce(e_f[:, half, :, :], cand[:, :, :, :], AX.X, ALU.add))
                if n == 15:
                    lk(dve.scalar_tensor_tensor(e_f[:, 0, :, :], e_f[:, 0, :, :], float(P), e_f[:, 1, :, :], ALU.mult, ALU.add))
                    dve.tensor_copy(idx[:, u, :].rearrange("p (h k) -> p h k", h=HEADS), e_f[:, 0, :, :]).then_inc(idx_ok, 1)
                    wv = w[:, u, :].rearrange("p (h k) -> p h k", h=HEADS)
                    dve.tensor_tensor(wv, top[:, :, :], top[:, :, 0:1].broadcast_to([P, HEADS, TOPK]), ALU.subtract).then_inc(wd_ok, 1)
                    dve.wait_ge(we_ok, t + 1)
                    dve.tensor_reduce(wsum[:, :, :], wv, AX.X, ALU.add).then_inc(w_ok, 1)
                    dve.wait_ge(w_ok, 3 * t + 1)
                    dve.reciprocal(wsum[:, :, :], wsum[:, :, :]).then_inc(w_ok, 1)
                    dve.wait_ge(w_ok, 3 * t + 2)
                    dve.tensor_tensor(wv, wv, wsum[:, :, :].broadcast_to([P, HEADS, TOPK]), ALU.mult).then_inc(w_ok, 1)
                    assert self.lk.n == LINKS, self.lk.n

        def main_pool(pool, t, u, n):
            pool.wait_ge(idx_ok, t + 1)
            for g in range(GROUPS):
                for free, loaded, to, table in ((u_free, u_loaded, u_rows, "peer_u"), (v_free, v_loaded, v_rows, "peer_v")):
                    for k in range(SLOTS):
                        c = g * SLOTS + k
                        pool.wait_ge(free, EXPERTS * t + c + 1)
                        pool.sem_inc(gate, 1)
                        pool.indirect_dma_start(to[0:n, k, :], None, io[table],
                                                bass.IndirectOffsetOnAxis(ap=idx[0:n, u, c:c + 1], axis=0)).then_inc(loaded[k], 16)

        def main_pe(pe, t, u, n, choosing):
            pe.wait_ge(y_ok, t)
            for hf in range(2):
                pe.matmul(acc[u][0:n, hf * 512:(hf + 1) * 512], zero[0:n, 0:n], h[0:n, u, hf * 512:(hf + 1) * 512], start=True, stop=False,
                          skip_group_check=True)
            for g in range(GROUPS):
                for k in range(SLOTS):
                    c = g * SLOTS + k
                    pe.wait_ge(diag_ok, EXPERTS * t + c + 1)
                    pe.wait_ge(v_loaded[k], (t * GROUPS + g) * 16 + 16)
                    for hf in range(2):
                        last = pe.matmul(acc[u][0:n, hf * 512:(hf + 1) * 512], diag[0:n, k, 0:n], v_rows[0:n, k, hf * 512:(hf + 1) * 512],
                                         start=False, stop=False, skip_group_check=True)
                    last.then_inc(v_free, 1)
                if choosing:
                    choose_pe(pe, t + 1, 1 - u, g)
            for hf in range(2):
                last = pe.matmul(acc[u][0:n, hf * 512:(hf + 1) * 512], keep["ident"][0:n, 0:n], h[0:n, u, hf * 512:(hf + 1) * 512],
                                 start=False, stop=True, skip_group_check=True)
            last.then_inc(acc_ps, 1)

        def main_act(act, t, u, n, choosing):
            for g in range(GROUPS):
                gp = g % 2
                act.wait_ge(u_free, EXPERTS * t + (g + 2) * SLOTS)
                act.activation(gl[0:n, gp, :], hid[0:n, gp, :], ACT.Gelu).then_inc(gl_ok, 1)
                act.wait_ge(act_ok, GROUPS * t + g + 1)
                for k in range(SLOTS):
                    act.wait_ge(v_free, EXPERTS * t + g * SLOTS + k + 1)
                    act.activation(diag[0:n, k, 0:n], keep["ident"][0:n, 0:n], ACT.Copy, scale=act_w[0:n, gp, k:k + 1]).then_inc(diag_ok, 1)
                if choosing:
                    choose_act(act, t + 1, 1 - u, g)
            act.wait_ge(acc_ps, t + 1)
            act.activation(h[0:n, u, :], acc[u][0:n, :], ACT.Square, accum_out=stat_f[0:n, 0:1]).then_inc(fss, 1)
            act.wait_ge(fss, t + 1)
            act.activation(stat_f[0:n, 1:2], stat_f[0:n, 0:1], ACT.Sqrt, scale=1.0 / D, bias=keep["eps"][0:n, 0:1]).then_inc(fsd, 1)

        def main_dve(dve, t, u, n, choosing):
            chooser = Chooser(dve, t + 1, 1 - u) if choosing else None
            for g in range(GROUPS):
                gp = g % 2
                for k in range(SLOTS):
                    dve.wait_ge(u_loaded[k], (t * GROUPS + g) * 16 + 16)
                    last = dve.tensor_tensor_reduce(out=u_rows[0:n, k, :], in0=u_rows[0:n, k, :], in1=xn[0:n, u, :], scale=1.0, scalar=0.0,
                                                    op0=ALU.mult, op1=ALU.add, accum_out=hid[0:n, gp, k:k + 1])
                    last.then_inc(u_free, 1)
                dve.wait_ge(gl_ok, GROUPS * t + g + 1)
                dve.tensor_tensor(act_w[0:n, gp, :], gl[0:n, gp, :], w[0:n, u, g * SLOTS:(g + 1) * SLOTS], ALU.mult).then_inc(act_ok, 1)
                if chooser:
                    chooser.step(g)
            dve.wait_ge(fsd, t + 1)
            dve.reciprocal(stat_f[0:n, 1:2], stat_f[0:n, 1:2]).then_inc(frs, 1)
            dve.wait_ge(frs, t + 1)
            dve.scalar_tensor_tensor(h[0:n, u, :], acc[u][0:n, :], stat_f[0:n, 1:2], gain_f[0:n, :], ALU.mult, ALU.mult).then_inc(y_ok, 1)

        def tiles(eng, main):
            with eng.Fori(0, 4) as i:
                for u in range(2):
                    main(eng, 2 * i + u, u, P, True)
            main(eng, 8, 0, NS, False)

        @block.sync
        def _(sp):
            for dst, src in ((gain2, "norm2_g"), (gain_f, "final_g")):
                sp.dma_start(dst[:, :], io[src].partition_broadcast(P)).then_inc(consts, 16)
            sp.dma_start(h[:, 0, :], io["h_scratch"][0:P, :]).then_inc(h_loaded[0], 16)
            for dst, src in ((wq, "peer_wq"), (keysT, "peer_keysT"), (iota, "c_iota16")):
                sp.dma_start(dst[:], io[src]).then_inc(consts, 16)

            def tile(sp, t, u, n, more):
                if more:
                    if u == 0:
                        sp.wait_ge(stored[1], 8 * t)
                    else:
                        sp.wait_ge(stored[0], 8 * t + 8)
                    sp.dma_start(h[:, 1 - u, :], io["h_scratch"][rows(t + 1), :]).then_inc(h_loaded[1 - u], 16)
                sp.wait_ge(y_ok, t + 1)
                if more:
                    sp.dma_start(io["y_prompt"][0, rows(t), :], h[:, u, :]).then_inc(stored[u], 16)
                else:
                    sp.dma_start(io["y_sample"].rearrange("b t d -> (b t) d"), h[0:n, u, :]).then_inc(stored[u], 16)

            tiles(sp, tile)
            sp.wait_ge(stored[0], 16 * 5)
            sp.wait_ge(stored[1], 16 * 4)

        @block.gpsimd
        def _(pool):
            pool.memset(zero[:, :], 0.0).then_inc(zero_ok, 1)
            tiles(pool, lambda eng, t, u, n, more: main_pool(eng, t, u, n))

        @block.tensor
        def _(pe):
            pe.sem_inc(v_free, SLOTS)
            pe.wait_ge(consts, 16 * 5)
            pe.wait_ge(zero_ok, 1)
            for step in range(GROUPS):
                choose_pe(pe, 0, 0, step)
            tiles(pe, main_pe)

        @block.scalar
        def _(act):
            for step in range(GROUPS):
                choose_act(act, 0, 0, step)
            tiles(act, main_act)

        @block.vector
        def _(dve):
            dve.sem_inc(u_free, SLOTS)
            dve.wait_ge(consts, 16 * 5)
            first = Chooser(dve, 0, 0)
            for step in range(GROUPS):
                first.step(step)
            tiles(dve, main_dve)


OUTPUTS = (
    ("y_prompt", (1, SEQ, D)), ("y_sample", (DB, DT, D)),
    ("new_k_prompt", (1, 1, SEQ, 8, 64)), ("new_v_prompt", (1, 1, SEQ, 8, 64)), ("new_logf_prompt", (1, 1, SEQ, 8)),
    ("new_conv_prompt", (1, 1, HALO, 512)), ("new_hgrn_prompt", (1, 1, 4, P, P)),
    ("new_k_sample", (1, DB, DT, 8, 64)), ("new_v_sample", (1, DB, DT, 8, 64)), ("new_logf_sample", (1, DB, DT, 8)),
    ("new_conv_sample", (1, DB, HALO, 512)), ("new_hgrn_sample", (1, DB, 4, P, P)),
)


def build(nc, io, stages):
    with ExitStack() as ctx:
        m = Place(nc, ctx)
        io["h_scratch"] = nc.dram_tensor("h_scratch", (TP, D), F32, kind="Internal").ap()
        keep = {"ident": m.sb("ident", [P, P]), "eps": m.sb("eps", [P, 1]),
                "psum": ctx.enter_context(nc.psum_tensor("psum", [P, 8 * 512], F32))}
        with ExitStack() as trunk_ctx:
            t = Place(nc, trunk_ctx)
            keep["xT"] = t.sb("xT", [P, KD, TP])
            keep["branch"] = t.sb("branch", [P, 12, T])
            keep["c_new"] = t.sb("c_new", [64, T])
            keep["q_new"], keep["k_new"] = t.sb("q_new", [P, 4, NS]), t.sb("k_new", [P, 4, NS])
            keep["v_new"] = t.sb("v_new", [NS, 512])
            for stage in stages[0]:
                stage(nc, io, keep)
        for stage in stages[1]:
            stage(nc, io, keep)


def laid_out(inputs):
    a = {k: np.asarray(v) for k, v in inputs.items()}
    w = a["w_in"][0].reshape(KD, P, -1).transpose(1, 0, 2)

    def tiles(starts, width=P):
        return np.concatenate([w[:, :, s:s + width].reshape(P, KD * width) for s in starts])

    out = {}
    out["x_all"] = np.concatenate([a["x_prompt"][0], a["x_sample"].reshape(NS, D), np.zeros((TP - T, D), np.float32)])
    out["w_conv"] = tiles([s + P * i for i in range(4) for s in (512, 0)])
    out["w_hgrn"] = tiles([s + P * h for h in range(4) for s in (1024, 1536, 2560, 2048)])
    out["w_fox"] = tiles([s + P * j for j in range(4) for s in (3072, 3584, 4096)])
    af = w[:, :, 4608:4616]
    zeros = np.zeros((P, KD, 24), np.float32)
    out["w_af"] = np.concatenate([af, zeros, af, zeros], 2).reshape(P, KD * 64)
    wb = a["w_branch"][0].reshape(3, 4, P, D).transpose(0, 2, 1, 3)
    out["w_merge"] = np.concatenate([
        np.concatenate([wb[n][:, :, P * i:P * (i + 1)], w[:, :, 4616 + D * n + P * i:4616 + D * n + P * (i + 1)]], 1)
        .reshape(P, 12 * P) for i in range(KD) for n in range(3)])
    out["w_out"] = a["w_out"][0].reshape(KD, P, D).transpose(1, 0, 2)
    out["norm1_g"], out["norm2_g"], out["final_g"] = a["norm1_g"][0], a["norm2_g"][0], a["final_g"]
    out["conv_taps"] = np.concatenate([a["conv_dw"][0], a["conv_db"]]).reshape(CONV_K + 1, 4, P).transpose(2, 1, 0)
    out["conv_ln"] = np.stack([a["conv_ln_g"][0], a["conv_ln_b"][0]]).reshape(2, 4, P).transpose(2, 0, 1)
    out["state_conv"] = a["state_conv"]
    out["state_convT"] = a["state_conv"][0].transpose(2, 0, 1)
    out["state_hgrn"] = a["state_hgrn"][0].transpose(1, 2, 0, 3).reshape(4 * P, DB, P)
    out["hg_lb"] = a["hg_lb_logits"][0].reshape(4, P).T
    out["hg_norm"] = a["hg_norm_g"][0].reshape(P, 1)
    fb = a["att_fb"][0]
    z24 = np.zeros(24, np.float32)
    out["att_fb"] = np.concatenate([fb, z24, fb, z24]).reshape(64, 1)
    out["cache_kT"] = a["cache_k"][0].reshape(PHYS, PAGE, 4, P).transpose(0, 3, 2, 1).reshape(PHYS * P, 4 * PAGE)
    out["cache_v"] = a["cache_v"][0].reshape(PHYS * PAGE, 512)
    out["cache_lfT"] = a["cache_logf"][0].transpose(0, 2, 1).reshape(PHYS * 8, PAGE)
    out["page_table"] = a["page_table"].reshape(DB * PAGES)
    out["peer_wq"] = a["peer_wq"][0].reshape(KD, P, 2048).transpose(1, 0, 2)
    out["peer_keysT"] = a["peer_keys"][0].reshape(16, P, P).transpose(2, 0, 1)
    out["peer_u"], out["peer_v"] = a["peer_u"][0], a["peer_v"][0]
    s, t = np.arange(P)[:, None], np.arange(P)[None, :]
    out["c_ident"] = np.eye(P, dtype=np.float32)
    out["c_eps"] = np.full((P, 1), EPS, np.float32)
    masks = [(s // (2 * h) == t // (2 * h)) & (s % (2 * h) < h) & (t % (2 * h) >= h) for h in LEVELS] + [s == t]
    out["c_levels"] = np.stack(masks, 1).astype(np.float32)
    reset = np.ones(T, np.float32)
    reset[0:SEQ:64] = 0
    reset[SEQ:T:DT] = 0
    out["c_reset"] = reset
    out["c_reset_c"] = np.ones(T, np.float32)
    out["c_reset_c"][0] = 0
    out["c_reset_c"][SEQ:T:DT] = 0
    out["c_batch"] = (np.arange(NS)[:, None] // DT == np.arange(DB)[None, :]).astype(np.float32)
    out["c_causal"] = np.where(t <= s, 0, NEG).astype(np.float32)
    lane = np.arange(64)
    out["c_rows"] = np.stack([np.where(lane < 8, -1, 0), np.where((lane >= 32) & (lane < 40), 1, 0)], 1).astype(np.float32)
    out["c_heads"] = np.stack([lane[:, None] == np.arange(8)[None], lane[:, None] - 32 == np.arange(8)[None]], 1).astype(np.float32)
    col = np.arange(P)
    head, used, tok = 2 * (col // 32) + (col % 32) // 8, col % 32 < 16, col % 8
    sel = (lane[:, None] == head[None]) & used[None]
    selq = (lane[:, None] - 32 == head[None]) & used[None]
    out["c_sel"] = np.stack([sel, selq], 1).astype(np.float32)
    key = np.arange(NS)
    allowed = (key[None, None] // DT == np.arange(DB)[None, :, None]) & (key[None, None] % DT <= tok[:, None, None])
    out["c_new"] = np.where(allowed, 0, NEG).astype(np.float32)
    out["c_lane"] = np.stack([np.arange(P), np.arange(P) % 8], 1).astype(np.int32)
    out["c_iota16"] = np.broadcast_to(np.arange(16, dtype=np.float32), (P, 16))
    return {k: np.ascontiguousarray(v) for k, v in out.items()}


STAGES = ((stage_norm, stage_conv, stage_hgrn, stage_fox, stage_fox_sample, stage_merge), (stage_peer,))


def kernel(**inputs):
    import concourse.bacc as bacc
    from concourse.bass_utils import run_bass_kernel_spmd

    nc = bacc.Bacc("TRN2", target_bir_lowering=False, num_devices=1)
    arrays = laid_out(inputs)
    io = {k: nc.dram_tensor("in_" + k, v.shape, mybir.dt.from_np(v.dtype), kind="ExternalInput").ap() for k, v in arrays.items()}
    for name, shape in OUTPUTS:
        io[name] = nc.dram_tensor("out_" + name, shape, F32, kind="ExternalOutput").ap()
    build(nc, io, STAGES)
    got = run_bass_kernel_spmd(nc, [{"in_" + k: v for k, v in arrays.items()}], core_ids=[0]).results[0]
    return tuple(got["out_" + name] for name, _ in OUTPUTS)
```

```python
from contextlib import ExitStack

import numpy as np

import concourse.bass as bass
from concourse import mybir

F32, I32, U32 = mybir.dt.float32, mybir.dt.int32, mybir.dt.uint32
ALU, ACT, AX = mybir.AluOpType, mybir.ActivationFunctionType, mybir.AxisListType

P = 128
D = 1024
KD = D // P
SEQ, DB, DT = 1024, 8, 8
NS = DB * DT
T = SEQ + NS
NT = 9
TP = NT * P
EPS = 1e-6
CHUNKS = ((0, 512), (512, 512), (1024, NS))
CONV_K, HALO = 31, 30
EXT_S = HALO + DT
PAGES, PAGE, PHYS = 8, 128, 80
LEVELS = (32, 16, 8, 4, 2, 1)
NEG = -1e30


def rows(i, n=P):
    return bass.ds(i * n, n)


def after(n):
    return n + 1


class Link:

    def __init__(self, eng, sem, base=0):
        self.eng, self.sem, self.base, self.n = eng, sem, base, 0

    def __call__(self, ins):
        self.n += 1
        ins.then_inc(self.sem, 1)
        self.eng.wait_ge(self.sem, after(self.base + self.n))


class Place:

    def __init__(self, nc, ctx, psum=None):
        self.nc, self.ctx, self.psum, self.banks, self.sems, self.start = nc, ctx, psum, 0, [], []
        ctx.callback(self.clear)

    def sb(self, name, shape, dt=F32):
        return self.ctx.enter_context(self.nc.sbuf_tensor(name, shape, dt))

    def bank(self, name, banks=1):
        self.banks += banks
        return self.psum[:, 512 * (self.banks - banks):512 * self.banks]

    def sem(self, name):
        self.sems.append(self.nc.alloc_semaphore(name))
        if "loaded" not in name:
            self.start.append(self.sems[-1])
        return self.sems[-1]

    def clear(self):
        if self.sems:
            self.nc.clear_and_free_semaphores(self.sems)
            self.nc.all_engine_barrier()

    def block(self):
        nc = self.nc
        engines = (nc.sync, nc.gpsimd, nc.scalar, nc.vector, nc.tensor)
        for n, sem in enumerate(self.start):
            engines[n % len(engines)].sem_inc(sem, 1)
        nc.all_engine_barrier()
        return self.ctx.enter_context(nc.Block())


def project(pe, weights, xT, banks, ready):
    for c, (off, n) in enumerate(CHUNKS):
        for k in range(KD):
            last = pe.matmul(banks[c][:, 0:n], weights[:, k * P:(k + 1) * P], xT[:, k, off:off + n],
                             start=(k == 0), stop=(k == KD - 1))
        last.then_inc(ready, 1)


def stage_norm(nc, io, keep):
    with ExitStack() as ctx:
        m = Place(nc, ctx, keep["psum"])
        x_in, xs = m.sb("n_x", [P, 3, D]), m.sb("n_xs", [P, 3, D])
        junk, gain = m.sb("n_junk", [P, D]), m.sb("n_gain", [P, D])
        ss, rstd = m.sb("n_ss", [P, 3]), m.sb("n_rstd", [P, 3])
        pt = [m.bank(f"n_pt{u}", 2) for u in range(3)]
        x_loaded = [m.sem(f"n_x_loaded{u}") for u in range(3)]
        consts, sumsq, std, recip, scaled, turned, stored = (
            m.sem("n_" + s) for s in ("consts", "sumsq", "std", "recip", "scaled", "turned", "stored"))
        block = m.block()

        def store(act, i, u):
            act.wait_ge(turned, after(3 * i + u + 1))
            act.activation(keep["xT"][:, :, rows(i * 3 + u)],
                           pt[u][:, :].rearrange("p (k t) -> p k t", k=KD), ACT.Copy).then_inc(stored, 1)

        @block.sync
        def _(sp):
            sp.dma_start(gain[:, :], io["norm1_g"].partition_broadcast(P)).then_inc(consts, 16)
            sp.dma_start(keep["ident"][:, :], io["c_ident"]).then_inc(consts, 16)
            sp.dma_start(keep["eps"][:, :], io["c_eps"]).then_inc(consts, 16)
            with sp.Fori(0, 3) as i:
                for u in range(3):
                    sp.wait_ge(scaled, after(3 * i))
                    sp.dma_start(x_in[:, u, :], io["x_all"][rows(i * 3 + u), :]).then_inc(x_loaded[u], 16)

        @block.scalar
        def _(act):
            act.wait_ge(consts, after(48))
            with act.Fori(0, 3) as i:
                for u in range(3):
                    act.wait_ge(x_loaded[u], i * 16 + 16)
                    act.wait_ge(recip, after(3 * i))
                    act.activation(junk[:, :], x_in[:, u, :], ACT.Square, accum_out=ss[:, u:u + 1]).then_inc(sumsq, 1)
                    act.wait_ge(sumsq, after(3 * i + u + 1))
                    act.activation(rstd[:, u:u + 1], ss[:, u:u + 1], ACT.Sqrt, scale=1.0 / D,
                                   bias=keep["eps"][:, 0:1]).then_inc(std, 1)
                    if u >= 1:
                        store(act, i, u - 1)
                store(act, i, 2)

        @block.vector
        def _(dve):
            dve.wait_ge(consts, after(48))
            with dve.Fori(0, 3) as i:
                for u in range(3):
                    dve.wait_ge(std, after(3 * i + u + 1))
                    dve.reciprocal(rstd[:, u:u + 1], rstd[:, u:u + 1]).then_inc(recip, 1)
                    dve.wait_ge(recip, after(3 * i + u + 1))
                    dve.wait_ge(turned, after(3 * i))
                    dve.scalar_tensor_tensor(xs[:, u, :], x_in[:, u, :], rstd[:, u:u + 1], gain[:, :],
                                             ALU.mult, ALU.mult).then_inc(scaled, 1)

        @block.tensor
        def _(pe):
            pe.wait_ge(consts, after(48))
            with pe.Fori(0, 3) as i:
                for u in range(3):
                    pe.wait_ge(scaled, after(3 * i + u + 1))
                    pe.wait_ge(stored, after(3 * i))
                    for k in range(KD):
                        last = pe.transpose(pt[u][:, k * P:(k + 1) * P], xs[:, u, k * P:(k + 1) * P],
                                            keep["ident"][:, :])
                    last.then_inc(turned, 1)


def stage_hgrn(nc, io, keep):
    with ExitStack() as ctx:
        m = Place(nc, ctx, keep["psum"])
        w = [m.sb(f"h_w{u}", [P, KD * P]) for u in range(2)]
        q, k, b = m.sb("h_q", [P, T]), m.sb("h_k", [P, T]), m.sb("h_b", [P, T])
        f, gate, lf = m.sb("h_f", [P, T]), m.sb("h_gate", [P, T]), m.sb("h_lf", [P, T])
        v = m.sb("h_v", [P, NT, P])
        reset = m.sb("h_reset", [P, T])
        decay, qe, ke = m.sb("h_decay", [P, T]), m.sb("h_qe", [P, T]), m.sb("h_ke", [P, T])
        qk = m.sb("h_qk", [P, len(LEVELS), T])
        masks = m.sb("h_masks", [P, 7, P])
        picked = m.sb("h_picked", [P, 7, P])
        at = [m.sb(f"h_at{u}", [P, P]) for u in range(2)]
        keT = m.sb("h_keT", [P, 2, P])
        state = m.sb("h_state", [P, 2, P])
        s_old, s_new, v_batch = m.sb("h_s_old", [P, DB, P]), m.sb("h_s_new", [P, DB, P]), m.sb("h_v_batch", [NS, DB, P])
        batch = m.sb("h_batch", [NS, DB])
        o, sq, std = m.sb("h_o", [P, T]), lf, f
        mean_w, lb, gain = m.sb("h_mean_w", [P, P]), m.sb("h_lb", [P, 8, 4]), m.sb("h_gain", [P, 1])
        pz = [m.bank(f"h_z{c}") for c in range(6)]
        pa6 = m.bank("h_a6", 2)
        pa = [pa6[:, 0:7 * P], None]
        p_turn, p_o, p_ds = pz[2], pz[3], pz[4]
        w_loaded = [m.sem(f"h_w{u}_loaded") for u in range(2)]
        (consts, pool_done, s_loaded, q_z, f_z, g_z, v_z, q_ok, f_ok, g_ok, v_ok, k_ok, fm_ok, lf_ok, b_ok, eb_ok, kd_sub, kd_exp,
         ke_ok, qe_ok, lv_sub, lv_exp, qk_ok, a_ok, at_ok, turn, turned, ds, st_ok, o_ps, o_ok, vb_ok, sq_ok, ms, sd_ok,
         rs_ok, y_ok, out_ok, link, tmp_ok, pick_ok, dss) = (
            m.sem("h_" + s) for s in (
                "consts pool s_loaded q_z f_z g_z v_z q_ok f_ok g_ok v_ok k_ok fm_ok lf_ok b_ok eb_ok kd_sub kd_exp ke_ok qe_ok "
                "lv_sub lv_exp qk_ok a_ok at_ok turn turned ds st_ok o_ps o_ok vb_ok sq_ok ms sd_ok rs_ok y_ok out link tmp "
                "pick_ok dss").split())
        NL = len(LEVELS)
        block = m.block()

        def halves(x, level):
            h = LEVELS[level]
            end = T if 2 * h <= DT else SEQ
            v4 = x[:, 0:end].rearrange("p (n s h) -> p n s h", s=2, h=h)
            return v4[:, :, 0, :], v4[:, :, 1, :], v4[:, :, 0, h - 1:h].broadcast_to([P, end // (2 * h), h])

        @block.sync
        def _(sp):
            sp.dma_start(reset[:, :], io["c_reset"].partition_broadcast(P)).then_inc(consts, 16)
            sp.dma_start(masks[:, :, :], io["c_levels"]).then_inc(consts, 16)
            sp.dma_start(batch[:, :], io["c_batch"]).then_inc(consts, 16)
            sp.dma_start(lb[:, 0, :], io["hg_lb"]).then_inc(consts, 16)
            sp.dma_start(gain[:, :], io["hg_norm"]).then_inc(consts, 16)
            with sp.Fori(0, 4) as i:
                for n, used in enumerate((g_z, v_z, None, None)):
                    u = n % 2
                    if used is None:
                        sp.wait_ge((q_z, f_z)[u], after(3 * i + 3))
                    else:
                        sp.wait_ge(used, after(3 * i))
                    sp.dma_start(w[u][:, :], io["w_hgrn"][rows(4 * i + n), :]).then_inc(w_loaded[u], 16)
                sp.wait_ge(dss, after(i))
                sp.dma_start(s_old[:, :, :], io["state_hgrn"][rows(i), :, :]).then_inc(s_loaded, 16)
                sp.wait_ge(dss, after(i + 1))
                sp.dma_start(io["new_hgrn_sample"][0].rearrange("b h k v -> h k b v")[bass.ds(i, 1)].rearrange("a k b v -> (a k) b v"), s_new[:, :, :]).then_inc(out_ok, 16)
                sp.dma_start(io["new_hgrn_prompt"][0, 0][bass.ds(i, 1)].rearrange("a k v -> (a k) v"), state[:, 0, :]).then_inc(out_ok, 16)
            sp.wait_ge(out_ok, after(16 * 8))

        @block.gpsimd
        def _(pool):
            pool.memset(mean_w[:, :], 1.0 / P).then_inc(pool_done, 1)

        @block.tensor
        def _(pe):
            pe.wait_ge(pool_done, after(1))
            with pe.Fori(0, 4) as i:
                pe.wait_ge(w_loaded[0], 32 * i + 16)
                pe.wait_ge(sd_ok, after(i))
                project(pe, w[0], keep["xT"], pz[0:3], q_z)
                pe.wait_ge(w_loaded[1], 32 * i + 16)
                pe.wait_ge(o_ok, after(NT * i))
                pe.wait_ge(dss, after(i))
                project(pe, w[1], keep["xT"], pz[3:6], f_z)
                pe.wait_ge(w_loaded[0], 32 * i + 32)
                pe.wait_ge(q_ok, after(3 * i + 3))
                project(pe, w[0], keep["xT"], pz[0:3], g_z)
                pe.wait_ge(w_loaded[1], 32 * i + 32)
                pe.wait_ge(f_ok, after(3 * i + 3))
                for t in range(NT):
                    for kk in range(KD):
                        last = pe.matmul(pz[3 + t // 4][:, t % 4 * P:(t % 4 + 1) * P], keep["xT"][:, kk, t * P:(t + 1) * P],
                                         w[1][:, kk * P:(kk + 1) * P], start=(kk == 0), stop=(kk == KD - 1))
                    if t % 4 == 3 or t == NT - 1:
                        last.then_inc(v_z, 1)
                pe.wait_ge(qk_ok, after(NL * i + NL))
                pe.wait_ge(v_ok, after(3 * i + 3))
                pe.wait_ge(g_ok, after(3 * i + 3))
                for t in range(NT):
                    n = P if t < NT - 1 else NS
                    cols = slice(t * P, t * P + n)
                    pe.wait_ge(ke_ok, after(i + 1))
                    pe.wait_ge(turned, after(NT * i + t))
                    pe.wait_ge(at_ok, after(NT * i + t))
                    first = 0 if t < NT - 1 else 3
                    for lv in range(first, NL + 1):
                        a, bb = (qk[:, lv, cols], qk[:, lv, cols]) if lv < NL else (k[:, cols], q[:, cols])
                        last = pe.matmul(pa6[0:n, lv * P:lv * P + n], a, bb, start=True, stop=True)
                    last.then_inc(a_ok, 1)
                    pe.transpose(p_turn[0:n, 0:P], ke[:, cols], keep["ident"][:, :]).then_inc(turn, 1)
                    pe.wait_ge(at_ok, after(NT * i + t + 1))
                    pe.wait_ge(o_ok, after(NT * i + t))
                    pe.wait_ge(qe_ok, after(i + 1))
                    if t < NT - 1:
                        pe.matmul(p_o[:, 0:P], v[:, t, :], at[t % 2][:, :], start=True, stop=False, skip_group_check=True)
                        pe.wait_ge(turned, after(NT * i + t + 1))
                        for c in range(2):
                            pe.wait_ge(st_ok, after(17 * i + 2 * t + c + 1))
                            last = pe.matmul(p_o[:, c * 64:c * 64 + 64], state[:, c, :], qe[:, t * P + c * 64:t * P + c * 64 + 64],
                                             start=False, stop=(c == 1), skip_group_check=True)
                            if c == 1:
                                last.then_inc(o_ps, 1)
                            pe.matmul(p_ds[:, c * P:(c + 1) * P], keT[c * 64:c * 64 + 64, t % 2, :], v[c * 64:c * 64 + 64, t, :],
                                      start=True, stop=True).then_inc(ds, 1)
                    else:
                        pe.matmul(p_o[:, 0:n], v[0:n, t, :], at[t % 2][0:n, 0:n], start=True, stop=False, skip_group_check=True)
                        pe.wait_ge(s_loaded, 16 * i + 16)
                        for bt in range(DB):
                            last = pe.matmul(p_o[:, bt * DT:(bt + 1) * DT], s_old[:, bt, :], qe[:, SEQ + bt * DT:SEQ + (bt + 1) * DT],
                                             start=False, stop=(bt == DB - 1), skip_group_check=True)
                        last.then_inc(o_ps, 1)
                        pe.wait_ge(turned, after(NT * i + t + 1))
                        pe.wait_ge(vb_ok, after(i + 1))
                        pe.wait_ge(st_ok, after(17 * i + 17))
                        for hf in range(2):
                            last = pe.matmul(pz[4 + hf][:, :], keT[0:n, t % 2, :], v_batch[:, 4 * hf:4 * hf + 4, :], start=True, stop=True)
                        last.then_inc(ds, 1)
                pe.wait_ge(sq_ok, after(i + 1))
                for c, (off, n) in enumerate(CHUNKS):
                    last = pe.matmul(pz[c][:, 0:n], mean_w[:, :], sq[:, off:off + n], start=True, stop=True)
                last.then_inc(ms, 1)

        @block.scalar
        def _(act):
            act.wait_ge(consts, after(80))
            with act.Fori(0, 4) as i:
                act.wait_ge(y_ok, after(i))
                for c, (off, n) in enumerate(CHUNKS):
                    act.wait_ge(q_z, after(3 * i + c + 1))
                    act.activation(q[:, off:off + n], pz[c][:, 0:n], ACT.Silu).then_inc(q_ok, 1)
                for c, (off, n) in enumerate(CHUNKS):
                    act.wait_ge(f_z, after(3 * i + c + 1))
                    act.activation(f[:, off:off + n], pz[3 + c][:, 0:n], ACT.Sigmoid).then_inc(f_ok, 1)
                for c, (off, n) in enumerate(CHUNKS):
                    act.wait_ge(g_z, after(3 * i + c + 1))
                    act.activation(gate[:, off:off + n], pz[c][:, 0:n], ACT.Sigmoid).then_inc(g_ok, 1)
                act.wait_ge(fm_ok, after(i + 1))
                act.activation(lf[:, :], lf[:, :], ACT.Ln).then_inc(lf_ok, 1)
                for c in range(3):
                    act.wait_ge(v_z, after(3 * i + c + 1))
                    if c < 2:
                        act.activation(v[:, 4 * c:4 * c + 4, :], pz[3 + c][:, :].rearrange("p (a n) -> p a n", a=4), ACT.Copy).then_inc(v_ok, 1)
                    else:
                        act.activation(v[:, 8, :], pz[5][:, 0:P], ACT.Copy).then_inc(v_ok, 1)
                act.wait_ge(b_ok, after(i + 1))
                act.activation(decay[:, :], b[:, :], ACT.Exp).then_inc(eb_ok, 1)
                act.wait_ge(kd_sub, after(i + 1))
                act.activation(ke[:, :], ke[:, :], ACT.Exp).then_inc(kd_exp, 1)
                for lv in range(NL):
                    end = T if 2 * LEVELS[lv] <= DT else SEQ
                    act.wait_ge(lv_sub, after(NL * i + lv + 1))
                    act.activation(qk[:, lv, 0:end], qk[:, lv, 0:end], ACT.Exp).then_inc(lv_exp, 1)
                for t in range(NT):
                    n = P if t < NT - 1 else NS
                    act.wait_ge(turn, after(NT * i + t + 1))
                    if t >= 2:
                        act.wait_ge(ds, after(17 * i + 2 * t - 2))
                    act.activation(keT[0:n, t % 2, :], p_turn[0:n, 0:P], ACT.Copy).then_inc(turned, 1)
                    act.wait_ge(o_ps, after(NT * i + t + 1))
                    act.activation(o[:, t * P:t * P + n], p_o[:, 0:n], ACT.Copy).then_inc(o_ok, 1)
                act.wait_ge(o_ok, after(NT * i + NT))
                act.activation(sq[:, :], o[:, :], ACT.Square).then_inc(sq_ok, 1)
                act.wait_ge(ms, after(i + 1))
                for c, (off, n) in enumerate(CHUNKS):
                    last = act.activation(std[:, off:off + n], pz[c][:, 0:n], ACT.Sqrt, bias=keep["eps"][:, 0:1])
                last.then_inc(sd_ok, 1)

        @block.vector
        def _(dve):
            lk = Link(dve, link)
            dve.wait_ge(consts, after(80))
            lk(dve.tensor_tensor(lb[:, 1, :], lb[:, 0, :], lb[:, 0, :], ALU.max))
            lk(dve.tensor_tensor(lb[:, 2, :], lb[:, 0, :], lb[:, 1, :], ALU.subtract))
            lk(dve.tensor_scalar(lb[:, 3, :], lb[:, 2, :], 1.0, None, ALU.add))
            lk(dve.reciprocal(lb[:, 4, :], lb[:, 3, :]))
            lk(dve.tensor_tensor(lb[:, 4, :], lb[:, 3, :], lb[:, 4, :], ALU.mult))
            lk(dve.tensor_tensor(lb[:, 5, :], lb[:, 4, :], lb[:, 4, :], ALU.subtract))
            lk(dve.tensor_scalar(lb[:, 5, :], lb[:, 5, :], 0.0, 1.0, ALU.max, ALU.min))
            lk(dve.tensor_scalar(lb[:, 6, :], lb[:, 5, :], -1.0, 1.0, ALU.mult, ALU.add))
            dve.wait_ge(pool_done, after(1))
            with dve.Fori(0, 4) as i:
                dve.wait_ge(f_ok, after(3 * i + 3))
                dve.tensor_scalar(f[:, :], f[:, :], lb[:, 6, bass.ds(i, 1)], lb[:, 5, bass.ds(i, 1)], ALU.mult, ALU.add).then_inc(tmp_ok, 1)
                dve.wait_ge(tmp_ok, after(2 * i + 1))
                dve.tensor_scalar(lf[:, :], f[:, :], 1e-20, None, ALU.max).then_inc(fm_ok, 1)
                dve.tensor_scalar(k[:, :], f[:, :], -1.0, 1.0, ALU.mult, ALU.add).then_inc(k_ok, 1)
                dve.wait_ge(lf_ok, after(i + 1))
                dve.tensor_tensor_scan(b[:, :], reset[:, :], lf[:, :], 0.0, ALU.mult, ALU.add).then_inc(b_ok, 1)
                dve.wait_ge(b_ok, after(i + 1))
                bp, bs = b[:, 0:SEQ].rearrange("p (n c) -> p n c", c=64), b[:, SEQ:T].rearrange("p (n c) -> p n c", c=DT)
                kp, ks = ke[:, 0:SEQ].rearrange("p (n c) -> p n c", c=64), ke[:, SEQ:T].rearrange("p (n c) -> p n c", c=DT)
                dve.tensor_tensor(kp, bp[:, :, 63:64].broadcast_to([P, 16, 64]), bp, ALU.subtract)
                dve.tensor_tensor(ks, bs[:, :, DT - 1:DT].broadcast_to([P, DB, DT]), bs, ALU.subtract).then_inc(kd_sub, 1)
                for lv in range(NL):
                    bl, br, ref = halves(b, lv)
                    xl, xr, _ = halves(qk[:, lv, :], lv)
                    dve.tensor_tensor(xl, ref, bl, ALU.subtract)
                    dve.tensor_tensor(xr, br, ref, ALU.subtract).then_inc(lv_sub, 1)
                dve.wait_ge(eb_ok, after(i + 1))
                dve.wait_ge(q_ok, after(3 * i + 3))
                dve.tensor_tensor(qe[:, :], q[:, :], decay[:, :], ALU.mult).then_inc(qe_ok, 1)
                dve.wait_ge(kd_exp, after(i + 1))
                dve.wait_ge(k_ok, after(i + 1))
                dve.tensor_tensor(ke[:, :], ke[:, :], k[:, :], ALU.mult).then_inc(ke_ok, 1)
                for lv in range(NL):
                    kl, _, _ = halves(k, lv)
                    _, qr, _ = halves(q, lv)
                    xl, xr, _ = halves(qk[:, lv, :], lv)
                    dve.wait_ge(lv_exp, after(NL * i + lv + 1))
                    dve.tensor_tensor(xl, xl, kl, ALU.mult)
                    dve.tensor_tensor(xr, xr, qr, ALU.mult).then_inc(qk_ok, 1)
                dve.wait_ge(out_ok, after(32 * i))
                dve.memset(state[:, 0, :], 0.0).then_inc(st_ok, 1)
                for t in range(NT):
                    n = P if t < NT - 1 else NS
                    dve.wait_ge(a_ok, after(NT * i + t + 1))
                    if t >= 2:
                        dve.wait_ge(o_ps, after(NT * i + t - 1))
                    first = 0 if t < NT - 1 else 3
                    products = pa6[0:n, 0:7 * P].rearrange("p (l t) -> p l t", l=7)[:, first:, 0:n]
                    dve.wait_ge(at_ok, after(NT * i + t))
                    dve.tensor_tensor(picked[0:n, first:, 0:n], products, masks[0:n, first:, 0:n], ALU.mult).then_inc(pick_ok, 1)
                    dve.wait_ge(pick_ok, after(NT * i + t + 1))
                    dve.tensor_reduce(at[t % 2][0:n, 0:n], picked[0:n, first:, 0:n].rearrange("p l t -> p t l"), AX.X, ALU.add).then_inc(at_ok, 1)
                    if t < NT - 1:
                        for c in range(2):
                            dve.wait_ge(ds, after(17 * i + 2 * t + c + 1))
                            dve.wait_ge(st_ok, after(17 * i + 2 * t + c + 1))
                            end = t * P + c * 64 + 63
                            dve.scalar_tensor_tensor(state[:, 1 - c, :], state[:, c, :], decay[:, end:end + 1],
                                                     p_ds[:, c * P:(c + 1) * P], ALU.mult, ALU.add).then_inc(st_ok, 1)
                    else:
                        dve.wait_ge(v_ok, after(3 * i + 3))
                        dve.tensor_tensor(v_batch[:, :, :], v[0:NS, t, :].unsqueeze(1).broadcast_to([NS, DB, P]),
                                          batch[:, :].unsqueeze(2).broadcast_to([NS, DB, P]), ALU.mult).then_inc(vb_ok, 1)
                        dve.wait_ge(s_loaded, 16 * i + 16)
                        ends = decay[:, SEQ:T].rearrange("p (n c) -> p n c", c=DT)[:, :, DT - 1:DT]
                        dve.tensor_tensor(s_new[:, :, :], s_old[:, :, :], ends.broadcast_to([P, DB, P]), ALU.mult).then_inc(tmp_ok, 1)
                        dve.wait_ge(tmp_ok, after(2 * i + 2))
                        dve.wait_ge(ds, after(17 * i + 17))
                        dve.wait_ge(o_ps, after(NT * i + NT))
                        for hf in range(2):
                            last = dve.tensor_tensor(s_new[:, 4 * hf:4 * hf + 4, :], s_new[:, 4 * hf:4 * hf + 4, :],
                                                     pz[4 + hf][:, :].rearrange("p (b v) -> p b v", b=4), ALU.add)
                        last.then_inc(dss, 1)
                dve.wait_ge(sd_ok, after(i + 1))
                dve.reciprocal(std[:, :], std[:, :]).then_inc(rs_ok, 1)
                dve.wait_ge(rs_ok, after(2 * i + 1))
                dve.scalar_tensor_tensor(o[:, :], o[:, :], gain[:, 0:1], std[:, :], ALU.mult, ALU.mult).then_inc(rs_ok, 1)
                dve.wait_ge(rs_ok, after(2 * i + 2))
                dve.tensor_tensor(keep["branch"][:, bass.ds(i + 4, 1), :], o[:, :], gate[:, :], ALU.mult).then_inc(y_ok, 1)


def stage_fox(nc, io, keep):
    with ExitStack() as ctx:
        m = Place(nc, ctx, keep["psum"])
        w = [m.sb(f"f_w{u}", [P, KD * P]) for u in range(3)]
        w_af = m.sb("f_w_af", [P, KD * 64])
        q = [m.sb(f"f_q{u}", [P, SEQ]) for u in range(2)]
        kT, v, k_tok = m.sb("f_kT", [P, T]), m.sb("f_v", [P, NT, P]), m.sb("f_k_tok", [P, NT, P])
        bias_q = [m.sb(f"f_bias_q{u}", [64, SEQ]) for u in range(2)]
        bias_k, a, lf = m.sb("f_bias_k", [64, T]), m.sb("f_a", [64, T]), m.sb("f_lf", [64, T])
        e1, reset = m.sb("f_e1", [64, T]), m.sb("f_reset", [64, T])
        lf_tok = m.sb("f_lf_tok", [P, NT, 8])
        row_coef, heads, fb = m.sb("f_rows", [64, 2]), m.sb("f_heads", [64, 2, 8]), m.sb("f_fb", [64, 1])
        causal = m.sb("f_causal", [P, P])
        p, pT = m.sb("f_p", [P, 2, SEQ]), m.sb("f_pT", [P, 2, SEQ])
        nmax, rsum, rinv, diag = m.sb("f_nmax", [P, 2]), m.sb("f_rsum", [P, 2]), m.sb("f_rinv", [P, 2]), m.sb("f_diag", [P, 2, P])
        ps = [m.bank(f"f_s{u}", 2) for u in range(2)]
        pt = [m.bank(f"f_t{u}") for u in range(2)]
        po = [m.bank(f"f_o{u}") for u in range(2)]
        pz = [ps[0][:, 0:512], ps[0][:, 512:1024], ps[1][:, 0:512], ps[1][:, 512:1024], pt[0], pt[1]]
        w_loaded = [m.sem(f"f_w{u}_loaded") for u in range(3)]
        (consts, af_loaded, pool_done, af_z, a_ok, abs_ok, exp0_ok, ln_ok, lf_ok, c_ok, lft, lft_ok, bk_ok, q_z, k_z, v_z,
         q_ok, k_ok, v_ok, kt_ps, kt_ok, bq_ok, s_ps, max_ok, exp_ok, ri_ok, diag_ok, t0_ps, t1_ps, t0_ok, t1_ok, pv, o_ok, stored) = (
            m.sem("f_" + s) for s in (
                "consts af_loaded pool af_z a_ok abs_ok exp0_ok ln_ok lf_ok c_ok lft lft_ok bk_ok q_z k_z v_z q_ok k_ok v_ok kt_ps kt_ok "
                "bq_ok s_ps max_ok exp_ok ri_ok diag_ok t0_ps t1_ps t0_ok t1_ok pv o_ok stored").split())
        block = m.block()
        UNITS = [(qi, hh) for qi in range(8) for hh in range(2)]
        cs, qs_s, ks_s, vs_s = keep["c_new"], keep["q_new"], keep["k_new"], keep["v_new"]

        def tokens(name, width):
            return io[name + "_prompt"].rearrange(f"a b (t p) {width} -> p (a b t) ({width})", p=P)

        @block.sync
        def _(sp):
            sp.dma_start(w_af[:, :], io["w_af"]).then_inc(af_loaded, 16)
            for dst, src in ((row_coef, "c_rows"), (heads, "c_heads"), (fb, "att_fb"), (causal, "c_causal")):
                sp.dma_start(dst[:], io[src]).then_inc(consts, 16)
            sp.dma_start(reset[:, :], io["c_reset_c"].partition_broadcast(64)).then_inc(consts, 16)
            with sp.Fori(0, 4) as i:
                for u, used in enumerate((q_z, k_z, v_z)):
                    sp.wait_ge(used, after(3 * i))
                    sp.dma_start(w[u][:, :], io["w_fox"][rows(3 * i + u), :]).then_inc(w_loaded[u], 16)
                for src, ok, name in ((v, v_ok, "new_v"), (k_tok, kt_ok, "new_k")):
                    sp.wait_ge(ok, after(3 * i + 3))
                    sp.dma_start(tokens(name, "h d")[:, :, rows(i)], src[:, 0:8, :]).then_inc(stored, 16)
                    sp.dma_start(io[name + "_sample"].rearrange("a b t h d -> (a b t) (h d)")[:, rows(i)], src[0:NS, 8, :]).then_inc(stored, 16)
            sp.wait_ge(lft_ok, after(2))
            with nc.allow_non_contiguous_dma(reason="8 values per token"):
                sp.dma_start(tokens("new_logf", "h"), lf_tok[:, 0:8, :]).then_inc(stored, 16)
                sp.dma_start(io["new_logf_sample"].rearrange("a b t h -> (a b t) h"), lf_tok[0:NS, 8, :]).then_inc(stored, 16)
            sp.wait_ge(stored, after(16 * 18))

        @block.gpsimd
        def _(pool):
            pool.memset(q[0][64:P, :], 0.0).then_inc(pool_done, 1)
            pool.memset(q[1][0:64, :], 0.0).then_inc(pool_done, 1)

        @block.tensor
        def _(pe):
            pe.wait_ge(af_loaded, 16)
            for c, (off, n) in enumerate(CHUNKS):
                for kk in range(KD):
                    last = pe.matmul(pz[c][0:64, 0:n], w_af[:, kk * 64:(kk + 1) * 64], keep["xT"][:, kk, off:off + n],
                                     start=(kk == 0), stop=(kk == KD - 1))
                last.then_inc(af_z, 1)
            pe.wait_ge(lf_ok, after(1))
            for t in range(NT):
                n = P if t < 8 else NS
                last = pe.transpose(po[t // 8][0:n, t % 8 * 64:t % 8 * 64 + 64], lf[:, t * P:t * P + n], keep["ident"][0:64, 0:64])
            last.then_inc(lft, 1)
            pe.wait_ge(pool_done, after(2))

            def scores(i, n_unit):
                qi, hh = UNITS[n_unit]
                u = n_unit % 2
                if n_unit >= 2:
                    pe.wait_ge(exp_ok, after(16 * i + n_unit - 1))
                for part in range(qi // 4 + 1):
                    n = min(512, (qi + 1) * P - part * 512)
                    out, keys = ps[u][:, part * 512:part * 512 + n], slice(part * 512, part * 512 + n)
                    pe.matmul(out, q[hh][:, qi * P:(qi + 1) * P], kT[:, keys], start=True, stop=False, skip_group_check=True)
                    last = pe.matmul(out, bias_q[hh][:, qi * P:(qi + 1) * P], bias_k[:, keys], start=False,
                                     stop=(part < qi // 4), skip_group_check=True)
                last = pe.matmul(ps[u][:, qi * P:(qi + 1) * P], keep["ident"][:, :], causal[:, :], start=False, stop=True,
                                 skip_group_check=True)
                last.then_inc(s_ps, 1)

            def turn(i, n_unit):
                qi, hh = UNITS[n_unit]
                u = n_unit % 2
                pe.wait_ge(diag_ok, after(16 * i + n_unit + 1))
                for part in range(qi // 4 + 1):
                    done = 16 * i + n_unit if part == 0 else 8 * i + n_unit - 8
                    pe.wait_ge((t0_ok, t1_ok)[part], after(done))
                    for kb in range(4 * part, min(4 * part + 4, qi + 1)):
                        last = pe.matmul(pt[part][:, kb % 4 * P:kb % 4 * P + P], p[:, u, kb * P:(kb + 1) * P], diag[:, u, :],
                                         start=True, stop=True)
                    last.then_inc((t0_ps, t1_ps)[part], 1)

            def values(i, n_unit):
                qi, hh = UNITS[n_unit]
                u = n_unit % 2
                pe.wait_ge(t0_ok, after(16 * i + n_unit + 1))
                if qi >= 4:
                    pe.wait_ge(t1_ok, after(8 * i + n_unit - 7))
                if hh == 0 and qi >= 2:
                    pe.wait_ge(o_ok, after(8 * i + qi - 1))
                for kb in range(qi + 1):
                    last = pe.matmul(po[qi % 2][hh * 64:(hh + 1) * 64, 0:P], v[:, kb, hh * 64:(hh + 1) * 64],
                                     pT[:, u, kb * P:(kb + 1) * P], start=(kb == 0), stop=(kb == qi))
                last.then_inc(pv, 1)

            with pe.Fori(0, 4) as i:
                pe.wait_ge(w_loaded[0], 16 * i + 16)
                pe.wait_ge(a_ok, after(3))
                pe.wait_ge(exp_ok, after(16 * i))
                project(pe, w[0], keep["xT"], pz[0:3], q_z)
                pe.wait_ge(w_loaded[1], 16 * i + 16)
                pe.wait_ge(t0_ok, after(16 * i))
                pe.wait_ge(t1_ok, after(8 * i))
                project(pe, w[1], keep["xT"], pz[3:6], k_z)
                pe.wait_ge(w_loaded[2], 16 * i + 16)
                pe.wait_ge(q_ok, after(3 * i + 3))
                for t in range(NT):
                    for kk in range(KD):
                        last = pe.matmul(pz[t // 4][:, t % 4 * P:(t % 4 + 1) * P], keep["xT"][:, kk, t * P:(t + 1) * P],
                                         w[2][:, kk * P:(kk + 1) * P], start=(kk == 0), stop=(kk == KD - 1))
                    if t % 4 == 3 or t == NT - 1:
                        last.then_inc(v_z, 1)
                pe.wait_ge(k_ok, after(3 * i + 3))
                for t in range(NT):
                    n = P if t < 8 else NS
                    last = pe.transpose(pz[3 + t // 4][0:n, t % 4 * P:(t % 4 + 1) * P], kT[:, t * P:t * P + n], keep["ident"][:, :])
                    if t % 4 == 3 or t == NT - 1:
                        last.then_inc(kt_ps, 1)
                pe.wait_ge(v_ok, after(3 * i + 3))
                pe.wait_ge(kt_ok, after(3 * i + 3))
                pe.wait_ge(bq_ok, after(2 * i + 2))
                pe.wait_ge(lft_ok, after(2))
                pe.wait_ge(o_ok, after(8 * i))
                scores(i, 0)
                for n_unit in range(16):
                    if n_unit + 1 < 16:
                        scores(i, n_unit + 1)
                    if n_unit >= 1:
                        values(i, n_unit - 1)
                    turn(i, n_unit)
                values(i, 15)

        @block.scalar
        def _(act):
            act.wait_ge(consts, after(80))
            for c, (off, n) in enumerate(CHUNKS):
                act.wait_ge(af_z, after(c + 1))
                act.activation(a[:, off:off + n], pz[c][0:64, 0:n], ACT.Identity, bias=fb[:, 0:1]).then_inc(a_ok, 1)
            act.wait_ge(a_ok, after(3))
            act.activation(e1[:, :], a[:, :], ACT.Abs).then_inc(abs_ok, 1)
            act.wait_ge(abs_ok, after(1))
            act.activation(e1[:, :], e1[:, :], ACT.Exp, scale=-1.0).then_inc(exp0_ok, 1)
            act.wait_ge(exp0_ok, after(1))
            act.activation(e1[:, :], e1[:, :], ACT.Ln, bias=1.0).then_inc(ln_ok, 1)
            act.wait_ge(lft, after(1))
            act.activation(lf_tok[:, 0:8, :], po[0][:, :].rearrange("p (t h) -> p t h", t=8)[:, :, 0:8], ACT.Copy).then_inc(lft_ok, 1)
            act.activation(lf_tok[0:NS, 8, :], po[1][0:NS, 0:8], ACT.Copy).then_inc(lft_ok, 1)
            with act.Fori(0, 4) as i:
                for c, (off, n) in enumerate(CHUNKS):
                    act.wait_ge(q_z, after(3 * i + c + 1))
                    if c < 2:
                        act.activation(q[0][0:64, off:off + n], pz[c][0:64, 0:n], ACT.Copy, scale=0.125)
                        act.activation(q[1][64:P, off:off + n], pz[c][64:P, 0:n], ACT.Copy, scale=0.125).then_inc(q_ok, 1)
                    else:
                        act.activation(qs_s[:, bass.ds(i, 1), :], pz[c][:, 0:n], ACT.Copy, scale=0.125).then_inc(q_ok, 1)
                act.wait_ge(stored, after(64 * i))
                for c in range(3):
                    act.wait_ge(v_z, after(3 * i + c + 1))
                    if c < 2:
                        act.activation(v[:, 4 * c:4 * c + 4, :], pz[c][:, :].rearrange("p (a n) -> p a n", a=4), ACT.Copy).then_inc(v_ok, 1)
                    else:
                        act.activation(vs_s[:, rows(i)], pz[c][0:NS, 0:P], ACT.Copy)
                        act.activation(v[:, 8, :], pz[c][:, 0:P], ACT.Copy).then_inc(v_ok, 1)
                for n_unit, (qi, hh) in enumerate(UNITS):
                    u, n = n_unit % 2, (qi + 1) * P
                    act.wait_ge(max_ok, after(16 * i + n_unit + 1))
                    if n_unit >= 2:
                        act.wait_ge(t0_ok, after(16 * i + n_unit - 1))
                        if UNITS[n_unit - 2][0] >= 4:
                            act.wait_ge(t1_ok, after(8 * i + n_unit - 9))
                        act.wait_ge(ri_ok, after(16 * i + n_unit - 1))
                    act.activation(p[:, u, 0:n], ps[u][:, 0:n], ACT.Exp, bias=nmax[:, u:u + 1], accum_out=rsum[:, u:u + 1]).then_inc(exp_ok, 1)
                    if qi >= 4:
                        act.wait_ge(t1_ps, after(8 * i + n_unit - 7))
                        if n_unit >= 10:
                            act.wait_ge(pv, after(16 * i + n_unit - 1))
                        act.activation(pT[:, u, 512:n], pt[1][:, 0:n - 512], ACT.Copy).then_inc(t1_ok, 1)

        def out_tile(dve, i, qi):
            dve.wait_ge(pv, after(16 * i + 2 * qi + 2))
            dve.tensor_copy(keep["branch"][:, bass.ds(i + 8, 1), qi * P:(qi + 1) * P], po[qi % 2][:, 0:P].unsqueeze(1)).then_inc(o_ok, 1)

        @block.vector
        def _(dve):
            dve.wait_ge(consts, after(80))
            dve.wait_ge(ln_ok, after(1))
            dve.scalar_tensor_tensor(lf[:, :], a[:, :], 0.0, e1[:, :], ALU.min, ALU.subtract).then_inc(lf_ok, 1)
            dve.wait_ge(lf_ok, after(1))
            dve.tensor_tensor_scan(cs[:, :], reset[:, :], lf[:, :], 0.0, ALU.mult, ALU.add).then_inc(c_ok, 1)
            dve.wait_ge(c_ok, after(1))
            dve.tensor_scalar(bias_k[:, :], cs[:, :], row_coef[:, 0:1], row_coef[:, 1:2], ALU.mult, ALU.add).then_inc(bk_ok, 1)
            with dve.Fori(0, 4) as i:
                dve.wait_ge(pv, after(16 * i))
                for hh in range(2):
                    dve.tensor_scalar(bias_q[hh][:, :], cs[:, 0:SEQ], heads[:, 1, bass.ds(2 * i + hh, 1)],
                                      heads[:, 0, bass.ds(2 * i + hh, 1)], ALU.mult, ALU.add).then_inc(bq_ok, 1)
                for c, (off, n) in enumerate(CHUNKS):
                    dve.wait_ge(k_z, after(3 * i + c + 1))
                    if c == 2:
                        dve.tensor_copy(ks_s[:, bass.ds(i, 1), :], pz[3 + c][:, 0:n].unsqueeze(1))
                    dve.tensor_copy(kT[:, off:off + n], pz[3 + c][:, 0:n]).then_inc(k_ok, 1)
                dve.wait_ge(stored, after(64 * i))
                for c in range(3):
                    dve.wait_ge(kt_ps, after(3 * i + c + 1))
                    if c < 2:
                        dve.tensor_copy(k_tok[:, 4 * c:4 * c + 4, :], pz[3 + c][:, :].rearrange("p (a n) -> p a n", a=4)).then_inc(kt_ok, 1)
                    else:
                        dve.tensor_copy(k_tok[0:NS, 8, :], pz[5][0:NS, 0:P]).then_inc(kt_ok, 1)

                def soft(n_unit):
                    qi, hh = UNITS[n_unit]
                    u, n = n_unit % 2, (qi + 1) * P
                    dve.wait_ge(s_ps, after(16 * i + n_unit + 1))
                    dve.tensor_reduce(nmax[:, u:u + 1], ps[u][:, 0:n], AX.X, ALU.max, negate=True).then_inc(max_ok, 1)

                soft(0)
                for n_unit, (qi, hh) in enumerate(UNITS):
                    u, n = n_unit % 2, (qi + 1) * P
                    dve.wait_ge(exp_ok, after(16 * i + n_unit + 1))
                    dve.reciprocal(rinv[:, u:u + 1], rsum[:, u:u + 1]).then_inc(ri_ok, 1)
                    dve.wait_ge(ri_ok, after(16 * i + n_unit + 1))
                    dve.tensor_scalar(diag[:, u, :], keep["ident"][:, :], rinv[:, u:u + 1], None, ALU.mult).then_inc(diag_ok, 1)
                    if n_unit + 1 < 16:
                        soft(n_unit + 1)
                    dve.wait_ge(t0_ps, after(16 * i + n_unit + 1))
                    if n_unit >= 2:
                        dve.wait_ge(pv, after(16 * i + n_unit - 1))
                    dve.tensor_copy(pT[:, u, 0:min(n, 512)], pt[0][:, 0:min(n, 512)]).then_inc(t0_ok, 1)
                    if n_unit >= 2 and n_unit % 2 == 1:
                        out_tile(dve, i, (n_unit - 3) // 2)
                out_tile(dve, i, 7)


def stage_conv_sample(nc, io, keep):
    with ExitStack() as ctx:
        m = Place(nc, ctx, keep["psum"])
        w = [m.sb("c_w_gate", [P, KD * P]), m.sb("c_w_value", [P, KD * P])]
        sig, val = m.sb("c_sig", [P, T]), m.sb("c_val", [P, T])
        ext_p, ext_s = m.sb("c_ext_p", [P, HALO + SEQ]), m.sb("c_ext_s", [P, DB, EXT_S])
        halos = m.sb("c_halos", [P, 4, DB, HALO])
        glu_s = m.sb("c_glu_s", [P, NS])
        acc_p, acc_s = m.sb("c_acc_p", [P, SEQ]), m.sb("c_acc_s", [P, DB, DT])
        y = keep["branch"]
        sq, std, rstd = m.sb("c_sq", [P, 4, 512]), m.sb("c_std", [P, 512]), m.sb("c_rstd", [P, 512])
        taps_all, taps = m.sb("c_taps_all", [P, 4, CONV_K + 1]), m.sb("c_taps", [P, CONV_K + 1])
        ln = m.sb("c_ln", [P, 2, 4])
        mean_w = m.sb("c_mean_w", [P, P])
        tail_p, tail_s = m.sb("c_tail_p", [HALO, 4 * P]), m.sb("c_tail_s", [NS, 4 * P])
        bank_a, bank_b, bank_s = m.bank("c_a"), m.bank("c_b"), m.bank("c_s")
        z_ps = [(bank_a, bank_b), (bank_a, bank_b), (bank_s[:, 0:NS], bank_s[:, NS:2 * NS])]
        ln_ps = [bank_a, bank_b, bank_s[:, 0:NS]]
        tail_ps = bank_s[:, P:3 * P]
        w_loaded = [m.sem("c_wg_loaded"), m.sem("c_wv_loaded")]
        (c_consts, halo0, z_ok, copied, glu, halo_ok, taps_ready, tap_done, tails, tails_out,
         mean, centred, squared, var, stdev, recip, normed, out_sem, swish) = (
            m.sem("c_" + s) for s in ("consts", "halo0", "z", "copied", "glu", "halo_ok", "taps", "tap", "tails", "tails_out",
                                      "mean", "centred", "squared", "var", "stdev", "recip", "normed", "out", "swish"))
        W = PAGES * PAGE
        pages = m.sb("g_pages", [P, DB * PAGES], I32)
        lane = m.sb("g_lane", [P, 2], I32)
        pages_f, idx_f, lane_f = m.sb("g_pages_f", [P, 64]), m.sb("g_idx_f", [P, 2, 64]), m.sb("g_lane_f", [P, 2])
        idx = m.sb("g_idx", [P, 2, 64], I32)
        idx_now = [m.sb(f"g_idx_now{u}", [P, 2, PAGES], I32) for u in range(2)]
        kc, vc = m.sb("g_kc", [P, PAGES, 512]), m.sb("g_vc", [P, PAGES, 512])
        lfc = m.sb("g_lfc", [64, W])
        c_all, bias_k, ones = m.sb("g_c_all", [64, W + NS]), m.sb("g_bias_k", [64, W + NS]), m.sb("g_ones", [64, W])
        row_coef, sel = m.sb("g_rows", [64, 2]), m.sb("g_sel", [64, 2, P])
        bias_q = m.sb("g_bias_q", [64, P])
        mask_new = m.sb("g_mask", [P, DB, NS])
        q_rows = m.sb("g_q_rows", [P, 4, 32])
        p, pT = m.sb("g_p", [P, W + NS]), m.sb("g_pT", [P, 9, P])
        nmax, rsum, rinv, diag = m.sb("g_nmax", [P, 1]), m.sb("g_rsum", [P, 1]), m.sb("g_rinv", [P, 1]), m.sb("g_diag", [P, P])
        ps3 = m.bank("g_s", 3)
        ps, po, pt_new = ps3[:, 0:W + NS], ps3[:, 1088:1216], ps3[:, 1216:1344]
        pt = m.bank("g_t", 2)
        k_loaded, v_loaded, lf_loaded = ([m.sem(f"g_{x}_loaded{n}") for n in range(PAGES)] for x in "kvl")
        (consts, pool_done, gate, idx_tmp, idx_ok, now_ok, c_ok, cn_ok, bk_ok, bq_ok, bq0, qr_ok, s_ps, max_ok, exp_ok, ri_ok, diag_ok,
         t_ps, t_ok, pv, o_ok) = (m.sem("g_" + s) for s in (
             "consts pool gate idx_tmp idx_ok now_ok c_ok cn_ok bk_ok bq_ok bq0 qr_ok s_ps max_ok exp_ok ri_ok diag_ok t_ps t_ok pv o_ok").split())
        block = m.block()
        c_new, q_new, k_new, v_new = keep["c_new"], keep["q_new"], keep["k_new"], keep["v_new"]

        def tiles(eng, body):
            with eng.Fori(0, 3) as i:
                body(i, True)
            body(3, False)

        @block.sync
        def _(sp):
            sp.dma_start(pages[:, :], io["page_table"].partition_broadcast(P)).then_inc(consts, 16)
            for dst, src in ((lane, "c_lane"), (row_coef, "c_rows"), (sel, "c_sel"), (mask_new, "c_new")):
                sp.dma_start(dst[:], io[src]).then_inc(consts, 16)
            for v in range(2):
                sp.dma_start(w[v][:, :], io["w_conv"][v * P:(v + 1) * P, :]).then_inc(w_loaded[v], 16)
            sp.dma_start(taps_all[:, :, :], io["conv_taps"]).then_inc(c_consts, 16)
            sp.dma_start(ln[:, :, :], io["conv_ln"]).then_inc(c_consts, 16)
            for i in range(4):
                sp.dma_start(halos[:, i, :, :], io["state_convT"][i * P:(i + 1) * P, :, :]).then_inc(c_consts, 16)
            with sp.Fori(0, 3) as i:
                for v in range(2):
                    sp.wait_ge(z_ok, after(6 * i + 6))
                    sp.dma_start(w[v][:, :], io["w_conv"][rows(i * 2 + 2 + v), :]).then_inc(w_loaded[v], 16)
            sp.dma_start(io["new_conv_sample"][0, :, 0:HALO - DT, :], io["state_conv"][0, :, DT:HALO, :]).then_inc(out_sem, 16)
            sp.wait_ge(tails_out, after(8))
            sp.dma_start(io["new_conv_prompt"][0, 0, :, :], tail_p[:, :]).then_inc(out_sem, 16)
            for b in range(DB):
                sp.dma_start(io["new_conv_sample"][0, b, HALO - DT:HALO, :], tail_s[b * DT:(b + 1) * DT, :]).then_inc(out_sem, 16)
            sp.wait_ge(out_sem, after(16 * (2 + DB)))

        @block.gpsimd
        def _(pool):
            pool.memset(mean_w[:, :], 1.0 / 512).then_inc(halo0, 1)
            pool.memset(ext_p[:, 0:HALO], 0.0).then_inc(halo0, 1)
            pool.memset(ones[:, :], 1.0)
            pool.memset(q_rows[:, :, :], 0.0).then_inc(pool_done, 1)
            pool.wait_ge(idx_ok, after(2))
            with pool.Fori(0, DB // 2) as half:
                for u in range(2):
                    b, now = half * 2 + u, idx_now[u]
                    pool.tensor_copy(now[:, :, :], idx[:, :, rows(b, PAGES)]).then_inc(now_ok, 1)
                    pool.wait_ge(now_ok, after(b + 1))
                    pool.wait_ge(c_ok, after(b))
                    pool.sem_inc(gate, 1)
                    for n in range(PAGES):
                        pool.indirect_dma_start(lfc[:, n * PAGE:(n + 1) * PAGE], None, io["cache_lfT"],
                                                bass.IndirectOffsetOnAxis(ap=now[0:64, 1, n:n + 1], axis=0)).then_inc(lf_loaded[n], 16)
                    pool.wait_ge(s_ps, after(b))
                    pool.sem_inc(gate, 1)
                    for n in range(PAGES):
                        pool.indirect_dma_start(kc[:, n, :], None, io["cache_kT"],
                                                bass.IndirectOffsetOnAxis(ap=now[:, 0, n:n + 1], axis=0)).then_inc(k_loaded[n], 16)
                    pool.wait_ge(pv, after(b))
                    pool.sem_inc(gate, 1)
                    for n in range(PAGES):
                        pool.indirect_dma_start(vc[:, n, :], None, io["cache_v"],
                                                bass.IndirectOffsetOnAxis(ap=now[:, 0, n:n + 1], axis=0)).then_inc(v_loaded[n], 16)

        @block.tensor
        def _(pe):
            def product(t, c, v):
                off, n = CHUNKS[c]
                pe.wait_ge(w_loaded[v], 16 * t + 16)
                if c == 1:
                    pe.wait_ge(copied, after(6 * t + v + 1))
                elif not isinstance(t, int) or t > 0:
                    pe.wait_ge(copied, after(6 * t + (v - 3 if c == 0 else v - 1)))
                if c == 2 and v == 0 and not (isinstance(t, int) and t == 0):
                    pe.wait_ge(tails_out, after(2 * t - 2))
                for kk in range(KD):
                    last = pe.matmul(z_ps[c][v][:, 0:n], w[v][:, kk * P:(kk + 1) * P], keep["xT"][:, kk, off:off + n],
                                     start=(kk == 0), stop=(kk == KD - 1))
                last.then_inc(z_ok, 1)

            def scores(b):
                pe.wait_ge(bq_ok, after(b + 1))
                pe.wait_ge(qr_ok, after(b + 1))
                pe.wait_ge(exp_ok, after(b))
                pe.wait_ge(o_ok, after(8 * b))
                for n in range(PAGES):
                    pe.wait_ge(k_loaded[n], 16 * b + 16)
                for part, (off, n) in enumerate(CHUNKS):
                    out = ps[:, off:off + n]
                    pe.matmul(out, bias_q[:, :], bias_k[:, off:off + n], start=True, stop=False, skip_group_check=True)
                    if part == 2:
                        pe.matmul(out, keep["ident"][:, :], mask_new[:, bass.ds(b, 1), :], start=False, stop=False, skip_group_check=True)
                    for pair in range(4):
                        keys = kc[:, 4 * part:4 * part + 4, pair * P:(pair + 1) * P] if part < 2 else k_new[:, pair, :]
                        last = pe.matmul(ps[pair * 32:pair * 32 + 32, off:off + n], q_rows[:, pair, :], keys, start=False,
                                         stop=True, skip_group_check=True)
                last.then_inc(s_ps, 1)

            def turn(b):
                pe.wait_ge(diag_ok, after(b + 1))
                pe.wait_ge(t_ok, after(2 * b))
                for n in range(9):
                    width = P if n < 8 else NS
                    out = pt[:, n * P:(n + 1) * P] if n < 8 else pt_new[0:NS, :]
                    last = pe.matmul(out, p[:, n * P:n * P + width], diag[:, :], start=True, stop=True)
                last.then_inc(t_ps, 1)

            def values(b):
                pe.wait_ge(t_ok, after(2 * b + 2))
                for n in range(PAGES):
                    pe.wait_ge(v_loaded[n], 16 * b + 16)
                for pair in range(4):
                    for n in range(9):
                        width = P if n < 8 else NS
                        vals = vc[:, n, pair * P:(pair + 1) * P] if n < 8 else v_new[:, pair * P:(pair + 1) * P]
                        last = pe.matmul(po[:, pair * 32:pair * 32 + 16], vals, pT[0:width, n, pair * 32:pair * 32 + 16],
                                         start=(n == 0), stop=(n == 8))
                last.then_inc(pv, 1)

            def round_(i, more):
                def z(c, v):
                    if more:
                        product(i + 1, c, v)
                scores(2 * i)
                z(0, 0)
                turn(2 * i)
                z(0, 1)
                values(2 * i)
                z(1, 0)
                scores(2 * i + 1)
                z(1, 1)
                turn(2 * i + 1)
                z(2, 0)
                z(2, 1)
                values(2 * i + 1)
                pe.wait_ge(glu, after(4 * i + 4))
                pe.wait_ge(tails_out, after(2 * i))
                if more:
                    pe.wait_ge(copied, after(6 * i + 12))
                pe.transpose(tail_ps[0:HALO, 0:P], ext_p[:, SEQ:SEQ + HALO], keep["ident"][:, :])
                pe.transpose(tail_ps[0:NS, P:2 * P], glu_s[:, :], keep["ident"][:, :]).then_inc(tails, 1)

            for c in range(3):
                for v in range(2):
                    product(0, c, v)
            pe.wait_ge(consts, after(80))
            tiles(pe, round_)
            pe.wait_ge(halo0, after(2))
            pe.wait_ge(tap_done, after(62 * 4))
            pe.wait_ge(tails_out, after(8))
            for c, (off, n) in enumerate(CHUNKS):
                for i in range(4):
                    last = pe.matmul(ln_ps[c][:, 0:n], mean_w[:, :], y[:, i, off:off + n], start=(i == 0), stop=(i == 3))
                last.then_inc(mean, 1)
            for c, (off, n) in enumerate(CHUNKS):
                pe.wait_ge(squared, after(c + 1))
                for i in range(4):
                    last = pe.matmul(ln_ps[c][:, 0:n], mean_w[:, :], sq[:, i, 0:n], start=(i == 0), stop=(i == 3))
                last.then_inc(var, 1)

        @block.scalar
        def _(act):
            def copy(t, c, v):
                off, n = CHUNKS[c]
                act.wait_ge(z_ok, after(6 * t + (6 if c == 2 else 2 * c + v + 1)))
                act.wait_ge(glu, after(4 * t))
                act.activation((sig, val)[v][:, off:off + n], z_ps[c][v][:, 0:n], (ACT.Sigmoid, ACT.Copy)[v]).then_inc(copied, 1)

            def exps(b):
                act.wait_ge(max_ok, after(b + 1))
                act.wait_ge(t_ps, after(b))
                act.wait_ge(ri_ok, after(b))
                act.activation(p[:, :], ps[:, :], ACT.Exp, bias=nmax[:, 0:1], accum_out=rsum[:, 0:1]).then_inc(exp_ok, 1)

            def turned(b):
                act.wait_ge(t_ps, after(b + 1))
                act.wait_ge(pv, after(b))
                act.activation(pT[:, 0:8, :], pt[:, 0:1024].rearrange("p (n r) -> p n r", n=8), ACT.Copy).then_inc(t_ok, 1)
                act.activation(pT[0:NS, 8, :], pt_new[0:NS, :], ACT.Copy).then_inc(t_ok, 1)

            def round_(i, more):
                def cp(c, v):
                    if more:
                        copy(i + 1, c, v)
                exps(2 * i)
                cp(0, 0)
                turned(2 * i)
                cp(0, 1)
                cp(1, 0)
                exps(2 * i + 1)
                cp(1, 1)
                turned(2 * i + 1)
                cp(2, 0)
                cp(2, 1)
                act.wait_ge(tails, after(i + 1))
                act.activation(tail_p[:, rows(i)], tail_ps[0:HALO, 0:P], ACT.Copy).then_inc(tails_out, 1)
                act.activation(tail_s[:, rows(i)], tail_ps[0:NS, P:2 * P], ACT.Copy).then_inc(tails_out, 1)

            act.wait_ge(c_consts, after(96))
            for c in range(3):
                for v in range(2):
                    copy(0, c, v)
            tiles(act, round_)
            for c, (off, n) in enumerate(CHUNKS):
                act.wait_ge(centred, after(c + 1))
                if c:
                    act.wait_ge(var, after(c))
                act.activation(sq[:, :, 0:n], y[:, 0:4, off:off + n], ACT.Square).then_inc(squared, 1)
                act.wait_ge(var, after(c + 1))
                if c:
                    act.wait_ge(recip, after(c))
                act.activation(std[:, 0:n], ln_ps[c][:, 0:n], ACT.Sqrt, bias=keep["eps"][:, 0:1]).then_inc(stdev, 1)
                act.wait_ge(normed, after(c + 1))
                for i in range(4):
                    act.activation(y[:, i, off:off + n], y[:, i, off:off + n], ACT.Silu,
                                   scale=ln[:, 0, i:i + 1], bias=ln[:, 1, i:i + 1]).then_inc(swish, 1)

        @block.vector
        def _(dve):
            def window(i):
                dve.wait_ge(copied, after(6 * i + 6))
                dve.wait_ge(tap_done, after(62 * i))
                dve.wait_ge(tails, after(i))
                dve.tensor_tensor(ext_p[:, HALO:HALO + SEQ], val[:, 0:SEQ], sig[:, 0:SEQ], ALU.mult).then_inc(glu, 1)
                dve.tensor_tensor(glu_s[:, :], val[:, SEQ:T], sig[:, SEQ:T], ALU.mult).then_inc(glu, 1)
                dve.tensor_tensor(ext_s[:, :, HALO:EXT_S], val[:, SEQ:T].rearrange("p (b t) -> p b t", b=DB),
                                  sig[:, SEQ:T].rearrange("p (b t) -> p b t", b=DB), ALU.mult).then_inc(glu, 1)
                dve.tensor_copy(ext_s[:, :, 0:HALO].unsqueeze(1), halos[:, rows(i, 1), :, :]).then_inc(glu, 1)
                dve.tensor_copy(taps[:, :].unsqueeze(1), taps_all[:, rows(i, 1), :]).then_inc(taps_ready, 1)
                dve.wait_ge(taps_ready, after(i + 1))
                dve.wait_ge(glu, after(4 * i + 4))

            def taps_of(i, first, end):
                for j in range(first, end):
                    last_tap = j == CONV_K - 1
                    out_p = y[:, rows(i, 1), 0:SEQ] if last_tap else acc_p[:, :]
                    out_s = (y[:, rows(i, 1), SEQ:T].rearrange("p a (b t) -> p (a b) t", b=DB) if last_tap
                             else acc_s[:, :, :])
                    for s, (out, win, prev) in enumerate(((out_p, ext_p[:, j:j + SEQ], acc_p[:, :]),
                                                          (out_s, ext_s[:, :, j:j + DT], acc_s[:, :, :]))):
                        if j == 0:
                            ins = dve.tensor_scalar(out, win, taps[:, 0:1], taps[:, CONV_K:CONV_K + 1], ALU.mult, ALU.add)
                        else:
                            dve.wait_ge(tap_done, after(62 * i + 2 * (j - 1) + s + 1))
                            ins = dve.scalar_tensor_tensor(out, win, taps[:, j:j + 1], prev, ALU.mult, ALU.add)
                        ins.then_inc(tap_done, 1)

            def prepare(b):
                for n in range(PAGES):
                    dve.wait_ge(lf_loaded[n], 16 * b + 16)
                dve.wait_ge(s_ps, after(b))
                dve.tensor_tensor_scan(c_all[:, 0:W], ones[:, :], lfc[:, :], 0.0, ALU.mult, ALU.add).then_inc(c_ok, 1)
                dve.wait_ge(c_ok, after(b + 1))
                dve.tensor_scalar(c_all[:, W:W + NS], c_new[:, SEQ:T], c_all[:, W - 1:W], None, ALU.add).then_inc(cn_ok, 1)
                dve.wait_ge(cn_ok, after(b + 1))
                dve.tensor_scalar(bias_k[:, :], c_all[:, :], row_coef[:, 0:1], row_coef[:, 1:2], ALU.mult, ALU.add).then_inc(bk_ok, 1)
                dve.tensor_tensor(bias_q[:, :].rearrange("p (g t) -> p g t", t=DT),
                                  c_all[:, bass.ds(b * DT + W, DT)].unsqueeze(1).broadcast_to([64, 16, DT]),
                                  sel[:, 1, :].rearrange("p (g t) -> p g t", t=DT), ALU.mult).then_inc(bq0, 1)
                dve.wait_ge(bq0, after(b + 1))
                dve.tensor_tensor(bias_q[:, :], bias_q[:, :], sel[:, 0, :], ALU.add).then_inc(bq_ok, 1)
                dve.tensor_copy(q_rows[0:64, :, 0:DT], q_new[0:64, :, rows(b, DT)])
                dve.tensor_copy(q_rows[64:P, :, DT:2 * DT], q_new[64:P, :, rows(b, DT)]).then_inc(qr_ok, 1)

            def maximum(b):
                dve.wait_ge(s_ps, after(b + 1))
                dve.tensor_reduce(nmax[:, :], ps[:, :], AX.X, ALU.max, negate=True).then_inc(max_ok, 1)

            def normalise(b):
                dve.wait_ge(exp_ok, after(b + 1))
                dve.reciprocal(rinv[:, :], rsum[:, :]).then_inc(ri_ok, 1)
                dve.wait_ge(ri_ok, after(b + 1))
                dve.tensor_scalar(diag[:, :], keep["ident"][:, :], rinv[:, 0:1], None, ALU.mult).then_inc(diag_ok, 1)

            def output(b):
                dve.wait_ge(pv, after(b + 1))
                for pair in range(4):
                    for hh in range(2):
                        dve.tensor_copy(keep["branch"][hh * 64:hh * 64 + 64, 8 + pair, bass.ds(b * DT + SEQ, DT)],
                                        po[hh * 64:hh * 64 + 64, pair * 32 + hh * DT:pair * 32 + hh * DT + DT]).then_inc(o_ok, 1)

            def round_(i, more):
                window(i)
                taps_of(i, 0, 3)
                maximum(2 * i)
                taps_of(i, 3, 4)
                normalise(2 * i)
                taps_of(i, 4, 7)
                prepare(2 * i + 1)
                taps_of(i, 7, 13)
                output(2 * i)
                taps_of(i, 13, 20)
                maximum(2 * i + 1)
                taps_of(i, 20, 21)
                normalise(2 * i + 1)
                taps_of(i, 21, CONV_K)
                if more:
                    prepare(2 * i + 2)
                output(2 * i + 1)

            lk = Link(dve, idx_tmp)
            dve.wait_ge(consts, after(80))
            lk(dve.tensor_copy(pages_f[:, :], pages[:, :]))
            lk(dve.tensor_copy(lane_f[:, :], lane[:, :]))
            for s, size in enumerate((P, 8)):
                lk(dve.tensor_scalar(idx_f[:, s, :], pages_f[:, :], float(size), lane_f[:, s:s + 1], ALU.mult, ALU.add))
                dve.tensor_copy(idx[:, s, :], idx_f[:, s, :]).then_inc(idx_ok, 1)
            dve.wait_ge(pool_done, after(1))
            dve.wait_ge(halo0, after(2))
            dve.wait_ge(c_consts, after(96))
            prepare(0)
            tiles(dve, round_)
            for c, (off, n) in enumerate(CHUNKS):
                dve.wait_ge(mean, after(c + 1))
                dve.tensor_tensor(y[:, 0:4, off:off + n], y[:, 0:4, off:off + n],
                                  ln_ps[c][:, 0:n].unsqueeze(1).broadcast_to([P, 4, n]), ALU.subtract).then_inc(centred, 1)
            for c, (off, n) in enumerate(CHUNKS):
                dve.wait_ge(stdev, after(c + 1))
                dve.reciprocal(rstd[:, 0:n], std[:, 0:n]).then_inc(recip, 1)
                dve.wait_ge(recip, after(c + 1))
                dve.wait_ge(squared, after(c + 1))
                dve.tensor_tensor(y[:, 0:4, off:off + n], y[:, 0:4, off:off + n],
                                  rstd[:, 0:n].unsqueeze(1).broadcast_to([P, 4, n]), ALU.mult).then_inc(normed, 1)


def stage_merge(nc, io, keep):
    with ExitStack() as ctx:
        m = Place(nc, ctx, keep["psum"])
        w = [m.sb(f"m_w{u}", [P, 12 * P]) for u in range(3)]
        sig = m.sb("m_sig", [P, T])
        part = m.sb("m_part", [P, T])
        acc = m.sb("m_acc", [P, T])
        merged = m.sb("m_merged", [P, KD, T])
        w_out = m.sb("m_w_out", [P, KD, D])
        x_in = h = m.sb("m_x", [P, 2, D])
        proj = [m.bank(f"m_p{c}") for c in range(3)]
        gate = [m.bank(f"m_g{c}") for c in range(3)]
        ph = [proj[0], proj[1], gate[0], gate[1]]
        w_loaded = [m.sem(f"m_w{u}_loaded") for u in range(3)]
        p_z2 = [m.sem(f"m_p_z2_{n}") for n in range(3)]
        x_loaded = [m.sem(f"m_x_loaded{u}") for u in range(2)]
        stored = [m.sem(f"m_h_unloaded{u}") for u in range(2)]
        (wo_loaded, p_z, g_z, sg_ok, part_ok, acc_ok, z_ok, ph_ok, h_ok) = (
            m.sem("m_" + s) for s in "wo_loaded p_z g_z sg_ok part_ok acc_ok z_ok ph_ok h_ok".split())
        block = m.block()

        @block.sync
        def _(sp):
            with sp.Fori(0, KD) as i:
                for n in range(3):
                    sp.wait_ge(p_z2[n], after(i))
                    sp.dma_start(w[n][:, :], io["w_merge"][rows(3 * i + n), :]).then_inc(w_loaded[n], 16)
            sp.dma_start(w_out[:, :, :], io["w_out"]).then_inc(wo_loaded, 16)
            for t in range(NT):
                u = t % 2
                if t >= 2:
                    sp.wait_ge(stored[u], 16 * (t // 2))
                sp.dma_start(x_in[:, u, :], io["x_all"][t * P:(t + 1) * P, :]).then_inc(x_loaded[u], 16)

        @block.gpsimd
        def _(pool):
            for t in range(NT):
                pool.wait_ge(h_ok, after(t + 1))
                pool.dma_start(io["h_scratch"][t * P:(t + 1) * P, :], h[:, t % 2, :]).then_inc(stored[t % 2], 16)
            for u in range(2):
                pool.wait_ge(stored[u], 16 * ((NT + 1 - u) // 2))

        @block.tensor
        def _(pe):
            with pe.Fori(0, KD) as i:
                for n in range(3):
                    pe.wait_ge(w_loaded[n], 16 * i + 16)
                    for c, (off, width) in enumerate(CHUNKS):
                        pe.wait_ge(sg_ok, after(9 * i + 3 * n))
                        for kk in range(KD):
                            last = pe.matmul(gate[c][:, 0:width], w[n][:, (4 + kk) * P:(5 + kk) * P],
                                             keep["xT"][:, kk, off:off + width], start=(kk == 0), stop=(kk == KD - 1))
                        last.then_inc(g_z, 1)
                    for c, (off, width) in enumerate(CHUNKS):
                        pe.wait_ge(part_ok, after(9 * i + 3 * n))
                        for kk in range(4):
                            last = pe.matmul(proj[c][:, 0:width], w[n][:, kk * P:(kk + 1) * P],
                                             keep["branch"][:, 4 * n + kk, off:off + width], start=(kk == 0), stop=(kk == 3))
                        last.then_inc(p_z if c < 2 else p_z2[n], 1)
            pe.wait_ge(wo_loaded, 16)
            pe.wait_ge(acc_ok, after(2 * KD))
            for t in range(NT):
                n = P if t < 8 else NS
                if t >= 2:
                    pe.wait_ge(h_ok, after(t - 1))
                for hf in range(2):
                    for kk in range(KD):
                        last = pe.matmul(ph[2 * (t % 2) + hf][0:n, :], merged[:, kk, t * P:t * P + n], w_out[:, kk, hf * 512:(hf + 1) * 512],
                                         start=(kk == 0), stop=(kk == KD - 1))
                last.then_inc(ph_ok, 1)

        @block.scalar
        def _(act):
            with act.Fori(0, KD) as i:
                for n in range(3):
                    for c, (off, width) in enumerate(CHUNKS):
                        act.wait_ge(g_z, after(9 * i + 3 * n + c + 1))
                        act.wait_ge(part_ok, after(9 * i + 3 * n))
                        act.activation(sig[:, off:off + width], gate[c][:, 0:width], ACT.Sigmoid).then_inc(sg_ok, 1)

        @block.vector
        def _(dve):
            with dve.Fori(0, KD) as i:
                for n in range(3):
                    for c, (off, width) in enumerate(CHUNKS):
                        dve.wait_ge(sg_ok, after(9 * i + 3 * n + c + 1))
                        if c < 2:
                            dve.wait_ge(p_z, after(6 * i + 2 * n + c + 1))
                        else:
                            dve.wait_ge(p_z2[n], after(i + 1))
                        dve.wait_ge(acc_ok, after(2 * i + max(n - 1, 0)))
                        to = (acc if n == 0 else part)[:, off:off + width]
                        dve.tensor_tensor(to, proj[c][:, 0:width], sig[:, off:off + width], ALU.mult).then_inc(part_ok, 1)
                    dve.wait_ge(part_ok, after(9 * i + 3 * n + 3))
                    if n > 0:
                        to = acc[:, :].unsqueeze(1) if n == 1 else merged[:, bass.ds(i, 1), :]
                        dve.tensor_tensor(to, acc[:, :].unsqueeze(1), part[:, :].unsqueeze(1), ALU.add).then_inc(acc_ok, 1)
            for t in range(NT):
                n, u = (P if t < 8 else NS), t % 2
                dve.wait_ge(ph_ok, after(t + 1))
                dve.wait_ge(x_loaded[u], 16 * (t // 2) + 16)
                for hf in range(2):
                    last = dve.tensor_tensor(h[0:n, u, hf * 512:(hf + 1) * 512], ph[2 * u + hf][0:n, :],
                                             x_in[0:n, u, hf * 512:(hf + 1) * 512], ALU.add)
                last.then_inc(h_ok, 1)


GROUPS, SLOTS = 16, 8
HEADS, TOPK = 8, 16


def stage_peer(nc, io, keep):
    with ExitStack() as ctx:
        m = Place(nc, ctx, keep["psum"])
        wq, keysT = m.sb("p_wq", [P, KD, 2048]), m.sb("p_keysT", [P, 16, P])
        u_rows, v_rows = m.sb("p_u_rows", [P, SLOTS, D]), m.sb("p_v_rows", [P, SLOTS, D])
        h, xn = m.sb("p_h", [P, 2, D]), m.sb("p_xn", [P, 2, D])
        xnT, qT, s = m.sb("p_xnT", [P, KD, P]), m.sb("p_qT", [P, 16, P]), m.sb("p_s", [P, 16, P])
        cand = m.sb("p_cand", [P, HEADS, TOPK, TOPK])
        gain2, gain_f = m.sb("p_gain2", [P, D]), m.sb("p_gain_f", [P, D])
        diag = m.sb("p_diag", [P, SLOTS, P])
        sv, si = m.sb("p_sv", [P, 16, TOPK]), m.sb("p_si", [P, 16, TOPK], U32)
        si_f = m.sb("p_si_f", [P, 16, TOPK])
        top, pos, pos2 = m.sb("p_top", [P, HEADS, TOPK]), m.sb("p_pos", [P, HEADS, TOPK], U32), m.sb("p_pos2", [P, HEADS, TOPK], U32)
        pos_f, e_f = m.sb("p_pos_f", [P, HEADS, TOPK]), m.sb("p_e_f", [P, 2, HEADS, TOPK])
        w, idx = m.sb("p_w", [P, 2, HEADS * TOPK]), m.sb("p_idx", [P, 2, HEADS * TOPK], U32)
        wsum, iota = m.sb("p_wsum", [P, HEADS, 1]), m.sb("p_iota", [P, TOPK])
        hid, gl, act_w = m.sb("p_hid", [P, 2, SLOTS]), m.sb("p_gl", [P, 2, SLOTS]), m.sb("p_act_w", [P, 2, SLOTS])
        stat, stat_f = m.sb("p_stat", [P, 2]), m.sb("p_stat_f", [P, 2])
        zero = m.sb("p_zero", [P, P])
        acc = [m.bank(f"p_acc{u}", 2) for u in range(2)]
        pb = [m.bank(f"p_b{u}") for u in range(4)]
        u_loaded, v_loaded = ([m.sem(f"p_{x}_loaded{n}") for n in range(SLOTS)] for x in "uv")
        h_loaded = [m.sem(f"p_h_loaded{u}") for u in range(2)]
        stored = [m.sem(f"p_stored{u}") for u in range(2)]
        (consts, gate, zero_ok, u_free, v_free, gl_ok, act_ok, diag_ok, acc_ps, y_ok, ss_ok, sd_ok, rs_ok, xn_ok, xt_ps, xt_ok,
         q_ps, q_ok, s_ps, s_ok, link, idx_ok, wd_ok, we_ok, w_ok, fss, fsd, frs) = (
            m.sem("p_" + x) for x in (
                "consts gate zero_ok u_free v_free gl_ok act_ok diag_ok acc_ps y_ok ss_ok sd_ok rs_ok xn_ok xt_ps xt_ok q_ps q_ok "
                "s_ps s_ok link idx_ok wd_ok we_ok w_ok fss fsd frs").split())
        block = m.block()
        LINKS = 1 + 16 * 5 + 1 + 8 * 5 + 12
        EXPERTS = HEADS * TOPK

        def choose_act(act, t, u, step):
            if step == 0:
                act.wait_ge(h_loaded[u], 16 * (t // 2) + 16 if isinstance(t, int) else t * 8 + 16 - 8 * u)
                act.wait_ge(xn_ok, after(t))
                act.activation(cand[:, 0:4, :, :].rearrange("p a b c -> p (a b c)"), h[:, u, :], ACT.Square,
                               accum_out=stat[:, 0:1]).then_inc(ss_ok, 1)
                act.wait_ge(ss_ok, after(t + 1))
                act.activation(stat[:, 1:2], stat[:, 0:1], ACT.Sqrt, scale=1.0 / D, bias=keep["eps"][:, 0:1]).then_inc(sd_ok, 1)
            if step == 1:
                for b in range(2):
                    act.wait_ge(xt_ps, after(2 * t + b + 1))
                    act.activation(xnT[:, 4 * b:4 * b + 4, :], pb[b].rearrange("p (k n) -> p k n", k=4), ACT.Copy).then_inc(xt_ok, 1)
            if step in (2, 3):
                for b in range(2 * step - 4, 2 * step - 2):
                    act.wait_ge(q_ps, after(4 * t + b + 1))
                    act.activation(qT[:, 4 * b:4 * b + 4, :], pb[(b + 2) % 4].rearrange("p (k n) -> p k n", k=4), ACT.Copy).then_inc(q_ok, 1)
            if step == 4:
                act.wait_ge(idx_ok, after(t))
                for b in range(4):
                    act.wait_ge(s_ps, after(4 * t + b + 1))
                    act.activation(s[:, 4 * b:4 * b + 4, :], pb[b].rearrange("p (k n) -> p k n", k=4), ACT.Copy).then_inc(s_ok, 1)
            if step == 15:
                act.wait_ge(wd_ok, after(t + 1))
                act.activation(w[:, u, :], w[:, u, :], ACT.Exp).then_inc(we_ok, 1)

        def choose_pe(pe, t, u, step):
            if step == 1:
                pe.wait_ge(xn_ok, after(t + 1))
                pe.wait_ge(s_ok, after(4 * t))
                for b in range(2):
                    for k in range(4 * b, 4 * b + 4):
                        last = pe.transpose(pb[b][:, k % 4 * P:k % 4 * P + P], xn[:, u, k * P:(k + 1) * P], keep["ident"][:, :])
                    last.then_inc(xt_ps, 1)
            if step in (2, 3):
                pe.wait_ge(xt_ok, after(2 * t + 2))
                for b in range(2 * step - 4, 2 * step - 2):
                    for c in range(4 * b, 4 * b + 4):
                        for k in range(KD):
                            last = pe.matmul(pb[(b + 2) % 4][:, c % 4 * P:c % 4 * P + P], wq[:, k, c * P:(c + 1) * P], xnT[:, k, :],
                                             start=(k == 0), stop=(k == KD - 1))
                    last.then_inc(q_ps, 1)
            if step == 4:
                pe.wait_ge(q_ok, after(4 * t + 4))
                for b in range(4):
                    for c in range(4 * b, 4 * b + 4):
                        last = pe.matmul(pb[b][:, c % 4 * P:c % 4 * P + P], qT[:, c, :], keysT[:, c, :], start=True, stop=True)
                    last.then_inc(s_ps, 1)

        class Chooser:

            def __init__(self, dve, t, u):
                self.dve, self.t, self.u = dve, t, u
                self.lk = Link(dve, link)

            def top16(self, values, val, ind):
                dve, lk = self.dve, self.lk
                lk(dve.max(val[:, 0:8], values))
                lk(dve.max_index(ind[:, 0:8], val[:, 0:8], values))
                lk(dve.match_replace(values, val[:, 0:8], values, -3.0e38))
                lk(dve.max(val[:, 8:16], values))
                lk(dve.max_index(ind[:, 8:16], val[:, 8:16], values))

            def step(self, n):
                dve, t, u, lk = self.dve, self.t, self.u, self.lk
                if n == 1:
                    dve.sem_clear(link)
                    dve.sem_inc(link, 1)
                    dve.wait_ge(sd_ok, after(t + 1))
                    dve.reciprocal(stat[:, 1:2], stat[:, 1:2]).then_inc(rs_ok, 1)
                    dve.wait_ge(rs_ok, after(t + 1))
                    dve.scalar_tensor_tensor(xn[:, u, :], h[:, u, :], stat[:, 1:2], gain2[:, :], ALU.mult, ALU.mult).then_inc(xn_ok, 1)
                first = (0, 3, 6, 9, 12, 14, 16)
                if 5 <= n <= 10:
                    if n == 5:
                        dve.wait_ge(s_ok, after(4 * t + 4))
                        lk(dve.memset(sv[:, :, :], 0.0))
                    for c in range(first[n - 5], first[n - 4]):
                        self.top16(s[:, c, :], sv[:, c, :], si[:, c, :])
                if n == 10:
                    pairs = sv[:, :, :].rearrange("p (h s) k -> p h s k", s=2)
                    shape = [P, HEADS, TOPK, TOPK]
                    lk(dve.tensor_tensor(cand[:, :, :, :], pairs[:, :, 0, :].unsqueeze(3).broadcast_to(shape),
                                         pairs[:, :, 1, :].unsqueeze(2).broadcast_to(shape), ALU.add))
                if 11 <= n <= 13:
                    for hd in range(3 * (n - 11), min(3 * (n - 11) + 3, HEADS)):
                        self.top16(cand[:, hd, :, :].rearrange("p a b -> p (a b)"), top[:, hd, :], pos[:, hd, :])
                if n in (14, 15):
                    half = n - 14
                    shape = [P, HEADS, TOPK, TOPK]
                    if half == 0:
                        lk(dve.tensor_copy(si_f[:, :, :], si[:, :, :]))
                        lk(dve.tensor_scalar(pos2[:, :, :], pos[:, :, :], 4, None, ALU.logical_shift_right))
                    else:
                        lk(dve.tensor_scalar(pos2[:, :, :], pos[:, :, :], 15, None, ALU.bitwise_and))
                    lk(dve.tensor_copy(pos_f[:, :, :], pos2[:, :, :]))
                    lk(dve.tensor_tensor(cand[:, :, :, :], pos_f[:, :, :].unsqueeze(3).broadcast_to(shape),
                                         iota[:, :].unsqueeze(1).unsqueeze(1).broadcast_to(shape), ALU.is_equal))
                    of_half = si_f[:, :, :].rearrange("p (h s) k -> p h s k", s=2)[:, :, half, :]
                    lk(dve.tensor_tensor(cand[:, :, :, :], cand[:, :, :, :], of_half.unsqueeze(2).broadcast_to(shape), ALU.mult))
                    lk(dve.tensor_reduce(e_f[:, half, :, :], cand[:, :, :, :], AX.X, ALU.add))
                if n == 15:
                    lk(dve.scalar_tensor_tensor(e_f[:, 0, :, :], e_f[:, 0, :, :], float(P), e_f[:, 1, :, :], ALU.mult, ALU.add))
                    dve.tensor_copy(idx[:, u, :].rearrange("p (h k) -> p h k", h=HEADS), e_f[:, 0, :, :]).then_inc(idx_ok, 1)
                    wv = w[:, u, :].rearrange("p (h k) -> p h k", h=HEADS)
                    dve.tensor_tensor(wv, top[:, :, :], top[:, :, 0:1].broadcast_to([P, HEADS, TOPK]), ALU.subtract).then_inc(wd_ok, 1)
                    dve.wait_ge(we_ok, after(t + 1))
                    dve.tensor_reduce(wsum[:, :, :], wv, AX.X, ALU.add).then_inc(w_ok, 1)
                    dve.wait_ge(w_ok, after(3 * t + 1))
                    dve.reciprocal(wsum[:, :, :], wsum[:, :, :]).then_inc(w_ok, 1)
                    dve.wait_ge(w_ok, after(3 * t + 2))
                    dve.tensor_tensor(wv, wv, wsum[:, :, :].broadcast_to([P, HEADS, TOPK]), ALU.mult).then_inc(w_ok, 1)
                    assert self.lk.n == LINKS, self.lk.n

        def main_pool(pool, t, u, n):
            pool.wait_ge(idx_ok, after(t + 1))
            for g in range(GROUPS):
                for free, loaded, to, table in ((u_free, u_loaded, u_rows, "peer_u"), (v_free, v_loaded, v_rows, "peer_v")):
                    for k in range(SLOTS):
                        c = g * SLOTS + k
                        pool.wait_ge(free, after(EXPERTS * t + c + 1))
                        pool.sem_inc(gate, 1)
                        pool.indirect_dma_start(to[0:n, k, :], None, io[table],
                                                bass.IndirectOffsetOnAxis(ap=idx[0:n, u, c:c + 1], axis=0)).then_inc(loaded[k], 16)

        def main_pe(pe, t, u, n, choosing):
            pe.wait_ge(y_ok, after(t))
            for hf in range(2):
                pe.matmul(acc[u][0:n, hf * 512:(hf + 1) * 512], zero[0:n, 0:n], h[0:n, u, hf * 512:(hf + 1) * 512], start=True, stop=False,
                          skip_group_check=True)
            for g in range(GROUPS):
                for k in range(SLOTS):
                    c = g * SLOTS + k
                    pe.wait_ge(diag_ok, after(EXPERTS * t + c + 1))
                    pe.wait_ge(v_loaded[k], (t * GROUPS + g) * 16 + 16)
                    for hf in range(2):
                        last = pe.matmul(acc[u][0:n, hf * 512:(hf + 1) * 512], diag[0:n, k, 0:n], v_rows[0:n, k, hf * 512:(hf + 1) * 512],
                                         start=False, stop=False, skip_group_check=True)
                    last.then_inc(v_free, 1)
                if choosing:
                    choose_pe(pe, t + 1, 1 - u, g)
            for hf in range(2):
                last = pe.matmul(acc[u][0:n, hf * 512:(hf + 1) * 512], keep["ident"][0:n, 0:n], h[0:n, u, hf * 512:(hf + 1) * 512],
                                 start=False, stop=True, skip_group_check=True)
            last.then_inc(acc_ps, 1)

        def main_act(act, t, u, n, choosing):
            for g in range(GROUPS):
                gp = g % 2
                act.wait_ge(u_free, after(EXPERTS * t + (g + 2) * SLOTS))
                act.activation(gl[0:n, gp, :], hid[0:n, gp, :], ACT.Gelu).then_inc(gl_ok, 1)
                act.wait_ge(act_ok, after(GROUPS * t + g + 1))
                for k in range(SLOTS):
                    act.wait_ge(v_free, after(EXPERTS * t + g * SLOTS + k + 1))
                    act.activation(diag[0:n, k, 0:n], keep["ident"][0:n, 0:n], ACT.Copy, scale=act_w[0:n, gp, k:k + 1]).then_inc(diag_ok, 1)
                if choosing:
                    choose_act(act, t + 1, 1 - u, g)
            act.wait_ge(acc_ps, after(t + 1))
            act.activation(h[0:n, u, :], acc[u][0:n, :], ACT.Square, accum_out=stat_f[0:n, 0:1]).then_inc(fss, 1)
            act.wait_ge(fss, after(t + 1))
            act.activation(stat_f[0:n, 1:2], stat_f[0:n, 0:1], ACT.Sqrt, scale=1.0 / D, bias=keep["eps"][0:n, 0:1]).then_inc(fsd, 1)

        def main_dve(dve, t, u, n, choosing):
            chooser = Chooser(dve, t + 1, 1 - u) if choosing else None
            for g in range(GROUPS):
                gp = g % 2
                for k in range(SLOTS):
                    dve.wait_ge(u_loaded[k], (t * GROUPS + g) * 16 + 16)
                    last = dve.tensor_tensor_reduce(out=u_rows[0:n, k, :], in0=u_rows[0:n, k, :], in1=xn[0:n, u, :], scale=1.0, scalar=0.0,
                                                    op0=ALU.mult, op1=ALU.add, accum_out=hid[0:n, gp, k:k + 1])
                    last.then_inc(u_free, 1)
                dve.wait_ge(gl_ok, after(GROUPS * t + g + 1))
                dve.tensor_tensor(act_w[0:n, gp, :], gl[0:n, gp, :], w[0:n, u, g * SLOTS:(g + 1) * SLOTS], ALU.mult).then_inc(act_ok, 1)
                if chooser:
                    chooser.step(g)
            dve.wait_ge(fsd, after(t + 1))
            dve.reciprocal(stat_f[0:n, 1:2], stat_f[0:n, 1:2]).then_inc(frs, 1)
            dve.wait_ge(frs, after(t + 1))
            dve.scalar_tensor_tensor(h[0:n, u, :], acc[u][0:n, :], stat_f[0:n, 1:2], gain_f[0:n, :], ALU.mult, ALU.mult).then_inc(y_ok, 1)

        def tiles(eng, main):
            with eng.Fori(0, 4) as i:
                for u in range(2):
                    main(eng, 2 * i + u, u, P, True)
            main(eng, 8, 0, NS, False)

        @block.sync
        def _(sp):
            for dst, src in ((gain2, "norm2_g"), (gain_f, "final_g")):
                sp.dma_start(dst[:, :], io[src].partition_broadcast(P)).then_inc(consts, 16)
            sp.dma_start(h[:, 0, :], io["h_scratch"][0:P, :]).then_inc(h_loaded[0], 16)
            for dst, src in ((wq, "peer_wq"), (keysT, "peer_keysT"), (iota, "c_iota16")):
                sp.dma_start(dst[:], io[src]).then_inc(consts, 16)

            def tile(sp, t, u, n, more):
                if more:
                    if u == 0:
                        sp.wait_ge(stored[1], after(8 * t))
                    else:
                        sp.wait_ge(stored[0], after(8 * t + 8))
                    sp.dma_start(h[:, 1 - u, :], io["h_scratch"][rows(t + 1), :]).then_inc(h_loaded[1 - u], 16)
                sp.wait_ge(y_ok, after(t + 1))
                if more:
                    sp.dma_start(io["y_prompt"][0, rows(t), :], h[:, u, :]).then_inc(stored[u], 16)
                else:
                    sp.dma_start(io["y_sample"].rearrange("b t d -> (b t) d"), h[0:n, u, :]).then_inc(stored[u], 16)

            tiles(sp, tile)
            sp.wait_ge(stored[0], after(16 * 5))
            sp.wait_ge(stored[1], after(16 * 4))

        @block.gpsimd
        def _(pool):
            pool.memset(zero[:, :], 0.0).then_inc(zero_ok, 1)
            tiles(pool, lambda eng, t, u, n, more: main_pool(eng, t, u, n))

        @block.tensor
        def _(pe):
            pe.sem_inc(v_free, SLOTS)
            pe.wait_ge(consts, after(16 * 5))
            pe.wait_ge(zero_ok, after(1))
            for step in range(GROUPS):
                choose_pe(pe, 0, 0, step)
            tiles(pe, main_pe)

        @block.scalar
        def _(act):
            for step in range(GROUPS):
                choose_act(act, 0, 0, step)
            tiles(act, main_act)

        @block.vector
        def _(dve):
            dve.sem_inc(u_free, SLOTS)
            dve.wait_ge(consts, after(16 * 5))
            first = Chooser(dve, 0, 0)
            for step in range(GROUPS):
                first.step(step)
            tiles(dve, main_dve)


OUTPUTS = (
    ("y_prompt", (1, SEQ, D)), ("y_sample", (DB, DT, D)),
    ("new_k_prompt", (1, 1, SEQ, 8, 64)), ("new_v_prompt", (1, 1, SEQ, 8, 64)), ("new_logf_prompt", (1, 1, SEQ, 8)),
    ("new_conv_prompt", (1, 1, HALO, 512)), ("new_hgrn_prompt", (1, 1, 4, P, P)),
    ("new_k_sample", (1, DB, DT, 8, 64)), ("new_v_sample", (1, DB, DT, 8, 64)), ("new_logf_sample", (1, DB, DT, 8)),
    ("new_conv_sample", (1, DB, HALO, 512)), ("new_hgrn_sample", (1, DB, 4, P, P)),
)


def build(nc, io, stages):
    with ExitStack() as ctx:
        m = Place(nc, ctx)
        io["h_scratch"] = nc.dram_tensor("h_scratch", (TP, D), F32, kind="Internal").ap()
        keep = {"ident": m.sb("ident", [P, P]), "eps": m.sb("eps", [P, 1]),
                "psum": ctx.enter_context(nc.psum_tensor("psum", [P, 8 * 512], F32))}
        with ExitStack() as trunk_ctx:
            t = Place(nc, trunk_ctx)
            keep["xT"] = t.sb("xT", [P, KD, TP])
            keep["branch"] = t.sb("branch", [P, 12, T])
            keep["c_new"] = t.sb("c_new", [64, T])
            keep["q_new"], keep["k_new"] = t.sb("q_new", [P, 4, NS]), t.sb("k_new", [P, 4, NS])
            keep["v_new"] = t.sb("v_new", [NS, 512])
            for stage in stages[0]:
                stage(nc, io, keep)
        for stage in stages[1]:
            stage(nc, io, keep)


def laid_out(inputs):
    a = {k: np.asarray(v) for k, v in inputs.items()}
    w = a["w_in"][0].reshape(KD, P, -1).transpose(1, 0, 2)

    def tiles(starts, width=P):
        return np.concatenate([w[:, :, s:s + width].reshape(P, KD * width) for s in starts])

    out = {}
    out["x_all"] = np.concatenate([a["x_prompt"][0], a["x_sample"].reshape(NS, D), np.zeros((TP - T, D), np.float32)])
    out["w_conv"] = tiles([s + P * i for i in range(4) for s in (512, 0)])
    out["w_hgrn"] = tiles([s + P * h for h in range(4) for s in (1024, 1536, 2560, 2048)])
    out["w_fox"] = tiles([s + P * j for j in range(4) for s in (3072, 3584, 4096)])
    af = w[:, :, 4608:4616]
    zeros = np.zeros((P, KD, 24), np.float32)
    out["w_af"] = np.concatenate([af, zeros, af, zeros], 2).reshape(P, KD * 64)
    wb = a["w_branch"][0].reshape(3, 4, P, D).transpose(0, 2, 1, 3)
    out["w_merge"] = np.concatenate([
        np.concatenate([wb[n][:, :, P * i:P * (i + 1)], w[:, :, 4616 + D * n + P * i:4616 + D * n + P * (i + 1)]], 1)
        .reshape(P, 12 * P) for i in range(KD) for n in range(3)])
    out["w_out"] = a["w_out"][0].reshape(KD, P, D).transpose(1, 0, 2)
    out["norm1_g"], out["norm2_g"], out["final_g"] = a["norm1_g"][0], a["norm2_g"][0], a["final_g"]
    out["conv_taps"] = np.concatenate([a["conv_dw"][0], a["conv_db"]]).reshape(CONV_K + 1, 4, P).transpose(2, 1, 0)
    out["conv_ln"] = np.stack([a["conv_ln_g"][0], a["conv_ln_b"][0]]).reshape(2, 4, P).transpose(2, 0, 1)
    out["state_conv"] = a["state_conv"]
    out["state_convT"] = a["state_conv"][0].transpose(2, 0, 1)
    out["state_hgrn"] = a["state_hgrn"][0].transpose(1, 2, 0, 3).reshape(4 * P, DB, P)
    out["hg_lb"] = a["hg_lb_logits"][0].reshape(4, P).T
    out["hg_norm"] = a["hg_norm_g"][0].reshape(P, 1)
    fb = a["att_fb"][0]
    z24 = np.zeros(24, np.float32)
    out["att_fb"] = np.concatenate([fb, z24, fb, z24]).reshape(64, 1)
    out["cache_kT"] = a["cache_k"][0].reshape(PHYS, PAGE, 4, P).transpose(0, 3, 2, 1).reshape(PHYS * P, 4 * PAGE)
    out["cache_v"] = a["cache_v"][0].reshape(PHYS * PAGE, 512)
    out["cache_lfT"] = a["cache_logf"][0].transpose(0, 2, 1).reshape(PHYS * 8, PAGE)
    out["page_table"] = a["page_table"].reshape(DB * PAGES)
    out["peer_wq"] = a["peer_wq"][0].reshape(KD, P, 2048).transpose(1, 0, 2)
    out["peer_keysT"] = a["peer_keys"][0].reshape(16, P, P).transpose(2, 0, 1)
    out["peer_u"], out["peer_v"] = a["peer_u"][0], a["peer_v"][0]
    s, t = np.arange(P)[:, None], np.arange(P)[None, :]
    out["c_ident"] = np.eye(P, dtype=np.float32)
    out["c_eps"] = np.full((P, 1), EPS, np.float32)
    masks = [(s // (2 * h) == t // (2 * h)) & (s % (2 * h) < h) & (t % (2 * h) >= h) for h in LEVELS] + [s == t]
    out["c_levels"] = np.stack(masks, 1).astype(np.float32)
    reset = np.ones(T, np.float32)
    reset[0:SEQ:64] = 0
    reset[SEQ:T:DT] = 0
    out["c_reset"] = reset
    out["c_reset_c"] = np.ones(T, np.float32)
    out["c_reset_c"][0] = 0
    out["c_reset_c"][SEQ:T:DT] = 0
    out["c_batch"] = (np.arange(NS)[:, None] // DT == np.arange(DB)[None, :]).astype(np.float32)
    out["c_causal"] = np.where(t <= s, 0, NEG).astype(np.float32)
    lane = np.arange(64)
    out["c_rows"] = np.stack([np.where(lane < 8, -1, 0), np.where((lane >= 32) & (lane < 40), 1, 0)], 1).astype(np.float32)
    out["c_heads"] = np.stack([lane[:, None] == np.arange(8)[None], lane[:, None] - 32 == np.arange(8)[None]], 1).astype(np.float32)
    col = np.arange(P)
    head, used, tok = 2 * (col // 32) + (col % 32) // 8, col % 32 < 16, col % 8
    sel = (lane[:, None] == head[None]) & used[None]
    selq = (lane[:, None] - 32 == head[None]) & used[None]
    out["c_sel"] = np.stack([sel, selq], 1).astype(np.float32)
    key = np.arange(NS)
    allowed = (key[None, None] // DT == np.arange(DB)[None, :, None]) & (key[None, None] % DT <= tok[:, None, None])
    out["c_new"] = np.where(allowed, 0, NEG).astype(np.float32)
    out["c_lane"] = np.stack([np.arange(P), np.arange(P) % 8], 1).astype(np.int32)
    out["c_iota16"] = np.broadcast_to(np.arange(16, dtype=np.float32), (P, 16))
    return {k: np.ascontiguousarray(v) for k, v in out.items()}


STAGES = ((stage_norm, stage_hgrn, stage_fox, stage_conv_sample, stage_merge), (stage_peer,))


def kernel(**inputs):
    import concourse.bacc as bacc
    from concourse.bass_utils import run_bass_kernel_spmd

    nc = bacc.Bacc("TRN2", target_bir_lowering=False, num_devices=1)
    arrays = laid_out(inputs)
    io = {k: nc.dram_tensor("in_" + k, v.shape, mybir.dt.from_np(v.dtype), kind="ExternalInput").ap() for k, v in arrays.items()}
    for name, shape in OUTPUTS:
        io[name] = nc.dram_tensor("out_" + name, shape, F32, kind="ExternalOutput").ap()
    build(nc, io, STAGES)
    got = run_bass_kernel_spmd(nc, [{"in_" + k: v for k, v in arrays.items()}], core_ids=[0]).results[0]
    return tuple(got["out_" + name] for name, _ in OUTPUTS)
```

```python
from contextlib import ExitStack

import numpy as np

import concourse.bass as bass
from concourse import mybir

F32, I32, U32 = mybir.dt.float32, mybir.dt.int32, mybir.dt.uint32
ALU, ACT, AX = mybir.AluOpType, mybir.ActivationFunctionType, mybir.AxisListType

P = 128
D = 1024
KD = D // P
SEQ, DB, DT = 1024, 8, 8
NS = DB * DT
T = SEQ + NS
NT = 9
TP = NT * P
EPS = 1e-6
CHUNKS = ((0, 512), (512, 512), (1024, NS))
THIRDS = ((0, 364), (364, 364), (728, 360))
CONV_K, HALO = 31, 30
EXT_S = HALO + DT
PAGES, PAGE, PHYS = 8, 128, 80
LEVELS = (32, 16, 8, 4, 2, 1)
NEG = -1e30


def rows(i, n=P):
    return bass.ds(i * n, n)


def after(n):
    return n + 1


class Link:

    def __init__(self, eng, sem, base=0):
        self.eng, self.sem, self.base, self.n = eng, sem, base, 0

    def __call__(self, ins):
        self.n += 1
        ins.then_inc(self.sem, 1)
        self.eng.wait_ge(self.sem, after(self.base + self.n))


class Place:

    def __init__(self, nc, ctx, psum=None):
        self.nc, self.ctx, self.psum, self.banks, self.sems, self.start = nc, ctx, psum, 0, [], []
        ctx.callback(self.clear)

    def sb(self, name, shape, dt=F32):
        return self.ctx.enter_context(self.nc.sbuf_tensor(name, shape, dt))

    def bank(self, name, banks=1):
        self.banks += banks
        return self.psum[:, 512 * (self.banks - banks):512 * self.banks]

    def sem(self, name):
        self.sems.append(self.nc.alloc_semaphore(name))
        if "loaded" not in name:
            self.start.append(self.sems[-1])
        return self.sems[-1]

    def clear(self):
        if self.sems:
            self.nc.clear_and_free_semaphores(self.sems)
            self.nc.all_engine_barrier()

    def block(self):
        nc = self.nc
        engines = (nc.sync, nc.gpsimd, nc.scalar, nc.vector, nc.tensor)
        for n, sem in enumerate(self.start):
            engines[n % len(engines)].sem_inc(sem, 1)
        nc.all_engine_barrier()
        return self.ctx.enter_context(nc.Block())


def project(pe, weights, xT, banks, ready, chunks=CHUNKS):
    for c, (off, n) in enumerate(chunks):
        for k in range(KD):
            last = pe.matmul(banks[c][:, 0:n], weights[:, k * P:(k + 1) * P], xT[:, k, off:off + n],
                             start=(k == 0), stop=(k == KD - 1))
        last.then_inc(ready, 1)


def stage_norm(nc, io, keep):
    with ExitStack() as ctx:
        m = Place(nc, ctx, keep["psum"])
        x_in, xs = m.sb("n_x", [P, NT, D]), m.sb("n_xs", [P, 3, D])
        junk, gain = m.sb("n_junk", [P, 2, D]), m.sb("n_gain", [P, D])
        ss, rstd = m.sb("n_ss", [P, NT]), m.sb("n_rstd", [P, NT])
        pt = [m.bank(f"n_pt{u}", 2) for u in range(4)]
        x_loaded = [m.sem(f"n_x_loaded{t}") for t in range(NT)]
        consts, sumsq, std, recip, scaled, turned, stored = (
            m.sem("n_" + s) for s in ("consts", "sumsq", "std", "recip", "scaled", "turned", "stored"))
        block = m.block()

        @block.sync
        def _(sp):
            for t in range(NT):
                sp.dma_start(x_in[:, t, :], io["x_all"][t * P:(t + 1) * P, :]).then_inc(x_loaded[t], 16)
                if t == 0:
                    sp.dma_start(gain[:, :], io["norm1_g"].partition_broadcast(P)).then_inc(consts, 16)
                    sp.dma_start(keep["ident"][:, :], io["c_ident"]).then_inc(consts, 16)
                    sp.dma_start(keep["eps"][:, :], io["c_eps"]).then_inc(consts, 16)

        @block.scalar
        def _(act):
            for t in range(NT):
                act.wait_ge(x_loaded[t], 16)
                if t >= 2:
                    act.wait_ge(sumsq, after(t - 1))
                act.activation(junk[:, t % 2, :], x_in[:, t, :], ACT.Square, accum_out=ss[:, t:t + 1]).then_inc(sumsq, 1)
            act.wait_ge(consts, after(48))
            act.wait_ge(sumsq, after(NT))
            act.activation(rstd[:, :], ss[:, :], ACT.Sqrt, scale=1.0 / D, bias=keep["eps"][:, 0:1]).then_inc(std, 1)
            for t in range(NT):
                act.wait_ge(turned, after(t + 1))
                act.activation(keep["xT"][:, :, t * P:(t + 1) * P], pt[t % 4][:, :].rearrange("p (k t) -> p k t", k=KD), ACT.Copy).then_inc(stored, 1)

        @block.vector
        def _(dve):
            dve.wait_ge(std, after(1))
            dve.reciprocal(rstd[:, :], rstd[:, :]).then_inc(recip, 1)
            dve.wait_ge(recip, after(1))
            for t in range(NT):
                if t >= 3:
                    dve.wait_ge(turned, after(t - 2))
                dve.scalar_tensor_tensor(xs[:, t % 3, :], x_in[:, t, :], rstd[:, t:t + 1], gain[:, :], ALU.mult, ALU.mult).then_inc(scaled, 1)

        @block.tensor
        def _(pe):
            pe.wait_ge(consts, after(48))
            for t in range(NT):
                pe.wait_ge(scaled, after(t + 1))
                if t >= 4:
                    pe.wait_ge(stored, after(t - 3))
                for k in range(KD):
                    last = pe.transpose(pt[t % 4][:, k * P:(k + 1) * P], xs[:, t % 3, k * P:(k + 1) * P], keep["ident"][:, :])
                last.then_inc(turned, 1)


def stage_hgrn(nc, io, keep):
    with ExitStack() as ctx:
        m = Place(nc, ctx, keep["psum"])
        w = [m.sb(f"h_w{u}", [P, KD * P]) for u in range(2)]
        q, k, b = m.sb("h_q", [P, T]), m.sb("h_k", [P, T]), m.sb("h_b", [P, T])
        f, gate, lf = m.sb("h_f", [P, T]), m.sb("h_gate", [P, T]), m.sb("h_lf", [P, T])
        v = m.sb("h_v", [P, NT, P])
        reset = m.sb("h_reset", [P, T])
        decay, qe, ke = m.sb("h_decay", [P, T]), m.sb("h_qe", [P, T]), m.sb("h_ke", [P, T])
        qk = m.sb("h_qk", [P, len(LEVELS), T])
        masks = m.sb("h_masks", [P, 7, P])
        picked = m.sb("h_picked", [P, 7, P])
        at = [m.sb(f"h_at{u}", [P, P]) for u in range(2)]
        keT = m.sb("h_keT", [P, 2, P])
        state = m.sb("h_state", [P, 4, P])
        s_old, s_new, v_batch = m.sb("h_s_old", [P, DB, P]), m.sb("h_s_new", [P, DB, P]), m.sb("h_v_batch", [NS, DB, P])
        batch = m.sb("h_batch", [NS, DB])
        o, sq, std = m.sb("h_o", [P, T]), lf, f
        mean_w, lb, gain = m.sb("h_mean_w", [P, P]), m.sb("h_lb", [P, 8, 4]), m.sb("h_gain", [P, 1])
        pz = [m.bank(f"h_z{c}") for c in range(6)]
        pa6 = m.bank("h_a6", 2)
        pa = [pa6, m.psum[:, 0:1024]]
        p_turn, p_o, p_ds = pz[2], pz[3], pz[4:6]
        w_loaded = [m.sem(f"h_w{u}_loaded") for u in range(2)]
        (consts, pool_done, s_loaded, q_z, f_z, g_z, v_z, q_ok, f_ok, g_ok, v_ok, k_ok, fm_ok, lf_ok, b_ok, eb_ok, kd_sub, kd_exp,
         ke_ok, qe_ok, lv_sub, lv_exp, qk_ok, a_ok, at_ok, turn, turned, ds, st_ok, o_ps, o_ok, vb_ok, sq_ok, ms, sd_ok,
         rs_ok, y_ok, out_ok, link, tmp_ok, pick_ok, dss, s0_used) = (
            m.sem("h_" + s) for s in (
                "consts pool s_loaded q_z f_z g_z v_z q_ok f_ok g_ok v_ok k_ok fm_ok lf_ok b_ok eb_ok kd_sub kd_exp ke_ok qe_ok "
                "lv_sub lv_exp qk_ok a_ok at_ok turn turned ds st_ok o_ps o_ok vb_ok sq_ok ms sd_ok rs_ok y_ok out link tmp "
                "pick_ok dss s0_used").split())
        NL = len(LEVELS)
        block = m.block()

        def halves(x, level):
            h = LEVELS[level]
            end = T if 2 * h <= DT else SEQ
            v4 = x[:, 0:end].rearrange("p (n s h) -> p n s h", s=2, h=h)
            return v4[:, :, 0, :], v4[:, :, 1, :], v4[:, :, 0, h - 1:h].broadcast_to([P, end // (2 * h), h])

        @block.sync
        def _(sp):
            sp.dma_start(reset[:, :], io["c_reset"].partition_broadcast(P)).then_inc(consts, 16)
            sp.dma_start(masks[:, :, :], io["c_levels"]).then_inc(consts, 16)
            sp.dma_start(batch[:, :], io["c_batch"]).then_inc(consts, 16)
            sp.dma_start(lb[:, 0, :], io["hg_lb"]).then_inc(consts, 16)
            sp.dma_start(gain[:, :], io["hg_norm"]).then_inc(consts, 16)
            with sp.Fori(0, 4) as i:
                for n, u, used, count in ((1, 1, v_z, 3 * i), (0, 0, g_z, 3 * i), (3, 1, f_z, 3 * i + 3), (2, 0, q_z, 3 * i + 3)):
                    sp.wait_ge(used, after(count))
                    sp.dma_start(w[u][:, :], io["w_hgrn"][rows(4 * i + n), :]).then_inc(w_loaded[u], 16)
                sp.wait_ge(dss, after(i))
                sp.dma_start(s_old[:, :, :], io["state_hgrn"][rows(i), :, :]).then_inc(s_loaded, 16)
                sp.wait_ge(dss, after(i + 1))
                sp.dma_start(io["new_hgrn_sample"][0].rearrange("b h k v -> h k b v")[bass.ds(i, 1)].rearrange("a k b v -> (a k) b v"), s_new[:, :, :]).then_inc(out_ok, 16)
                sp.dma_start(io["new_hgrn_prompt"][0, 0][bass.ds(i, 1)].rearrange("a k v -> (a k) v"), state[:, 0, :]).then_inc(out_ok, 16)
            sp.wait_ge(out_ok, after(16 * 8))

        @block.gpsimd
        def _(pool):
            pool.memset(mean_w[:, :], 1.0 / P).then_inc(pool_done, 1)

        @block.tensor
        def _(pe):
            pe.wait_ge(pool_done, after(1))
            with pe.Fori(0, 4) as i:
                pe.wait_ge(w_loaded[1], 32 * i + 16)
                pe.wait_ge(o_ok, after(NT * i))
                pe.wait_ge(dss, after(i))
                project(pe, w[1], keep["xT"], pz[3:6], f_z, THIRDS)
                pe.wait_ge(w_loaded[0], 32 * i + 16)
                pe.wait_ge(sd_ok, after(i))
                project(pe, w[0], keep["xT"], pz[0:3], q_z, THIRDS)
                pe.wait_ge(w_loaded[1], 32 * i + 32)
                pe.wait_ge(f_ok, after(3 * i + 3))
                for t in range(NT):
                    for kk in range(KD):
                        last = pe.matmul(pz[3 + t // 4][:, t % 4 * P:(t % 4 + 1) * P], keep["xT"][:, kk, t * P:(t + 1) * P],
                                         w[1][:, kk * P:(kk + 1) * P], start=(kk == 0), stop=(kk == KD - 1))
                    if t % 4 == 3 or t == NT - 1:
                        last.then_inc(v_z, 1)
                pe.wait_ge(w_loaded[0], 32 * i + 32)
                pe.wait_ge(q_ok, after(3 * i + 3))
                project(pe, w[0], keep["xT"], pz[0:3], g_z, THIRDS)

                def scores(t):
                    n = P if t < NT - 1 else NS
                    cols = slice(t * P, t * P + n)
                    if t == 0:
                        pe.wait_ge(qk_ok, after(NL * i + NL))
                        pe.wait_ge(ke_ok, after(i + 1))
                        pe.wait_ge(g_ok, after(3 * i + 3))
                    pe.wait_ge(turned, after(NT * i + t))
                    if t >= 2:
                        pe.wait_ge(at_ok, after(NT * i + t - 1))
                    first = 0 if t < NT - 1 else 3
                    for lv in range(first, NL + 1):
                        a, bb = (qk[:, lv, cols], qk[:, lv, cols]) if lv < NL else (k[:, cols], q[:, cols])
                        last = pe.matmul(pa[t % 2][0:n, lv * P:lv * P + n], a, bb, start=True, stop=True)
                    last.then_inc(a_ok, 1)
                    pe.transpose(p_turn[0:n, 0:P], ke[:, cols], keep["ident"][:, :]).then_inc(turn, 1)

                scores(0)
                pe.wait_ge(v_ok, after(3 * i + 3))
                for t in range(NT):
                    n = P if t < NT - 1 else NS
                    if t < NT - 1:
                        scores(t + 1)
                        pe.wait_ge(turned, after(NT * i + t + 1))
                        pe.wait_ge(st_ok, after(17 * i + 2 * t + 1))
                        for c in range(2):
                            pe.matmul(p_ds[c][:, 0:P], keT[c * 64:c * 64 + 64, t % 2, :], v[c * 64:c * 64 + 64, t, :],
                                      start=True, stop=True).then_inc(ds, 1)
                        pe.wait_ge(at_ok, after(NT * i + t + 1))
                        pe.wait_ge(o_ok, after(NT * i + t))
                        pe.wait_ge(qe_ok, after(i + 1))
                        pe.matmul(p_o[:, 0:P], v[:, t, :], at[t % 2][:, :], start=True, stop=False, skip_group_check=True)
                        for c in range(2):
                            pe.wait_ge(st_ok, after(17 * i + 2 * t + c + 1))
                            pe.matmul(p_o[:, c * 64:c * 64 + 64], state[:, (2 * t + c) % 4, :], qe[:, t * P + c * 64:t * P + c * 64 + 64],
                                      start=False, stop=(c == 1), skip_group_check=True).then_inc((s0_used, o_ps)[c], 1)
                    else:
                        pe.wait_ge(at_ok, after(NT * i + t + 1))
                        pe.wait_ge(o_ok, after(NT * i + t))
                        pe.matmul(p_o[:, 0:n], v[0:n, t, :], at[t % 2][0:n, 0:n], start=True, stop=False, skip_group_check=True)
                        pe.wait_ge(s_loaded, 16 * i + 16)
                        for bt in range(DB):
                            last = pe.matmul(p_o[:, bt * DT:(bt + 1) * DT], s_old[:, bt, :], qe[:, SEQ + bt * DT:SEQ + (bt + 1) * DT],
                                             start=False, stop=(bt == DB - 1), skip_group_check=True)
                        last.then_inc(o_ps, 1)
                        pe.wait_ge(turned, after(NT * i + t + 1))
                        pe.wait_ge(vb_ok, after(i + 1))
                        pe.wait_ge(st_ok, after(17 * i + 17))
                        for hf in range(2):
                            last = pe.matmul(pz[4 + hf][:, :], keT[0:n, t % 2, :], v_batch[:, 4 * hf:4 * hf + 4, :], start=True, stop=True)
                        last.then_inc(ds, 1)
                pe.wait_ge(sq_ok, after(i + 1))
                for c, (off, n) in enumerate(THIRDS):
                    last = pe.matmul(pz[c][:, 0:n], mean_w[:, :], sq[:, off:off + n], start=True, stop=True)
                last.then_inc(ms, 1)

        @block.scalar
        def _(act):
            act.wait_ge(consts, after(80))
            with act.Fori(0, 4) as i:
                act.wait_ge(y_ok, after(i))
                for c, (off, n) in enumerate(THIRDS):
                    act.wait_ge(f_z, after(3 * i + c + 1))
                    act.activation(f[:, off:off + n], pz[3 + c][:, 0:n], ACT.Sigmoid).then_inc(f_ok, 1)
                act.wait_ge(fm_ok, after(i + 1))
                act.activation(lf[:, :], lf[:, :], ACT.Ln).then_inc(lf_ok, 1)
                for c, (off, n) in enumerate(THIRDS):
                    act.wait_ge(q_z, after(3 * i + c + 1))
                    act.activation(q[:, off:off + n], pz[c][:, 0:n], ACT.Silu).then_inc(q_ok, 1)
                act.wait_ge(b_ok, after(i + 1))
                act.activation(decay[:, :], b[:, :], ACT.Exp).then_inc(eb_ok, 1)
                act.wait_ge(kd_sub, after(i + 1))
                act.activation(ke[:, :], ke[:, :], ACT.Exp).then_inc(kd_exp, 1)
                for lv in range(NL):
                    end = T if 2 * LEVELS[lv] <= DT else SEQ
                    act.wait_ge(lv_sub, after(NL * i + lv + 1))
                    act.activation(qk[:, lv, 0:end], qk[:, lv, 0:end], ACT.Exp).then_inc(lv_exp, 1)
                for c in range(3):
                    act.wait_ge(v_z, after(3 * i + c + 1))
                    if c < 2:
                        act.activation(v[:, 4 * c:4 * c + 4, :], pz[3 + c][:, :].rearrange("p (a n) -> p a n", a=4), ACT.Copy).then_inc(v_ok, 1)
                    else:
                        act.activation(v[:, 8, :], pz[5][:, 0:P], ACT.Copy).then_inc(v_ok, 1)
                for c, (off, n) in enumerate(THIRDS):
                    act.wait_ge(g_z, after(3 * i + c + 1))
                    act.activation(gate[:, off:off + n], pz[c][:, 0:n], ACT.Sigmoid).then_inc(g_ok, 1)
                for t in range(NT):
                    n = P if t < NT - 1 else NS
                    act.wait_ge(turn, after(NT * i + t + 1))
                    if t >= 2:
                        act.wait_ge(ds, after(17 * i + 2 * t - 2))
                    act.activation(keT[0:n, t % 2, :], p_turn[0:n, 0:P], ACT.Copy).then_inc(turned, 1)
                    act.wait_ge(o_ps, after(NT * i + t + 1))
                    act.activation(o[:, t * P:t * P + n], p_o[:, 0:n], ACT.Copy).then_inc(o_ok, 1)
                act.wait_ge(o_ok, after(NT * i + NT))
                act.activation(sq[:, :], o[:, :], ACT.Square).then_inc(sq_ok, 1)
                act.wait_ge(ms, after(i + 1))
                for c, (off, n) in enumerate(THIRDS):
                    last = act.activation(std[:, off:off + n], pz[c][:, 0:n], ACT.Sqrt, bias=keep["eps"][:, 0:1])
                last.then_inc(sd_ok, 1)

        @block.vector
        def _(dve):
            lk = Link(dve, link)
            dve.wait_ge(consts, after(80))
            lk(dve.tensor_tensor(lb[:, 1, :], lb[:, 0, :], lb[:, 0, :], ALU.max))
            lk(dve.tensor_tensor(lb[:, 2, :], lb[:, 0, :], lb[:, 1, :], ALU.subtract))
            lk(dve.tensor_scalar(lb[:, 3, :], lb[:, 2, :], 1.0, None, ALU.add))
            lk(dve.reciprocal(lb[:, 4, :], lb[:, 3, :]))
            lk(dve.tensor_tensor(lb[:, 4, :], lb[:, 3, :], lb[:, 4, :], ALU.mult))
            lk(dve.tensor_tensor(lb[:, 5, :], lb[:, 4, :], lb[:, 4, :], ALU.subtract))
            lk(dve.tensor_scalar(lb[:, 5, :], lb[:, 5, :], 0.0, 1.0, ALU.max, ALU.min))
            lk(dve.tensor_scalar(lb[:, 6, :], lb[:, 5, :], -1.0, 1.0, ALU.mult, ALU.add))
            dve.wait_ge(pool_done, after(1))
            with dve.Fori(0, 4) as i:
                dve.wait_ge(f_ok, after(3 * i + 3))
                dve.tensor_scalar(f[:, :], f[:, :], lb[:, 6, bass.ds(i, 1)], lb[:, 5, bass.ds(i, 1)], ALU.mult, ALU.add).then_inc(tmp_ok, 1)
                dve.wait_ge(tmp_ok, after(2 * i + 1))
                dve.tensor_scalar(lf[:, :], f[:, :], 1e-20, None, ALU.max).then_inc(fm_ok, 1)
                dve.tensor_scalar(k[:, :], f[:, :], -1.0, 1.0, ALU.mult, ALU.add).then_inc(k_ok, 1)
                dve.wait_ge(lf_ok, after(i + 1))
                dve.tensor_tensor_scan(b[:, :], reset[:, :], lf[:, :], 0.0, ALU.mult, ALU.add).then_inc(b_ok, 1)
                dve.wait_ge(b_ok, after(i + 1))
                bp, bs = b[:, 0:SEQ].rearrange("p (n c) -> p n c", c=64), b[:, SEQ:T].rearrange("p (n c) -> p n c", c=DT)
                kp, ks = ke[:, 0:SEQ].rearrange("p (n c) -> p n c", c=64), ke[:, SEQ:T].rearrange("p (n c) -> p n c", c=DT)
                dve.tensor_tensor(kp, bp[:, :, 63:64].broadcast_to([P, 16, 64]), bp, ALU.subtract)
                dve.tensor_tensor(ks, bs[:, :, DT - 1:DT].broadcast_to([P, DB, DT]), bs, ALU.subtract).then_inc(kd_sub, 1)
                for lv in range(NL):
                    bl, br, ref = halves(b, lv)
                    xl, xr, _ = halves(qk[:, lv, :], lv)
                    dve.tensor_tensor(xl, ref, bl, ALU.subtract)
                    dve.tensor_tensor(xr, br, ref, ALU.subtract).then_inc(lv_sub, 1)
                dve.wait_ge(eb_ok, after(i + 1))
                dve.wait_ge(q_ok, after(3 * i + 3))
                dve.tensor_tensor(qe[:, :], q[:, :], decay[:, :], ALU.mult).then_inc(qe_ok, 1)
                dve.wait_ge(kd_exp, after(i + 1))
                dve.wait_ge(k_ok, after(i + 1))
                dve.tensor_tensor(ke[:, :], ke[:, :], k[:, :], ALU.mult).then_inc(ke_ok, 1)
                for lv in range(NL):
                    kl, _, _ = halves(k, lv)
                    _, qr, _ = halves(q, lv)
                    xl, xr, _ = halves(qk[:, lv, :], lv)
                    dve.wait_ge(lv_exp, after(NL * i + lv + 1))
                    dve.tensor_tensor(xl, xl, kl, ALU.mult)
                    dve.tensor_tensor(xr, xr, qr, ALU.mult).then_inc(qk_ok, 1)
                dve.wait_ge(out_ok, after(32 * i))
                dve.memset(state[:, 0, :], 0.0).then_inc(st_ok, 1)

                def pick(t):
                    n = P if t < NT - 1 else NS
                    dve.wait_ge(a_ok, after(NT * i + t + 1))
                    if t >= 2:
                        dve.wait_ge(o_ps, after(NT * i + t - 1))
                    first = 0 if t < NT - 1 else 3
                    products = pa[t % 2][0:n, 0:7 * P].rearrange("p (l t) -> p l t", l=7)[:, first:, 0:n]
                    dve.wait_ge(at_ok, after(NT * i + t))
                    dve.tensor_tensor(picked[0:n, first:, 0:n], products, masks[0:n, first:, 0:n], ALU.mult).then_inc(pick_ok, 1)
                    dve.wait_ge(pick_ok, after(NT * i + t + 1))
                    dve.tensor_reduce(at[t % 2][0:n, 0:n], picked[0:n, first:, 0:n].rearrange("p l t -> p t l"), AX.X, ALU.add).then_inc(at_ok, 1)

                pick(0)
                for t in range(NT):
                    if t < NT - 1:
                        for c in range(2):
                            dve.wait_ge(ds, after(17 * i + 2 * t + c + 1))
                            dve.wait_ge(st_ok, after(17 * i + 2 * t + c + 1))
                            if c == 0:
                                dve.wait_ge(o_ps, after(NT * i + max(t - 1, 0)))
                            else:
                                dve.wait_ge(s0_used, after(8 * i + t))
                            end = t * P + c * 64 + 63
                            dve.scalar_tensor_tensor(state[:, (2 * t + c + 1) % 4, :], state[:, (2 * t + c) % 4, :], decay[:, end:end + 1],
                                                     p_ds[c][:, 0:P], ALU.mult, ALU.add).then_inc(st_ok, 1)
                        pick(t + 1)
                    else:
                        dve.wait_ge(v_ok, after(3 * i + 3))
                        dve.tensor_tensor(v_batch[:, :, :], v[0:NS, t, :].unsqueeze(1).broadcast_to([NS, DB, P]),
                                          batch[:, :].unsqueeze(2).broadcast_to([NS, DB, P]), ALU.mult).then_inc(vb_ok, 1)
                        dve.wait_ge(s_loaded, 16 * i + 16)
                        ends = decay[:, SEQ:T].rearrange("p (n c) -> p n c", c=DT)[:, :, DT - 1:DT]
                        dve.tensor_tensor(s_new[:, :, :], s_old[:, :, :], ends.broadcast_to([P, DB, P]), ALU.mult).then_inc(tmp_ok, 1)
                        dve.wait_ge(tmp_ok, after(2 * i + 2))
                        dve.wait_ge(ds, after(17 * i + 17))
                        dve.wait_ge(o_ps, after(NT * i + NT))
                        for hf in range(2):
                            last = dve.tensor_tensor(s_new[:, 4 * hf:4 * hf + 4, :], s_new[:, 4 * hf:4 * hf + 4, :],
                                                     pz[4 + hf][:, :].rearrange("p (b v) -> p b v", b=4), ALU.add)
                        last.then_inc(dss, 1)
                dve.wait_ge(sd_ok, after(i + 1))
                dve.reciprocal(std[:, :], std[:, :]).then_inc(rs_ok, 1)
                dve.wait_ge(rs_ok, after(2 * i + 1))
                dve.scalar_tensor_tensor(o[:, :], o[:, :], gain[:, 0:1], std[:, :], ALU.mult, ALU.mult).then_inc(rs_ok, 1)
                dve.wait_ge(rs_ok, after(2 * i + 2))
                dve.tensor_tensor(keep["branch"][:, bass.ds(i + 4, 1), :], o[:, :], gate[:, :], ALU.mult).then_inc(y_ok, 1)


def stage_fox(nc, io, keep):
    with ExitStack() as ctx:
        m = Place(nc, ctx, keep["psum"])
        w = [m.sb(f"f_w{u}", [P, KD * P]) for u in range(3)]
        w_af = m.sb("f_w_af", [P, KD * P])
        q = [m.sb(f"f_q{u}", [P, SEQ]) for u in range(2)]
        kb = [m.sb(f"f_kb{u}", [P, T]) for u in range(2)]
        v, k_tok = m.sb("f_v", [P, NT, P]), m.sb("f_k_tok", [P, NT, P])
        a, lf, e1, reset = (m.sb("f_" + x, [P, T]) for x in ("a", "lf", "e1", "reset"))
        own, other = (slice(0, 64), slice(64, P)), (slice(64, P), slice(0, 64))
        lf_tok = m.sb("f_lf_tok", [P, NT, 8])
        row_coef, heads, fb = m.sb("f_rows", [P, 2]), m.sb("f_heads", [P, 2, 8]), m.sb("f_fb", [P, 1])
        causal = m.sb("f_causal", [P, P])
        p, pT = m.sb("f_p", [P, 2, SEQ]), m.sb("f_pT", [P, 2, SEQ])
        nmax, rsum, rinv, diag = m.sb("f_nmax", [P, 2]), m.sb("f_rsum", [P, 2]), m.sb("f_rinv", [P, 2]), m.sb("f_diag", [P, 2, P])
        ps = [m.bank(f"f_s{u}", 2) for u in range(2)]
        pt = [m.bank(f"f_t{u}") for u in range(2)]
        po = [m.bank(f"f_o{u}") for u in range(2)]
        pz = [ps[0][:, 0:512], ps[0][:, 512:1024], ps[1][:, 0:512], ps[1][:, 512:1024], pt[0], pt[1]]
        w_loaded = [m.sem(f"f_w{u}_loaded") for u in range(3)]
        (consts, af_loaded, af_z, a_ok, abs_ok, exp0_ok, ln_ok, lf_ok, c_ok, lft, lft_ok, bk_ok, q_z, k_z, v_z,
         q_ok, k_ok, v_ok, kt_ps, kt_ok, bq_ok, s_ps, max_ok, exp_ok, ri_ok, diag_ok, t0_ps, t1_ps, t0_ok, t1_ok, pv, o_ok, stored) = (
            m.sem("f_" + s) for s in (
                "consts af_loaded af_z a_ok abs_ok exp0_ok ln_ok lf_ok c_ok lft lft_ok bk_ok q_z k_z v_z q_ok k_ok v_ok kt_ps kt_ok "
                "bq_ok s_ps max_ok exp_ok ri_ok diag_ok t0_ps t1_ps t0_ok t1_ok pv o_ok stored").split())
        block = m.block()
        UNITS = [(qi, hh) for qi in range(8) for hh in range(2)]
        cs, qs_s, ks_s, vs_s = keep["c_new"], keep["q_new"], keep["k_new"], keep["v_new"]

        def tokens(name, width):
            return io[name + "_prompt"].rearrange(f"a b (t p) {width} -> p (a b t) ({width})", p=P)

        @block.sync
        def _(sp):
            sp.dma_start(w_af[:, :], io["w_af"]).then_inc(af_loaded, 16)
            for dst, src in ((row_coef, "c_rows"), (heads, "c_heads"), (fb, "att_fb"), (causal, "c_causal")):
                sp.dma_start(dst[:], io[src]).then_inc(consts, 16)
            sp.dma_start(reset[:, :], io["c_reset_c"].partition_broadcast(P)).then_inc(consts, 16)
            with sp.Fori(0, 4) as i:
                for u, used in enumerate((q_z, k_z, v_z)):
                    sp.wait_ge(used, after(3 * i))
                    sp.dma_start(w[u][:, :], io["w_fox"][rows(3 * i + u), :]).then_inc(w_loaded[u], 16)
                for src, ok, name in ((v, v_ok, "new_v"), (k_tok, kt_ok, "new_k")):
                    sp.wait_ge(ok, after(3 * i + 3))
                    sp.dma_start(tokens(name, "h d")[:, :, rows(i)], src[:, 0:8, :]).then_inc(stored, 16)
                    sp.dma_start(io[name + "_sample"].rearrange("a b t h d -> (a b t) (h d)")[:, rows(i)], src[0:NS, 8, :]).then_inc(stored, 16)
            sp.wait_ge(lft_ok, after(2))
            with nc.allow_non_contiguous_dma(reason="8 values per token"):
                sp.dma_start(tokens("new_logf", "h"), lf_tok[:, 0:8, :]).then_inc(stored, 16)
                sp.dma_start(io["new_logf_sample"].rearrange("a b t h -> (a b t) h"), lf_tok[0:NS, 8, :]).then_inc(stored, 16)
            sp.wait_ge(stored, after(16 * 18))

        @block.tensor
        def _(pe):
            pe.wait_ge(af_loaded, 16)
            for c, (off, n) in enumerate(CHUNKS):
                for kk in range(KD):
                    last = pe.matmul(pz[c][:, 0:n], w_af[:, kk * P:(kk + 1) * P], keep["xT"][:, kk, off:off + n],
                                     start=(kk == 0), stop=(kk == KD - 1))
                last.then_inc(af_z, 1)
            pe.wait_ge(lf_ok, after(1))
            for t in range(NT):
                n = P if t < 8 else NS
                last = pe.transpose(po[t // 8][0:n, t % 8 * 64:t % 8 * 64 + 64], lf[0:64, t * P:t * P + n], keep["ident"][0:64, 0:64])
            last.then_inc(lft, 1)

            def scores(i, n_unit):
                qi, hh = UNITS[n_unit]
                u = n_unit % 2
                if n_unit >= 2:
                    pe.wait_ge(exp_ok, after(16 * i + n_unit - 1))
                for part in range(qi // 4 + 1):
                    n = min(512, (qi + 1) * P - part * 512)
                    out, keys = ps[u][:, part * 512:part * 512 + n], slice(part * 512, part * 512 + n)
                    pe.matmul(out, q[hh][:, qi * P:(qi + 1) * P], kb[hh][:, keys], start=True, stop=(part < qi // 4),
                              skip_group_check=True)
                last = pe.matmul(ps[u][:, qi * P:(qi + 1) * P], keep["ident"][:, :], causal[:, :], start=False, stop=True,
                                 skip_group_check=True)
                last.then_inc(s_ps, 1)

            def turn(i, n_unit):
                qi, hh = UNITS[n_unit]
                u = n_unit % 2
                pe.wait_ge(diag_ok, after(16 * i + n_unit + 1))
                for part in range(qi // 4 + 1):
                    done = 16 * i + n_unit if part == 0 else 8 * i + n_unit - 8
                    pe.wait_ge((t0_ok, t1_ok)[part], after(done))
                    for kb in range(4 * part, min(4 * part + 4, qi + 1)):
                        last = pe.matmul(pt[part][:, kb % 4 * P:kb % 4 * P + P], p[:, u, kb * P:(kb + 1) * P], diag[:, u, :],
                                         start=True, stop=True)
                    last.then_inc((t0_ps, t1_ps)[part], 1)

            def values(i, n_unit):
                qi, hh = UNITS[n_unit]
                u = n_unit % 2
                pe.wait_ge(t0_ok, after(16 * i + n_unit + 1))
                if qi >= 4:
                    pe.wait_ge(t1_ok, after(8 * i + n_unit - 7))
                if hh == 0 and qi >= 2:
                    pe.wait_ge(o_ok, after(8 * i + qi - 1))
                for kb in range(qi + 1):
                    last = pe.matmul(po[qi % 2][hh * 64:(hh + 1) * 64, 0:P], v[:, kb, hh * 64:(hh + 1) * 64],
                                     pT[:, u, kb * P:(kb + 1) * P], start=(kb == 0), stop=(kb == qi))
                last.then_inc(pv, 1)

            with pe.Fori(0, 4) as i:
                pe.wait_ge(w_loaded[0], 16 * i + 16)
                pe.wait_ge(a_ok, after(3))
                pe.wait_ge(exp_ok, after(16 * i))
                project(pe, w[0], keep["xT"], pz[0:3], q_z)
                pe.wait_ge(w_loaded[1], 16 * i + 16)
                pe.wait_ge(t0_ok, after(16 * i))
                pe.wait_ge(t1_ok, after(8 * i))
                project(pe, w[1], keep["xT"], pz[3:6], k_z)
                pe.wait_ge(w_loaded[2], 16 * i + 16)
                pe.wait_ge(q_ok, after(3 * i + 3))
                for t in range(NT):
                    for kk in range(KD):
                        last = pe.matmul(pz[t // 4][:, t % 4 * P:(t % 4 + 1) * P], keep["xT"][:, kk, t * P:(t + 1) * P],
                                         w[2][:, kk * P:(kk + 1) * P], start=(kk == 0), stop=(kk == KD - 1))
                    if t % 4 == 3 or t == NT - 1:
                        last.then_inc(v_z, 1)
                pe.wait_ge(k_ok, after(3 * i + 3))
                for t in range(NT):
                    n = P if t < 8 else NS
                    for hh in range(2):
                        at = t % 4 * P + hh * 64
                        last = pe.matmul(pz[3 + t // 4][0:n, at:at + 64], kb[hh][:, t * P:t * P + n],
                                         keep["ident"][:, hh * 64:hh * 64 + 64], start=True, stop=True)
                    if t % 4 == 3 or t == NT - 1:
                        last.then_inc(kt_ps, 1)
                pe.wait_ge(v_ok, after(3 * i + 3))
                pe.wait_ge(kt_ok, after(3 * i + 3))
                pe.wait_ge(bq_ok, after(2 * i + 2))
                pe.wait_ge(lft_ok, after(2))
                pe.wait_ge(o_ok, after(8 * i))
                scores(i, 0)
                for n_unit in range(16):
                    if n_unit + 1 < 16:
                        scores(i, n_unit + 1)
                    if n_unit >= 1:
                        values(i, n_unit - 1)
                    turn(i, n_unit)
                values(i, 15)

        @block.scalar
        def _(act):
            act.wait_ge(consts, after(80))
            for c, (off, n) in enumerate(CHUNKS):
                act.wait_ge(af_z, after(c + 1))
                act.activation(a[:, off:off + n], pz[c][:, 0:n], ACT.Identity, bias=fb[:, 0:1]).then_inc(a_ok, 1)
            act.wait_ge(a_ok, after(3))
            act.activation(e1[:, :], a[:, :], ACT.Abs).then_inc(abs_ok, 1)
            act.wait_ge(abs_ok, after(1))
            act.activation(e1[:, :], e1[:, :], ACT.Exp, scale=-1.0).then_inc(exp0_ok, 1)
            act.wait_ge(exp0_ok, after(1))
            act.activation(e1[:, :], e1[:, :], ACT.Ln, bias=1.0).then_inc(ln_ok, 1)
            act.wait_ge(lft, after(1))
            act.activation(lf_tok[:, 0:8, :], po[0][:, :].rearrange("p (t h) -> p t h", t=8)[:, :, 0:8], ACT.Copy).then_inc(lft_ok, 1)
            act.activation(lf_tok[0:NS, 8, :], po[1][0:NS, 0:8], ACT.Copy).then_inc(lft_ok, 1)
            with act.Fori(0, 4) as i:
                for c, (off, n) in enumerate(CHUNKS):
                    act.wait_ge(q_z, after(3 * i + c + 1))
                    if c < 2:
                        act.activation(q[0][0:64, off:off + n], pz[c][0:64, 0:n], ACT.Copy, scale=0.125)
                        act.activation(q[1][64:P, off:off + n], pz[c][64:P, 0:n], ACT.Copy, scale=0.125).then_inc(q_ok, 1)
                    else:
                        act.activation(qs_s[:, bass.ds(i, 1), :], pz[c][:, 0:n], ACT.Copy, scale=0.125).then_inc(q_ok, 1)
                act.wait_ge(stored, after(64 * i))
                for c in range(3):
                    act.wait_ge(v_z, after(3 * i + c + 1))
                    if c < 2:
                        act.activation(v[:, 4 * c:4 * c + 4, :], pz[c][:, :].rearrange("p (a n) -> p a n", a=4), ACT.Copy).then_inc(v_ok, 1)
                    else:
                        act.activation(vs_s[:, rows(i)], pz[c][0:NS, 0:P], ACT.Copy)
                        act.activation(v[:, 8, :], pz[c][:, 0:P], ACT.Copy).then_inc(v_ok, 1)
                for n_unit, (qi, hh) in enumerate(UNITS):
                    u, n = n_unit % 2, (qi + 1) * P
                    act.wait_ge(max_ok, after(16 * i + n_unit + 1))
                    if n_unit >= 2:
                        act.wait_ge(t0_ok, after(16 * i + n_unit - 1))
                        if UNITS[n_unit - 2][0] >= 4:
                            act.wait_ge(t1_ok, after(8 * i + n_unit - 9))
                        act.wait_ge(ri_ok, after(16 * i + n_unit - 1))
                    act.activation(p[:, u, 0:n], ps[u][:, 0:n], ACT.Exp, bias=nmax[:, u:u + 1], accum_out=rsum[:, u:u + 1]).then_inc(exp_ok, 1)
                    if qi >= 4:
                        act.wait_ge(t1_ps, after(8 * i + n_unit - 7))
                        if n_unit >= 10:
                            act.wait_ge(pv, after(16 * i + n_unit - 1))
                        act.activation(pT[:, u, 512:n], pt[1][:, 0:n - 512], ACT.Copy).then_inc(t1_ok, 1)

        def out_tile(dve, i, qi):
            dve.wait_ge(pv, after(16 * i + 2 * qi + 2))
            dve.tensor_copy(keep["branch"][:, bass.ds(i + 8, 1), qi * P:(qi + 1) * P], po[qi % 2][:, 0:P].unsqueeze(1)).then_inc(o_ok, 1)

        @block.vector
        def _(dve):
            dve.wait_ge(consts, after(80))
            dve.wait_ge(ln_ok, after(1))
            dve.scalar_tensor_tensor(lf[:, :], a[:, :], 0.0, e1[:, :], ALU.min, ALU.subtract).then_inc(lf_ok, 1)
            dve.wait_ge(lf_ok, after(1))
            dve.tensor_tensor_scan(cs[:, :], reset[:, :], lf[:, :], 0.0, ALU.mult, ALU.add).then_inc(c_ok, 1)
            dve.wait_ge(c_ok, after(1))
            for hh in range(2):
                r = other[hh]
                dve.tensor_scalar(kb[hh][r, :], cs[r, :], row_coef[r, 0:1], row_coef[r, 1:2], ALU.mult, ALU.add).then_inc(bk_ok, 1)
            with dve.Fori(0, 4) as i:
                dve.wait_ge(pv, after(16 * i))
                for hh in range(2):
                    r = other[hh]
                    dve.tensor_scalar(q[hh][r, :], cs[r, 0:SEQ], heads[r, 1, bass.ds(2 * i + hh, 1)],
                                      heads[r, 0, bass.ds(2 * i + hh, 1)], ALU.mult, ALU.add).then_inc(bq_ok, 1)
                for c, (off, n) in enumerate(CHUNKS):
                    dve.wait_ge(k_z, after(3 * i + c + 1))
                    if c == 2:
                        dve.tensor_copy(ks_s[:, bass.ds(i, 1), :], pz[3 + c][:, 0:n].unsqueeze(1))
                    dve.tensor_copy(kb[0][own[0], off:off + n], pz[3 + c][own[0], 0:n])
                    dve.tensor_copy(kb[1][own[1], off:off + n], pz[3 + c][own[1], 0:n]).then_inc(k_ok, 1)
                dve.wait_ge(stored, after(64 * i))
                for c in range(3):
                    dve.wait_ge(kt_ps, after(3 * i + c + 1))
                    if c < 2:
                        dve.tensor_copy(k_tok[:, 4 * c:4 * c + 4, :], pz[3 + c][:, :].rearrange("p (a n) -> p a n", a=4)).then_inc(kt_ok, 1)
                    else:
                        dve.tensor_copy(k_tok[0:NS, 8, :], pz[5][0:NS, 0:P]).then_inc(kt_ok, 1)

                def soft(n_unit):
                    qi, hh = UNITS[n_unit]
                    u, n = n_unit % 2, (qi + 1) * P
                    dve.wait_ge(s_ps, after(16 * i + n_unit + 1))
                    dve.tensor_reduce(nmax[:, u:u + 1], ps[u][:, 0:n], AX.X, ALU.max, negate=True).then_inc(max_ok, 1)

                soft(0)
                for n_unit, (qi, hh) in enumerate(UNITS):
                    u, n = n_unit % 2, (qi + 1) * P
                    dve.wait_ge(exp_ok, after(16 * i + n_unit + 1))
                    dve.reciprocal(rinv[:, u:u + 1], rsum[:, u:u + 1]).then_inc(ri_ok, 1)
                    dve.wait_ge(ri_ok, after(16 * i + n_unit + 1))
                    dve.tensor_scalar(diag[:, u, :], keep["ident"][:, :], rinv[:, u:u + 1], None, ALU.mult).then_inc(diag_ok, 1)
                    if n_unit + 1 < 16:
                        soft(n_unit + 1)
                    dve.wait_ge(t0_ps, after(16 * i + n_unit + 1))
                    if n_unit >= 2:
                        dve.wait_ge(pv, after(16 * i + n_unit - 1))
                    dve.tensor_copy(pT[:, u, 0:min(n, 512)], pt[0][:, 0:min(n, 512)]).then_inc(t0_ok, 1)
                    if n_unit >= 2 and n_unit % 2 == 1:
                        out_tile(dve, i, (n_unit - 3) // 2)
                out_tile(dve, i, 7)


def stage_conv_sample(nc, io, keep):
    with ExitStack() as ctx:
        m = Place(nc, ctx, keep["psum"])
        w = [m.sb("c_w_gate", [P, KD * P]), m.sb("c_w_value", [P, KD * P])]
        sig, val = m.sb("c_sig", [P, T]), m.sb("c_val", [P, T])
        ext_p, ext_s = m.sb("c_ext_p", [P, HALO + SEQ]), m.sb("c_ext_s", [P, DB, EXT_S])
        halos = m.sb("c_halos", [P, 4, DB, HALO])
        glu_s = m.sb("c_glu_s", [P, NS])
        acc_p, acc_s = m.sb("c_acc_p", [P, SEQ]), m.sb("c_acc_s", [P, DB, DT])
        y = keep["branch"]
        sq, std, rstd = m.sb("c_sq", [P, 4, 512]), sig, val
        taps_all, taps = m.sb("c_taps_all", [P, 4, CONV_K + 1]), m.sb("c_taps", [P, CONV_K + 1])
        ln = m.sb("c_ln", [P, 2, 4])
        mean_w = m.sb("c_mean_w", [P, P])
        tail_p, tail_s = m.sb("c_tail_p", [HALO, 4 * P]), m.sb("c_tail_s", [NS, 4 * P])
        bank_a, bank_b, bank_s = m.bank("c_a"), m.bank("c_b"), m.bank("c_s")
        z_ps = [(bank_a, bank_b), (bank_a, bank_b), (bank_s[:, 0:NS], bank_s[:, NS:2 * NS])]
        ln_ps = [bank_a, bank_b, bank_s[:, 0:NS]]
        tail_ps = bank_s[:, P:3 * P]
        w_loaded = [m.sem("c_wg_loaded"), m.sem("c_wv_loaded")]
        (c_consts, halo0, z_ok, copied, glu, halo_ok, taps_ready, tap_done, tails, tails_out,
         mean, centred, squared, var, stdev, recip, normed, out_sem, swish) = (
            m.sem("c_" + s) for s in ("consts", "halo0", "z", "copied", "glu", "halo_ok", "taps", "tap", "tails", "tails_out",
                                      "mean", "centred", "squared", "var", "stdev", "recip", "normed", "out", "swish"))
        W = PAGES * PAGE
        pages = m.sb("g_pages", [P, DB * PAGES], I32)
        lane = m.sb("g_lane", [P, 2], I32)
        pages_f, idx_f, lane_f = m.sb("g_pages_f", [P, 64]), m.sb("g_idx_f", [P, 2, 64]), m.sb("g_lane_f", [P, 2])
        idx = m.sb("g_idx", [P, 2, 64], I32)
        idx_now = [m.sb(f"g_idx_now{u}", [P, 2, PAGES], I32) for u in range(2)]
        kc, vc = m.sb("g_kc", [P, PAGES, 512]), m.sb("g_vc", [P, PAGES, 512])
        lfc = m.sb("g_lfc", [64, W])
        c_all, bias_k, ones = m.sb("g_c_all", [64, W + NS]), m.sb("g_bias_k", [64, W + NS]), m.sb("g_ones", [64, W])
        row_coef, sel = m.sb("g_rows", [64, 2]), m.sb("g_sel", [64, 2, P])
        bias_q = m.sb("g_bias_q", [64, P])
        mask_new = m.sb("g_mask", [P, DB, NS])
        q_rows = m.sb("g_q_rows", [P, 4, 32])
        p, pT = m.sb("g_p", [P, W + NS]), m.sb("g_pT", [P, 9, P])
        nmax, rsum, rinv, diag = m.sb("g_nmax", [P, 1]), m.sb("g_rsum", [P, 1]), m.sb("g_rinv", [P, 1]), m.sb("g_diag", [P, P])
        ps3 = m.bank("g_s", 3)
        ps, po, pt_new = ps3[:, 0:W + NS], ps3[:, 1088:1216], ps3[:, 1216:1344]
        pt = m.bank("g_t", 2)
        k_loaded, v_loaded, lf_loaded = ([m.sem(f"g_{x}_loaded{n}") for n in range(PAGES)] for x in "kvl")
        (consts, pool_done, gate, idx_tmp, idx_ok, now_ok, c_ok, cn_ok, bk_ok, bq_ok, bq0, qr_ok, s_ps, max_ok, exp_ok, ri_ok, diag_ok,
         t_ps, t_ok, pv, o_ok) = (m.sem("g_" + s) for s in (
             "consts pool gate idx_tmp idx_ok now_ok c_ok cn_ok bk_ok bq_ok bq0 qr_ok s_ps max_ok exp_ok ri_ok diag_ok t_ps t_ok pv o_ok").split())
        block = m.block()
        c_new, q_new, k_new, v_new = keep["c_new"][0:64, :], keep["q_new"], keep["k_new"], keep["v_new"]

        def tiles(eng, body):
            with eng.Fori(0, 3) as i:
                body(i, True)
            body(3, False)

        @block.sync
        def _(sp):
            sp.dma_start(pages[:, :], io["page_table"].partition_broadcast(P)).then_inc(consts, 16)
            for dst, src in ((lane, "c_lane"), (sel, "c_sel"), (mask_new, "c_new")):
                sp.dma_start(dst[:], io[src]).then_inc(consts, 16)
            sp.dma_start(row_coef[:, :], io["c_rows"][0:64, :]).then_inc(consts, 16)
            for v in range(2):
                sp.dma_start(w[v][:, :], io["w_conv"][v * P:(v + 1) * P, :]).then_inc(w_loaded[v], 16)
            sp.dma_start(taps_all[:, :, :], io["conv_taps"]).then_inc(c_consts, 16)
            sp.dma_start(ln[:, :, :], io["conv_ln"]).then_inc(c_consts, 16)
            for i in range(4):
                sp.dma_start(halos[:, i, :, :], io["state_convT"][i * P:(i + 1) * P, :, :]).then_inc(c_consts, 16)
            with sp.Fori(0, 3) as i:
                for v in range(2):
                    sp.wait_ge(z_ok, after(6 * i + 6))
                    sp.dma_start(w[v][:, :], io["w_conv"][rows(i * 2 + 2 + v), :]).then_inc(w_loaded[v], 16)
            sp.dma_start(io["new_conv_sample"][0, :, 0:HALO - DT, :], io["state_conv"][0, :, DT:HALO, :]).then_inc(out_sem, 16)
            sp.wait_ge(tails_out, after(8))
            sp.dma_start(io["new_conv_prompt"][0, 0, :, :], tail_p[:, :]).then_inc(out_sem, 16)
            for b in range(DB):
                sp.dma_start(io["new_conv_sample"][0, b, HALO - DT:HALO, :], tail_s[b * DT:(b + 1) * DT, :]).then_inc(out_sem, 16)
            sp.wait_ge(out_sem, after(16 * (2 + DB)))

        @block.gpsimd
        def _(pool):
            pool.memset(mean_w[:, :], 1.0 / 512).then_inc(halo0, 1)
            pool.memset(ext_p[:, 0:HALO], 0.0).then_inc(halo0, 1)
            pool.memset(ones[:, :], 1.0)
            pool.memset(q_rows[:, :, :], 0.0).then_inc(pool_done, 1)
            pool.wait_ge(idx_ok, after(2))
            with pool.Fori(0, DB // 2) as half:
                for u in range(2):
                    b, now = half * 2 + u, idx_now[u]
                    pool.tensor_copy(now[:, :, :], idx[:, :, rows(b, PAGES)]).then_inc(now_ok, 1)
                    pool.wait_ge(now_ok, after(b + 1))
                    pool.wait_ge(c_ok, after(b))
                    pool.sem_inc(gate, 1)
                    for n in range(PAGES):
                        pool.indirect_dma_start(lfc[:, n * PAGE:(n + 1) * PAGE], None, io["cache_lfT"],
                                                bass.IndirectOffsetOnAxis(ap=now[0:64, 1, n:n + 1], axis=0)).then_inc(lf_loaded[n], 16)
                    pool.wait_ge(s_ps, after(b))
                    pool.sem_inc(gate, 1)
                    for n in range(PAGES):
                        pool.indirect_dma_start(kc[:, n, :], None, io["cache_kT"],
                                                bass.IndirectOffsetOnAxis(ap=now[:, 0, n:n + 1], axis=0)).then_inc(k_loaded[n], 16)
                    pool.wait_ge(pv, after(b))
                    pool.sem_inc(gate, 1)
                    for n in range(PAGES):
                        pool.indirect_dma_start(vc[:, n, :], None, io["cache_v"],
                                                bass.IndirectOffsetOnAxis(ap=now[:, 0, n:n + 1], axis=0)).then_inc(v_loaded[n], 16)

        @block.tensor
        def _(pe):
            def product(t, c, v):
                off, n = CHUNKS[c]
                pe.wait_ge(w_loaded[v], 16 * t + 16)
                if c == 1:
                    pe.wait_ge(copied, after(6 * t + v + 1))
                elif not isinstance(t, int) or t > 0:
                    pe.wait_ge(copied, after(6 * t + (v - 3 if c == 0 else v - 1)))
                if c == 2 and v == 0 and not (isinstance(t, int) and t == 0):
                    pe.wait_ge(tails_out, after(2 * t - 2))
                for kk in range(KD):
                    last = pe.matmul(z_ps[c][v][:, 0:n], w[v][:, kk * P:(kk + 1) * P], keep["xT"][:, kk, off:off + n],
                                     start=(kk == 0), stop=(kk == KD - 1))
                last.then_inc(z_ok, 1)

            def scores(b):
                pe.wait_ge(bq_ok, after(b + 1))
                pe.wait_ge(qr_ok, after(b + 1))
                pe.wait_ge(exp_ok, after(b))
                pe.wait_ge(o_ok, after(8 * b))
                for n in range(PAGES):
                    pe.wait_ge(k_loaded[n], 16 * b + 16)
                for part, (off, n) in enumerate(CHUNKS):
                    out = ps[:, off:off + n]
                    pe.matmul(out, bias_q[:, :], bias_k[:, off:off + n], start=True, stop=False, skip_group_check=True)
                    if part == 2:
                        pe.matmul(out, keep["ident"][:, :], mask_new[:, bass.ds(b, 1), :], start=False, stop=False, skip_group_check=True)
                    for pair in range(4):
                        keys = kc[:, 4 * part:4 * part + 4, pair * P:(pair + 1) * P] if part < 2 else k_new[:, pair, :]
                        last = pe.matmul(ps[pair * 32:pair * 32 + 32, off:off + n], q_rows[:, pair, :], keys, start=False,
                                         stop=True, skip_group_check=True)
                last.then_inc(s_ps, 1)

            def turn(b):
                pe.wait_ge(diag_ok, after(b + 1))
                pe.wait_ge(t_ok, after(2 * b))
                for n in range(9):
                    width = P if n < 8 else NS
                    out = pt[:, n * P:(n + 1) * P] if n < 8 else pt_new[0:NS, :]
                    last = pe.matmul(out, p[:, n * P:n * P + width], diag[:, :], start=True, stop=True)
                last.then_inc(t_ps, 1)

            def values(b):
                pe.wait_ge(t_ok, after(2 * b + 2))
                for n in range(PAGES):
                    pe.wait_ge(v_loaded[n], 16 * b + 16)
                for pair in range(4):
                    for n in range(9):
                        width = P if n < 8 else NS
                        vals = vc[:, n, pair * P:(pair + 1) * P] if n < 8 else v_new[:, pair * P:(pair + 1) * P]
                        last = pe.matmul(po[:, pair * 32:pair * 32 + 16], vals, pT[0:width, n, pair * 32:pair * 32 + 16],
                                         start=(n == 0), stop=(n == 8))
                last.then_inc(pv, 1)

            def round_(i, more):
                def z(c, v):
                    if more:
                        product(i + 1, c, v)
                scores(2 * i)
                z(0, 0)
                turn(2 * i)
                z(0, 1)
                values(2 * i)
                z(1, 0)
                scores(2 * i + 1)
                z(1, 1)
                turn(2 * i + 1)
                z(2, 0)
                z(2, 1)
                values(2 * i + 1)
                pe.wait_ge(glu, after(4 * i + 4))
                pe.wait_ge(tails_out, after(2 * i))
                if more:
                    pe.wait_ge(copied, after(6 * i + 12))
                pe.transpose(tail_ps[0:HALO, 0:P], ext_p[:, SEQ:SEQ + HALO], keep["ident"][:, :])
                pe.transpose(tail_ps[0:NS, P:2 * P], glu_s[:, :], keep["ident"][:, :]).then_inc(tails, 1)

            for c in range(3):
                for v in range(2):
                    product(0, c, v)
            pe.wait_ge(consts, after(80))
            tiles(pe, round_)
            pe.wait_ge(halo0, after(2))
            pe.wait_ge(tap_done, after(62 * 4))
            pe.wait_ge(tails_out, after(8))
            for c, (off, n) in enumerate(CHUNKS):
                for i in range(4):
                    last = pe.matmul(ln_ps[c][:, 0:n], mean_w[:, :], y[:, i, off:off + n], start=(i == 0), stop=(i == 3))
                last.then_inc(mean, 1)
            for c, (off, n) in enumerate(CHUNKS):
                pe.wait_ge(squared, after(c + 1))
                for i in range(4):
                    last = pe.matmul(ln_ps[c][:, 0:n], mean_w[:, :], sq[:, i, 0:n], start=(i == 0), stop=(i == 3))
                last.then_inc(var, 1)

        @block.scalar
        def _(act):
            def copy(t, c, v):
                off, n = CHUNKS[c]
                act.wait_ge(z_ok, after(6 * t + (6 if c == 2 else 2 * c + v + 1)))
                act.wait_ge(glu, after(4 * t))
                act.activation((sig, val)[v][:, off:off + n], z_ps[c][v][:, 0:n], (ACT.Sigmoid, ACT.Copy)[v]).then_inc(copied, 1)

            def exps(b):
                act.wait_ge(max_ok, after(b + 1))
                act.wait_ge(t_ps, after(b))
                act.wait_ge(ri_ok, after(b))
                act.activation(p[:, :], ps[:, :], ACT.Exp, bias=nmax[:, 0:1], accum_out=rsum[:, 0:1]).then_inc(exp_ok, 1)

            def turned(b):
                act.wait_ge(t_ps, after(b + 1))
                act.wait_ge(pv, after(b))
                act.activation(pT[:, 0:8, :], pt[:, 0:1024].rearrange("p (n r) -> p n r", n=8), ACT.Copy).then_inc(t_ok, 1)
                act.activation(pT[0:NS, 8, :], pt_new[0:NS, :], ACT.Copy).then_inc(t_ok, 1)

            def round_(i, more):
                def cp(c, v):
                    if more:
                        copy(i + 1, c, v)
                exps(2 * i)
                cp(0, 0)
                turned(2 * i)
                cp(0, 1)
                cp(1, 0)
                exps(2 * i + 1)
                cp(1, 1)
                turned(2 * i + 1)
                cp(2, 0)
                cp(2, 1)
                act.wait_ge(tails, after(i + 1))
                act.activation(tail_p[:, rows(i)], tail_ps[0:HALO, 0:P], ACT.Copy).then_inc(tails_out, 1)
                act.activation(tail_s[:, rows(i)], tail_ps[0:NS, P:2 * P], ACT.Copy).then_inc(tails_out, 1)

            act.wait_ge(c_consts, after(96))
            for c in range(3):
                for v in range(2):
                    copy(0, c, v)
            tiles(act, round_)
            def root(c):
                off, n = CHUNKS[c]
                act.wait_ge(var, after(c + 1))
                act.activation(std[:, off:off + n], ln_ps[c][:, 0:n], ACT.Sqrt, bias=keep["eps"][:, 0:1]).then_inc(stdev, 1)

            for c, (off, n) in enumerate(CHUNKS):
                act.wait_ge(centred, after(c + 1))
                if c:
                    act.wait_ge(var, after(c))
                act.activation(sq[:, :, 0:n], y[:, 0:4, off:off + n], ACT.Square).then_inc(squared, 1)
                if c:
                    root(c - 1)
            root(2)
            act.wait_ge(normed, after(3))
            for i in range(4):
                act.activation(y[:, i, :], y[:, i, :], ACT.Silu, scale=ln[:, 0, i:i + 1], bias=ln[:, 1, i:i + 1]).then_inc(swish, 1)

        @block.vector
        def _(dve):
            def window(i):
                dve.wait_ge(copied, after(6 * i + 6))
                dve.wait_ge(tap_done, after(62 * i))
                dve.wait_ge(tails, after(i))
                dve.tensor_tensor(ext_p[:, HALO:HALO + SEQ], val[:, 0:SEQ], sig[:, 0:SEQ], ALU.mult).then_inc(glu, 1)
                dve.tensor_tensor(glu_s[:, :], val[:, SEQ:T], sig[:, SEQ:T], ALU.mult).then_inc(glu, 1)
                dve.tensor_tensor(ext_s[:, :, HALO:EXT_S], val[:, SEQ:T].rearrange("p (b t) -> p b t", b=DB),
                                  sig[:, SEQ:T].rearrange("p (b t) -> p b t", b=DB), ALU.mult).then_inc(glu, 1)
                dve.tensor_copy(ext_s[:, :, 0:HALO].unsqueeze(1), halos[:, rows(i, 1), :, :]).then_inc(glu, 1)
                dve.tensor_copy(taps[:, :].unsqueeze(1), taps_all[:, rows(i, 1), :]).then_inc(taps_ready, 1)
                dve.wait_ge(taps_ready, after(i + 1))
                dve.wait_ge(glu, after(4 * i + 4))

            def taps_of(i, first, end):
                for j in range(first, end):
                    last_tap = j == CONV_K - 1
                    out_p = y[:, rows(i, 1), 0:SEQ] if last_tap else acc_p[:, :]
                    out_s = (y[:, rows(i, 1), SEQ:T].rearrange("p a (b t) -> p (a b) t", b=DB) if last_tap
                             else acc_s[:, :, :])
                    for s, (out, win, prev) in enumerate(((out_p, ext_p[:, j:j + SEQ], acc_p[:, :]),
                                                          (out_s, ext_s[:, :, j:j + DT], acc_s[:, :, :]))):
                        if j == 0:
                            ins = dve.tensor_scalar(out, win, taps[:, 0:1], taps[:, CONV_K:CONV_K + 1], ALU.mult, ALU.add)
                        else:
                            dve.wait_ge(tap_done, after(62 * i + 2 * (j - 1) + s + 1))
                            ins = dve.scalar_tensor_tensor(out, win, taps[:, j:j + 1], prev, ALU.mult, ALU.add)
                        ins.then_inc(tap_done, 1)

            def prepare(b):
                for n in range(PAGES):
                    dve.wait_ge(lf_loaded[n], 16 * b + 16)
                dve.wait_ge(s_ps, after(b))
                dve.tensor_tensor_scan(c_all[:, 0:W], ones[:, :], lfc[:, :], 0.0, ALU.mult, ALU.add).then_inc(c_ok, 1)
                dve.wait_ge(c_ok, after(b + 1))
                dve.tensor_scalar(c_all[:, W:W + NS], c_new[:, SEQ:T], c_all[:, W - 1:W], None, ALU.add).then_inc(cn_ok, 1)
                dve.wait_ge(cn_ok, after(b + 1))
                dve.tensor_scalar(bias_k[:, :], c_all[:, :], row_coef[:, 0:1], row_coef[:, 1:2], ALU.mult, ALU.add).then_inc(bk_ok, 1)
                dve.tensor_tensor(bias_q[:, :].rearrange("p (g t) -> p g t", t=DT),
                                  c_all[:, bass.ds(b * DT + W, DT)].unsqueeze(1).broadcast_to([64, 16, DT]),
                                  sel[:, 1, :].rearrange("p (g t) -> p g t", t=DT), ALU.mult).then_inc(bq0, 1)
                dve.wait_ge(bq0, after(b + 1))
                dve.tensor_tensor(bias_q[:, :], bias_q[:, :], sel[:, 0, :], ALU.add).then_inc(bq_ok, 1)
                dve.tensor_copy(q_rows[0:64, :, 0:DT], q_new[0:64, :, rows(b, DT)])
                dve.tensor_copy(q_rows[64:P, :, DT:2 * DT], q_new[64:P, :, rows(b, DT)]).then_inc(qr_ok, 1)

            def maximum(b):
                dve.wait_ge(s_ps, after(b + 1))
                dve.tensor_reduce(nmax[:, :], ps[:, :], AX.X, ALU.max, negate=True).then_inc(max_ok, 1)

            def normalise(b):
                dve.wait_ge(exp_ok, after(b + 1))
                dve.reciprocal(rinv[:, :], rsum[:, :]).then_inc(ri_ok, 1)
                dve.wait_ge(ri_ok, after(b + 1))
                dve.tensor_scalar(diag[:, :], keep["ident"][:, :], rinv[:, 0:1], None, ALU.mult).then_inc(diag_ok, 1)

            def output(b):
                dve.wait_ge(pv, after(b + 1))
                for pair in range(4):
                    for hh in range(2):
                        dve.tensor_copy(keep["branch"][hh * 64:hh * 64 + 64, 8 + pair, bass.ds(b * DT + SEQ, DT)],
                                        po[hh * 64:hh * 64 + 64, pair * 32 + hh * DT:pair * 32 + hh * DT + DT]).then_inc(o_ok, 1)

            def round_(i, more):
                window(i)
                taps_of(i, 0, 3)
                maximum(2 * i)
                taps_of(i, 3, 4)
                normalise(2 * i)
                taps_of(i, 4, 7)
                prepare(2 * i + 1)
                taps_of(i, 7, 13)
                output(2 * i)
                taps_of(i, 13, 20)
                maximum(2 * i + 1)
                taps_of(i, 20, 21)
                normalise(2 * i + 1)
                taps_of(i, 21, CONV_K)
                if more:
                    prepare(2 * i + 2)
                output(2 * i + 1)

            lk = Link(dve, idx_tmp)
            dve.wait_ge(consts, after(80))
            lk(dve.tensor_copy(pages_f[:, :], pages[:, :]))
            lk(dve.tensor_copy(lane_f[:, :], lane[:, :]))
            for s, size in enumerate((P, 8)):
                lk(dve.tensor_scalar(idx_f[:, s, :], pages_f[:, :], float(size), lane_f[:, s:s + 1], ALU.mult, ALU.add))
                dve.tensor_copy(idx[:, s, :], idx_f[:, s, :]).then_inc(idx_ok, 1)
            dve.wait_ge(pool_done, after(1))
            dve.wait_ge(halo0, after(2))
            dve.wait_ge(c_consts, after(96))
            prepare(0)
            tiles(dve, round_)
            for c, (off, n) in enumerate(CHUNKS):
                dve.wait_ge(mean, after(c + 1))
                dve.tensor_tensor(y[:, 0:4, off:off + n], y[:, 0:4, off:off + n],
                                  ln_ps[c][:, 0:n].unsqueeze(1).broadcast_to([P, 4, n]), ALU.subtract).then_inc(centred, 1)
            for c, (off, n) in enumerate(CHUNKS):
                dve.wait_ge(stdev, after(c + 1))
                dve.reciprocal(rstd[:, off:off + n], std[:, off:off + n]).then_inc(recip, 1)
                dve.wait_ge(recip, after(c + 1))
                dve.wait_ge(squared, after(c + 1))
                dve.tensor_tensor(y[:, 0:4, off:off + n], y[:, 0:4, off:off + n],
                                  rstd[:, off:off + n].unsqueeze(1).broadcast_to([P, 4, n]), ALU.mult).then_inc(normed, 1)


def stage_merge(nc, io, keep):
    with ExitStack() as ctx:
        m = Place(nc, ctx, keep["psum"])
        w = [m.sb(f"m_w{u}", [P, 12 * P]) for u in range(3)]
        sig = m.sb("m_sig", [P, T])
        part = m.sb("m_part", [P, T])
        acc = m.sb("m_acc", [P, T])
        merged = keep["merged"]
        proj = [m.bank(f"m_p{c}") for c in range(3)]
        gate = [m.bank(f"m_g{c}") for c in range(3)]
        w_loaded = [m.sem(f"m_w{u}_loaded") for u in range(3)]
        p_z2 = [m.sem(f"m_p_z2_{n}") for n in range(3)]
        wo_loaded, p_z, g_z, sg_ok, part_ok, acc_ok = (m.sem("m_" + s) for s in "wo_loaded p_z g_z sg_ok part_ok acc_ok".split())
        block = m.block()

        @block.sync
        def _(sp):
            with sp.Fori(0, KD) as i:
                for n in range(3):
                    sp.wait_ge(p_z2[n], after(i))
                    sp.dma_start(w[n][:, :], io["w_merge"][rows(3 * i + n), :]).then_inc(w_loaded[n], 16)
            sp.dma_start(keep["w_out"][:, :, :], io["w_out"]).then_inc(wo_loaded, 16)
            sp.wait_ge(wo_loaded, 16)

        @block.tensor
        def _(pe):
            with pe.Fori(0, KD) as i:
                for n in range(3):
                    pe.wait_ge(w_loaded[n], 16 * i + 16)
                    for c, (off, width) in enumerate(THIRDS):
                        pe.wait_ge(sg_ok, after(9 * i + 3 * n))
                        for kk in range(KD):
                            last = pe.matmul(gate[c][:, 0:width], w[n][:, (4 + kk) * P:(5 + kk) * P],
                                             keep["xT"][:, kk, off:off + width], start=(kk == 0), stop=(kk == KD - 1))
                        last.then_inc(g_z, 1)
                    for c, (off, width) in enumerate(THIRDS):
                        pe.wait_ge(part_ok, after(9 * i + 3 * n))
                        for kk in range(4):
                            last = pe.matmul(proj[c][:, 0:width], w[n][:, kk * P:(kk + 1) * P],
                                             keep["branch"][:, 4 * n + kk, off:off + width], start=(kk == 0), stop=(kk == 3))
                        last.then_inc(p_z if c < 2 else p_z2[n], 1)

        @block.scalar
        def _(act):
            with act.Fori(0, KD) as i:
                for n in range(3):
                    for c, (off, width) in enumerate(THIRDS):
                        act.wait_ge(g_z, after(9 * i + 3 * n + c + 1))
                        act.wait_ge(part_ok, after(9 * i + 3 * n))
                        act.activation(sig[:, off:off + width], gate[c][:, 0:width], ACT.Sigmoid).then_inc(sg_ok, 1)

        @block.vector
        def _(dve):
            with dve.Fori(0, KD) as i:
                for n in range(3):
                    for c, (off, width) in enumerate(THIRDS):
                        dve.wait_ge(sg_ok, after(9 * i + 3 * n + c + 1))
                        if c < 2:
                            dve.wait_ge(p_z, after(6 * i + 2 * n + c + 1))
                        else:
                            dve.wait_ge(p_z2[n], after(i + 1))
                        dve.wait_ge(acc_ok, after(2 * i + max(n - 1, 0)))
                        to = (acc if n == 0 else part)[:, off:off + width]
                        dve.tensor_tensor(to, proj[c][:, 0:width], sig[:, off:off + width], ALU.mult).then_inc(part_ok, 1)
                    dve.wait_ge(part_ok, after(9 * i + 3 * n + 3))
                    if n > 0:
                        to = acc[:, :].unsqueeze(1) if n == 1 else merged[:, bass.ds(i, 1), :]
                        dve.tensor_tensor(to, acc[:, :].unsqueeze(1), part[:, :].unsqueeze(1), ALU.add).then_inc(acc_ok, 1)


GROUPS, SLOTS = 16, 8
HEADS, TOPK = 8, 16


def stage_peer(nc, io, keep):
    with ExitStack() as ctx:
        m = Place(nc, ctx, keep["psum"])
        wq, keysT, s, diag = keep["wq"], keep["keysT"], keep["s"], keep["diag"]
        w_out, merged, u_rows, v_rows = keep["w_out"], keep["merged"], keep["u_rows"], keep["v_rows"]
        h, xn = m.sb("p_h", [P, 2, D]), m.sb("p_xn", [P, 2, D])
        xnT, qT = m.sb("p_xnT", [P, KD, P]), m.sb("p_qT", [P, 16, P])
        cand = m.sb("p_cand", [P, HEADS, TOPK, TOPK])
        gain2, gain_f = m.sb("p_gain2", [P, D]), m.sb("p_gain_f", [P, D])
        sv, si = m.sb("p_sv", [P, 16, TOPK]), m.sb("p_si", [P, 16, TOPK], U32)
        si_f = m.sb("p_si_f", [P, 16, TOPK])
        top, pos, pos2 = m.sb("p_top", [P, HEADS, TOPK]), m.sb("p_pos", [P, HEADS, TOPK], U32), m.sb("p_pos2", [P, HEADS, TOPK], U32)
        pos_f, e_f = m.sb("p_pos_f", [P, HEADS, TOPK]), m.sb("p_e_f", [P, 2, HEADS, TOPK])
        w, idx = m.sb("p_w", [P, 2, HEADS * TOPK]), m.sb("p_idx", [P, 2, HEADS * TOPK], U32)
        wsum, iota = m.sb("p_wsum", [P, HEADS, 1]), m.sb("p_iota", [P, TOPK])
        hid, gl, act_w = m.sb("p_hid", [P, 2, SLOTS]), m.sb("p_gl", [P, 2, SLOTS]), m.sb("p_act_w", [P, 2, SLOTS])
        stat, stat_f = m.sb("p_stat", [P, 2]), m.sb("p_stat_f", [P, 2])
        zero = m.sb("p_zero", [P, P])
        ident_twice = m.sb("p_ident_twice", [P, NS])
        acc = [m.bank(f"p_acc{u}", 2) for u in range(2)]
        pb = [m.bank(f"p_b{u}") for u in range(4)]
        u_loaded, v_loaded = ([m.sem(f"p_{x}_loaded{n}") for n in range(SLOTS)] for x in "uv")
        h_loaded = [m.sem(f"p_h_loaded{u}") for u in range(2)]
        stored = [m.sem(f"p_stored{u}") for u in range(2)]
        x_loaded = [m.sem(f"p_x_loaded{u}") for u in range(3)]
        h_stored = [m.sem(f"p_h_stored{u}") for u in range(2)]
        (consts, twice_ok, halved, ph_ok, h_ok, gate, zero_ok, u_free, v_free, gl_ok, act_ok, diag_ok, acc_ps, y_ok, ss_ok, sd_ok, rs_ok, xn_ok, xt_ps, xt_ok,
         q_ps, q_ok, s_ps, s_ok, link, idx_ok, wd_ok, we_ok, w_ok, fss, fsd, frs) = (
            m.sem("p_" + x) for x in (
                "consts twice_ok halved ph_ok h_ok gate zero_ok u_free v_free gl_ok act_ok diag_ok acc_ps y_ok ss_ok sd_ok rs_ok xn_ok xt_ps xt_ok q_ps q_ok "
                "s_ps s_ok link idx_ok wd_ok we_ok w_ok fss fsd frs").split())
        block = m.block()
        LINKS = 1 + 16 * 5 + 1 + 8 * 5 + 12
        EXPERTS = HEADS * TOPK

        def choose_act(act, t, u, step):
            if step == 0:
                if isinstance(t, int) and t == 0:
                    act.wait_ge(h_ok, after(1))
                else:
                    act.wait_ge(h_loaded[u], t * 8 + 8 * u)
                act.wait_ge(xn_ok, after(t))
                act.activation(cand[:, 0:4, :, :].rearrange("p a b c -> p (a b c)"), h[:, u, :], ACT.Square,
                               accum_out=stat[:, 0:1]).then_inc(ss_ok, 1)
                act.wait_ge(ss_ok, after(t + 1))
                act.activation(stat[:, 1:2], stat[:, 0:1], ACT.Sqrt, scale=1.0 / D, bias=keep["eps"][:, 0:1]).then_inc(sd_ok, 1)
            if step == 1:
                for b in range(2):
                    act.wait_ge(xt_ps, after(2 * t + b + 1))
                    act.activation(xnT[:, 4 * b:4 * b + 4, :], pb[b].rearrange("p (k n) -> p k n", k=4), ACT.Copy).then_inc(xt_ok, 1)
            if 2 <= step <= 5:
                b = step - 2
                act.wait_ge(q_ps, after(4 * t + b + 1))
                act.activation(qT[:, 4 * b:4 * b + 4, :], pb[(b + 2) % 4].rearrange("p (k n) -> p k n", k=4), ACT.Copy).then_inc(q_ok, 1)
            if step == 6:
                act.wait_ge(idx_ok, after(t))
                for b in range(4):
                    act.wait_ge(s_ps, after(4 * t + b + 1))
                    act.activation(s[:, 4 * b:4 * b + 4, :], pb[b].rearrange("p (k n) -> p k n", k=4), ACT.Copy).then_inc(s_ok, 1)
            if step == 13:
                act.wait_ge(wd_ok, after(t + 1))
                act.activation(w[:, u, :], w[:, u, :], ACT.Exp).then_inc(we_ok, 1)

        def choose_pe(pe, t, u, step):
            if step == 0:
                pe.wait_ge(xn_ok, after(t + 1))
                pe.wait_ge(s_ok, after(4 * t))
                for b in range(2):
                    for k in range(4 * b, 4 * b + 4):
                        last = pe.transpose(pb[b][:, k % 4 * P:k % 4 * P + P], xn[:, u, k * P:(k + 1) * P], keep["ident"][:, :])
                    last.then_inc(xt_ps, 1)
            if 1 <= step <= 4:
                pe.wait_ge(xt_ok, after(2 * t + 2))
                b = step - 1
                for c in range(4 * b, 4 * b + 4):
                    for k in range(KD):
                        last = pe.matmul(pb[(b + 2) % 4][:, c % 4 * P:c % 4 * P + P], wq[:, k, c * P:(c + 1) * P], xnT[:, k, :],
                                         start=(k == 0), stop=(k == KD - 1))
                last.then_inc(q_ps, 1)
            if step == 5:
                pe.wait_ge(q_ok, after(4 * t + 4))
                for b in range(4):
                    for c in range(4 * b, 4 * b + 4):
                        last = pe.matmul(pb[b][:, c % 4 * P:c % 4 * P + P], qT[:, c, :], keysT[:, c, :], start=True, stop=True)
                    last.then_inc(s_ps, 1)

        class Chooser:

            def __init__(self, dve, t, u):
                self.dve, self.t, self.u = dve, t, u
                self.lk = Link(dve, link)

            def top16(self, values, val, ind):
                dve, lk = self.dve, self.lk
                lk(dve.max(val[:, 0:8], values))
                lk(dve.max_index(ind[:, 0:8], val[:, 0:8], values))
                lk(dve.match_replace(values, val[:, 0:8], values, -3.0e38))
                lk(dve.max(val[:, 8:16], values))
                lk(dve.max_index(ind[:, 8:16], val[:, 8:16], values))

            def step(self, n):
                dve, t, u, lk = self.dve, self.t, self.u, self.lk
                if n == 0:
                    dve.sem_clear(link)
                    dve.sem_inc(link, 1)
                    dve.wait_ge(sd_ok, after(t + 1))
                    dve.reciprocal(stat[:, 1:2], stat[:, 1:2]).then_inc(rs_ok, 1)
                    dve.wait_ge(rs_ok, after(t + 1))
                    dve.scalar_tensor_tensor(xn[:, u, :], h[:, u, :], stat[:, 1:2], gain2[:, :], ALU.mult, ALU.mult).then_inc(xn_ok, 1)
                if 6 <= n <= 9:
                    if n == 6:
                        dve.wait_ge(s_ok, after(4 * t + 4))
                        lk(dve.memset(sv[:, :, :], 0.0))
                    for c in range(4 * (n - 6), 4 * (n - 5)):
                        self.top16(s[:, c, :], sv[:, c, :], si[:, c, :])
                if n == 9:
                    pairs = sv[:, :, :].rearrange("p (h s) k -> p h s k", s=2)
                    shape = [P, HEADS, TOPK, TOPK]
                    lk(dve.tensor_tensor(cand[:, :, :, :], pairs[:, :, 0, :].unsqueeze(3).broadcast_to(shape),
                                         pairs[:, :, 1, :].unsqueeze(2).broadcast_to(shape), ALU.add))
                if 10 <= n <= 11:
                    for hd in range(4 * (n - 10), 4 * (n - 9)):
                        self.top16(cand[:, hd, :, :].rearrange("p a b -> p (a b)"), top[:, hd, :], pos[:, hd, :])
                if n in (12, 13):
                    half = n - 12
                    shape = [P, HEADS, TOPK, TOPK]
                    if half == 0:
                        lk(dve.tensor_copy(si_f[:, :, :], si[:, :, :]))
                        lk(dve.tensor_scalar(pos2[:, :, :], pos[:, :, :], 4, None, ALU.logical_shift_right))
                    else:
                        lk(dve.tensor_scalar(pos2[:, :, :], pos[:, :, :], 15, None, ALU.bitwise_and))
                    lk(dve.tensor_copy(pos_f[:, :, :], pos2[:, :, :]))
                    lk(dve.tensor_tensor(cand[:, :, :, :], pos_f[:, :, :].unsqueeze(3).broadcast_to(shape),
                                         iota[:, :].unsqueeze(1).unsqueeze(1).broadcast_to(shape), ALU.is_equal))
                    of_half = si_f[:, :, :].rearrange("p (h s) k -> p h s k", s=2)[:, :, half, :]
                    lk(dve.tensor_tensor(cand[:, :, :, :], cand[:, :, :, :], of_half.unsqueeze(2).broadcast_to(shape), ALU.mult))
                    lk(dve.tensor_reduce(e_f[:, half, :, :], cand[:, :, :, :], AX.X, ALU.add))
                if n == 13:
                    lk(dve.scalar_tensor_tensor(e_f[:, 0, :, :], e_f[:, 0, :, :], float(P), e_f[:, 1, :, :], ALU.mult, ALU.add))
                    dve.tensor_copy(idx[:, u, :].rearrange("p (h k) -> p h k", h=HEADS), e_f[:, 0, :, :]).then_inc(idx_ok, 1)
                    wv = w[:, u, :].rearrange("p (h k) -> p h k", h=HEADS)
                    dve.tensor_tensor(wv, top[:, :, :], top[:, :, 0:1].broadcast_to([P, HEADS, TOPK]), ALU.subtract).then_inc(wd_ok, 1)
                    dve.wait_ge(we_ok, after(t + 1))
                    dve.tensor_reduce(wsum[:, :, :], wv, AX.X, ALU.add).then_inc(w_ok, 1)
                    dve.wait_ge(w_ok, after(3 * t + 1))
                    dve.reciprocal(wsum[:, :, :], wsum[:, :, :]).then_inc(w_ok, 1)
                    dve.wait_ge(w_ok, after(3 * t + 2))
                    dve.tensor_tensor(wv, wv, wsum[:, :, :].broadcast_to([P, HEADS, TOPK]), ALU.mult).then_inc(w_ok, 1)
                    assert self.lk.n == LINKS, self.lk.n

        def main_pool(pool, t, u, n):
            if n == P:
                pool.wait_ge(idx_ok, after(t + 1))
            else:
                pool.wait_ge(halved, after(2))
            for g in range(GROUPS * n // P):
                for free, loaded, to, table in ((u_free, u_loaded, u_rows, "peer_u"), (v_free, v_loaded, v_rows, "peer_v")):
                    for k in range(SLOTS):
                        c = g * SLOTS + k
                        pool.wait_ge(free, after(EXPERTS * t + c + 1))
                        pool.sem_inc(gate, 1)
                        pool.indirect_dma_start(to[:, k, :], None, io[table],
                                                bass.IndirectOffsetOnAxis(ap=idx[:, u, c:c + 1], axis=0)).then_inc(loaded[k], 16)

        def main_pe(pe, t, u, n, choosing):
            pe.wait_ge(y_ok, after(t))
            for hf in range(2):
                pe.matmul(acc[u][0:n, hf * 512:(hf + 1) * 512], zero[:, 0:n], h[:, u, hf * 512:(hf + 1) * 512], start=True, stop=False,
                          skip_group_check=True)
            for g in range(GROUPS * n // P):
                for k in range(SLOTS):
                    c = g * SLOTS + k
                    pe.wait_ge(diag_ok, after(EXPERTS * t + c + 1))
                    pe.wait_ge(v_loaded[k], (t * GROUPS + g) * 16 + 16)
                    for hf in range(2):
                        last = pe.matmul(acc[u][0:n, hf * 512:(hf + 1) * 512], diag[:, k, 0:n], v_rows[:, k, hf * 512:(hf + 1) * 512],
                                         start=False, stop=False, skip_group_check=True)
                    last.then_inc(v_free, 1)
                if choosing:
                    choose_pe(pe, t + 1, 1 - u, g)
            for hf in range(2):
                last = pe.matmul(acc[u][0:n, hf * 512:(hf + 1) * 512], keep["ident"][0:n, 0:n], h[0:n, u, hf * 512:(hf + 1) * 512],
                                 start=False, stop=True, skip_group_check=True)
            last.then_inc(acc_ps, 1)

        def main_act(act, t, u, n, choosing):
            if n < P:
                act.wait_ge(twice_ok, after(1))
            for g in range(GROUPS * n // P):
                gp = g % 2
                act.wait_ge(u_free, after(EXPERTS * t + (g + 2) * SLOTS))
                act.activation(gl[:, gp, :], hid[:, gp, :], ACT.Gelu).then_inc(gl_ok, 1)
                act.wait_ge(act_ok, after(GROUPS * t + g + 1))
                for k in range(SLOTS):
                    act.wait_ge(v_free, after(EXPERTS * t + g * SLOTS + k + 1))
                    act.activation(diag[:, k, 0:n], (keep["ident"] if n == P else ident_twice)[:, :], ACT.Copy, scale=act_w[:, gp, k:k + 1]).then_inc(diag_ok, 1)
                if choosing:
                    choose_act(act, t + 1, 1 - u, g)
            act.wait_ge(acc_ps, after(t + 1))
            act.activation(h[0:n, u, :], acc[u][0:n, :], ACT.Square, accum_out=stat_f[0:n, 0:1]).then_inc(fss, 1)
            act.wait_ge(fss, after(t + 1))
            act.activation(stat_f[0:n, 1:2], stat_f[0:n, 0:1], ACT.Sqrt, scale=1.0 / D, bias=keep["eps"][0:n, 0:1]).then_inc(fsd, 1)

        def main_dve(dve, t, u, n, choosing):
            chooser = Chooser(dve, t + 1, 1 - u) if choosing else None
            if n < P:
                dve.wait_ge(idx_ok, after(t + 1))
                dve.wait_ge(w_ok, after(3 * t + 3))
                for x in (idx, w):
                    dve.tensor_copy(x[NS:P, u, 0:EXPERTS // 2], x[NS:P, u, EXPERTS // 2:EXPERTS]).then_inc(halved, 1)
                dve.wait_ge(halved, after(2))
            for g in range(GROUPS * n // P):
                gp = g % 2
                for k in range(SLOTS):
                    dve.wait_ge(u_loaded[k], (t * GROUPS + g) * 16 + 16)
                    last = dve.tensor_tensor_reduce(out=u_rows[:, k, :], in0=u_rows[:, k, :], in1=xn[:, u, :], scale=1.0, scalar=0.0,
                                                    op0=ALU.mult, op1=ALU.add, accum_out=hid[:, gp, k:k + 1])
                    last.then_inc(u_free, 1)
                dve.wait_ge(gl_ok, after(GROUPS * t + g + 1))
                dve.tensor_tensor(act_w[:, gp, :], gl[:, gp, :], w[:, u, g * SLOTS:(g + 1) * SLOTS], ALU.mult).then_inc(act_ok, 1)
                if chooser:
                    chooser.step(g)
            dve.wait_ge(fsd, after(t + 1))
            dve.reciprocal(stat_f[0:n, 1:2], stat_f[0:n, 1:2]).then_inc(frs, 1)
            dve.wait_ge(frs, after(t + 1))
            dve.scalar_tensor_tensor(h[0:n, u, :], acc[u][0:n, :], stat_f[0:n, 1:2], gain_f[0:n, :], ALU.mult, ALU.mult).then_inc(y_ok, 1)

        def tiles(eng, main):
            with eng.Fori(0, 4) as i:
                for u in range(2):
                    main(eng, 2 * i + u, u, P, True)
            main(eng, 8, 0, NS, False)

        def staged(t):
            return h[:, 0, :] if t == 0 else h[:, 1, :] if t % 2 else xn[:, 1, :]

        def out_product(pe, t):
            n = P if t < 8 else NS
            if t >= 2:
                pe.wait_ge(h_ok, after(t - 1))
            for hf in range(2):
                for kk in range(KD):
                    last = pe.matmul(acc[t % 2][0:n, hf * 512:(hf + 1) * 512], merged[:, kk, t * P:t * P + n],
                                     w_out[:, kk, hf * 512:(hf + 1) * 512], start=(kk == 0), stop=(kk == KD - 1))
            last.then_inc(ph_ok, 1)

        def residual(dve, t):
            n = P if t < 8 else NS
            dve.wait_ge(ph_ok, after(t + 1))
            dve.wait_ge(x_loaded[t % 2 if t else 2], 16 * ((t + 1) // 2) if t else 16)
            dve.tensor_tensor(staged(t)[0:n, :], acc[t % 2][0:n, :], staged(t)[0:n, :], ALU.add).then_inc(h_ok, 1)

        @block.sync
        def _(sp):
            for dst, src in ((gain2, "norm2_g"), (gain_f, "final_g")):
                sp.dma_start(dst[:, :], io[src].partition_broadcast(P)).then_inc(consts, 16)
            for t in range(3):
                sp.dma_start(staged(t), io["x_all"][t * P:(t + 1) * P, :]).then_inc(x_loaded[(2, 1, 0)[t]], 16)
            for dst, src in ((wq, "peer_wq"), (keysT, "peer_keysT"), (iota, "c_iota16")):
                sp.dma_start(dst[:], io[src]).then_inc(consts, 16)
            for t in range(1, NT):
                sp.wait_ge(h_ok, after(t + 1))
                if t < NT - 1:
                    sp.dma_start(io["h_scratch"][t * P:(t + 1) * P, :], staged(t)).then_inc(h_stored[t % 2], 16)
                else:
                    for start in (t * P, t * P + NS):
                        sp.dma_start(io["h_scratch"][start:start + NS, :], staged(t)[0:NS, :]).then_inc(h_stored[t % 2], 16)
                if t + 2 < NT:
                    sp.wait_ge(h_stored[t % 2], after(16 * ((t + 1) // 2)))
                    sp.dma_start(staged(t + 2), io["x_all"][(t + 2) * P:(t + 3) * P, :]).then_inc(x_loaded[t % 2], 16)
            sp.wait_ge(h_stored[0], after(16 * 5))
            sp.wait_ge(h_stored[1], after(16 * 4))

            def tile(sp, t, u, n, more):
                if more:
                    if u == 0:
                        sp.wait_ge(stored[1], after(8 * t))
                    else:
                        sp.wait_ge(stored[0], after(8 * t + 8))
                    sp.dma_start(h[:, 1 - u, :], io["h_scratch"][rows(t + 1), :]).then_inc(h_loaded[1 - u], 16)
                sp.wait_ge(y_ok, after(t + 1))
                if more:
                    sp.dma_start(io["y_prompt"][0, rows(t), :], h[:, u, :]).then_inc(stored[u], 16)
                else:
                    sp.dma_start(io["y_sample"].rearrange("b t d -> (b t) d"), h[0:n, u, :]).then_inc(stored[u], 16)

            tiles(sp, tile)
            sp.wait_ge(stored[0], after(16 * 5))
            sp.wait_ge(stored[1], after(16 * 4))

        @block.gpsimd
        def _(pool):
            pool.memset(zero[:, :], 0.0).then_inc(zero_ok, 1)
            pool.wait_ge(ph_ok, after(NT))
            tiles(pool, lambda eng, t, u, n, more: main_pool(eng, t, u, n))

        @block.tensor
        def _(pe):
            pe.sem_inc(v_free, SLOTS)
            for t in range(3):
                out_product(pe, t)
            pe.wait_ge(consts, after(16 * 5))
            pe.wait_ge(zero_ok, after(1))
            for step in range(GROUPS):
                choose_pe(pe, 0, 0, step)
            for t in range(3, NT):
                out_product(pe, t)
            pe.wait_ge(h_ok, after(NT))
            tiles(pe, main_pe)

        @block.scalar
        def _(act):
            for step in range(GROUPS):
                choose_act(act, 0, 0, step)
            tiles(act, main_act)

        @block.vector
        def _(dve):
            dve.sem_inc(u_free, SLOTS)
            dve.tensor_tensor(ident_twice[:, :], keep["ident"][:, 0:NS], keep["ident"][:, NS:P], ALU.add).then_inc(twice_ok, 1)
            residual(dve, 0)
            dve.wait_ge(consts, after(16 * 5))
            first = Chooser(dve, 0, 0)
            for step in range(GROUPS):
                first.step(step)
                for t in {0: (1, 2), 7: (3,), 8: (4,), 9: (5,), 11: (6,), 13: (7, 8)}.get(step, ()):
                    residual(dve, t)
            tiles(dve, main_dve)


OUTPUTS = (
    ("y_prompt", (1, SEQ, D)), ("y_sample", (DB, DT, D)),
    ("new_k_prompt", (1, 1, SEQ, 8, 64)), ("new_v_prompt", (1, 1, SEQ, 8, 64)), ("new_logf_prompt", (1, 1, SEQ, 8)),
    ("new_conv_prompt", (1, 1, HALO, 512)), ("new_hgrn_prompt", (1, 1, 4, P, P)),
    ("new_k_sample", (1, DB, DT, 8, 64)), ("new_v_sample", (1, DB, DT, 8, 64)), ("new_logf_sample", (1, DB, DT, 8)),
    ("new_conv_sample", (1, DB, HALO, 512)), ("new_hgrn_sample", (1, DB, 4, P, P)),
)


def build(nc, io, stages):
    with ExitStack() as ctx:
        m = Place(nc, ctx)
        io["h_scratch"] = nc.dram_tensor("h_scratch", (TP, D), F32, kind="Internal").ap()
        keep = {"ident": m.sb("ident", [P, P]), "eps": m.sb("eps", [P, 1]),
                "psum": ctx.enter_context(nc.psum_tensor("psum", [P, 8 * 512], F32))}
        wide = m.sb("wide", [P, KD * TP + 12 * T])
        keep["xT"] = wide[:, 0:KD * TP].rearrange("p (k t) -> p k t", k=KD)
        keep["branch"] = wide[:, KD * TP:].rearrange("p (c t) -> p c t", c=12)
        sizes, at = (("wq", KD, 2048), ("keysT", 16, P), ("s", 16, P), ("diag", SLOTS, P)), 0
        for name, k, n in sizes:
            keep[name] = wide[:, at:at + k * n].rearrange("p (k n) -> p k n", k=k)
            at += k * n
        with ExitStack() as trunk_ctx:
            t = Place(nc, trunk_ctx)
            keep["c_new"] = t.sb("c_new", [P, T])
            keep["q_new"], keep["k_new"] = t.sb("q_new", [P, 4, NS]), t.sb("k_new", [P, 4, NS])
            keep["v_new"] = t.sb("v_new", [NS, 512])
            for stage in stages[0]:
                stage(nc, io, keep)
        late = m.sb("late", [P, KD * D + KD * T])
        keep["w_out"] = late[:, 0:KD * D].rearrange("p (k n) -> p k n", k=KD)
        keep["merged"] = late[:, KD * D:].rearrange("p (k n) -> p k n", k=KD)
        keep["u_rows"] = late[:, 0:SLOTS * D].rearrange("p (k n) -> p k n", k=SLOTS)
        keep["v_rows"] = late[:, SLOTS * D:2 * SLOTS * D].rearrange("p (k n) -> p k n", k=SLOTS)
        for stage in stages[1]:
            stage(nc, io, keep)


def laid_out(inputs):
    a = {k: np.asarray(v) for k, v in inputs.items()}
    w = a["w_in"][0].reshape(KD, P, -1).transpose(1, 0, 2)

    def tiles(starts, width=P):
        return np.concatenate([w[:, :, s:s + width].reshape(P, KD * width) for s in starts])

    out = {}
    out["x_all"] = np.concatenate([a["x_prompt"][0], a["x_sample"].reshape(NS, D), np.zeros((TP - T, D), np.float32)])
    out["w_conv"] = tiles([s + P * i for i in range(4) for s in (512, 0)])
    out["w_hgrn"] = tiles([s + P * h for h in range(4) for s in (1024, 1536, 2560, 2048)])
    out["w_fox"] = tiles([s + P * j for j in range(4) for s in (3072, 3584, 4096)])
    af = w[:, :, 4608:4616]
    zeros = np.zeros((P, KD, 24), np.float32)
    out["w_af"] = np.concatenate([af, zeros] * 4, 2).reshape(P, KD * P)
    wb = a["w_branch"][0].reshape(3, 4, P, D).transpose(0, 2, 1, 3)
    out["w_merge"] = np.concatenate([
        np.concatenate([wb[n][:, :, P * i:P * (i + 1)], w[:, :, 4616 + D * n + P * i:4616 + D * n + P * (i + 1)]], 1)
        .reshape(P, 12 * P) for i in range(KD) for n in range(3)])
    out["w_out"] = a["w_out"][0].reshape(KD, P, D).transpose(1, 0, 2)
    out["norm1_g"], out["norm2_g"], out["final_g"] = a["norm1_g"][0], a["norm2_g"][0], a["final_g"]
    out["conv_taps"] = np.concatenate([a["conv_dw"][0], a["conv_db"]]).reshape(CONV_K + 1, 4, P).transpose(2, 1, 0)
    out["conv_ln"] = np.stack([a["conv_ln_g"][0], a["conv_ln_b"][0]]).reshape(2, 4, P).transpose(2, 0, 1)
    out["state_conv"] = a["state_conv"]
    out["state_convT"] = a["state_conv"][0].transpose(2, 0, 1)
    out["state_hgrn"] = a["state_hgrn"][0].transpose(1, 2, 0, 3).reshape(4 * P, DB, P)
    out["hg_lb"] = a["hg_lb_logits"][0].reshape(4, P).T
    out["hg_norm"] = a["hg_norm_g"][0].reshape(P, 1)
    fb = a["att_fb"][0]
    z24 = np.zeros(24, np.float32)
    out["att_fb"] = np.concatenate([fb, z24] * 4).reshape(P, 1)
    out["cache_kT"] = a["cache_k"][0].reshape(PHYS, PAGE, 4, P).transpose(0, 3, 2, 1).reshape(PHYS * P, 4 * PAGE)
    out["cache_v"] = a["cache_v"][0].reshape(PHYS * PAGE, 512)
    out["cache_lfT"] = a["cache_logf"][0].transpose(0, 2, 1).reshape(PHYS * 8, PAGE)
    out["page_table"] = a["page_table"].reshape(DB * PAGES)
    out["peer_wq"] = a["peer_wq"][0].reshape(KD, P, 2048).transpose(1, 0, 2)
    out["peer_keysT"] = a["peer_keys"][0].reshape(16, P, P).transpose(2, 0, 1)
    out["peer_u"], out["peer_v"] = a["peer_u"][0], a["peer_v"][0]
    s, t = np.arange(P)[:, None], np.arange(P)[None, :]
    out["c_ident"] = np.eye(P, dtype=np.float32)
    out["c_eps"] = np.full((P, 1), EPS, np.float32)
    masks = [(s // (2 * h) == t // (2 * h)) & (s % (2 * h) < h) & (t % (2 * h) >= h) for h in LEVELS] + [s == t]
    out["c_levels"] = np.stack(masks, 1).astype(np.float32)
    reset = np.ones(T, np.float32)
    reset[0:SEQ:64] = 0
    reset[SEQ:T:DT] = 0
    out["c_reset"] = reset
    out["c_reset_c"] = np.ones(T, np.float32)
    out["c_reset_c"][0] = 0
    out["c_reset_c"][SEQ:T:DT] = 0
    out["c_batch"] = (np.arange(NS)[:, None] // DT == np.arange(DB)[None, :]).astype(np.float32)
    out["c_causal"] = np.where(t <= s, 0, NEG).astype(np.float32)
    lane = np.arange(64)
    out["c_rows"] = np.tile(np.stack([np.where(lane < 8, -1, 0), np.where((lane >= 32) & (lane < 40), 1, 0)], 1).astype(np.float32), (2, 1))
    out["c_heads"] = np.tile(np.stack([lane[:, None] == np.arange(8)[None], lane[:, None] - 32 == np.arange(8)[None]], 1).astype(np.float32), (2, 1, 1))
    col = np.arange(P)
    head, used, tok = 2 * (col // 32) + (col % 32) // 8, col % 32 < 16, col % 8
    sel = (lane[:, None] == head[None]) & used[None]
    selq = (lane[:, None] - 32 == head[None]) & used[None]
    out["c_sel"] = np.stack([sel, selq], 1).astype(np.float32)
    key = np.arange(NS)
    allowed = (key[None, None] // DT == np.arange(DB)[None, :, None]) & (key[None, None] % DT <= tok[:, None, None])
    out["c_new"] = np.where(allowed, 0, NEG).astype(np.float32)
    out["c_lane"] = np.stack([np.arange(P), np.arange(P) % 8], 1).astype(np.int32)
    out["c_iota16"] = np.broadcast_to(np.arange(16, dtype=np.float32), (P, 16))
    return {k: np.ascontiguousarray(v) for k, v in out.items()}


STAGES = ((stage_norm, stage_hgrn, stage_fox, stage_conv_sample), (stage_merge, stage_peer))


def kernel(**inputs):
    import concourse.bacc as bacc
    from concourse.bass_utils import run_bass_kernel_spmd

    nc = bacc.Bacc("TRN2", target_bir_lowering=False, num_devices=1)
    arrays = laid_out(inputs)
    io = {k: nc.dram_tensor("in_" + k, v.shape, mybir.dt.from_np(v.dtype), kind="ExternalInput").ap() for k, v in arrays.items()}
    for name, shape in OUTPUTS:
        io[name] = nc.dram_tensor("out_" + name, shape, F32, kind="ExternalOutput").ap()
    build(nc, io, STAGES)
    got = run_bass_kernel_spmd(nc, [{"in_" + k: v for k, v in arrays.items()}], core_ids=[0]).results[0]
    return tuple(got["out_" + name] for name, _ in OUTPUTS)
```
